# Optimizing a Trainium2 kernel written in Bass

```python
import math
import jax
import jax.numpy as jnp
from jax import lax
import numpy as np
import jax, jax.numpy as jnp

D_MODEL = 1024
BATCH = 1
SEQ = 512
DEPTH = 2

N_MEM = 256
GROUP_WIDTH = 512
D_MIX = 4 * GROUP_WIDTH
NORM_EPS = 1e-6

RET_HEADS = 4
RET_HEAD_DIM = 128
RET_CHUNK = 128
ROPE_BASE = 10000.0

SSD_HEADS = 8
SSD_HEAD_DIM = 64
SSD_GROUPS = 2
SSD_STATE = 128
SSD_CONV = 4
SSD_CHUNK = 128
SSD_BC = SSD_GROUPS * SSD_STATE
SSD_CONV_DIM = GROUP_WIDTH + 2 * SSD_BC
SSD_NORM_GROUP = GROUP_WIDTH // SSD_GROUPS
DT_MIN = 1e-3
DT_MAX = 1e-1
A_INIT_MIN = 1.0
A_INIT_MAX = 16.0

SB_HEADS = 4
SB_HEAD_DIM = 128
SB_BLOCK = 128

MEM_HEADS = 4
MEM_HEAD_DIM = 128

IN_SIZES = (GROUP_WIDTH, GROUP_WIDTH, GROUP_WIDTH, GROUP_WIDTH,
            SSD_CONV_DIM, GROUP_WIDTH, SSD_HEADS,
            GROUP_WIDTH, GROUP_WIDTH, GROUP_WIDTH, GROUP_WIDTH,
            GROUP_WIDTH, GROUP_WIDTH)
D_IN = sum(IN_SIZES)


def rmsnorm(x, g):
    xf = x.astype(jnp.float32)
    y = xf * lax.rsqrt(jnp.mean(xf * xf, axis=-1, keepdims=True) + NORM_EPS)
    return (y * g.astype(jnp.float32)).astype(x.dtype)

def apply_rope(t):
    s, d = t.shape[1], t.shape[-1]
    inv_freq = ROPE_BASE ** (-jnp.arange(0, d, 2, dtype=jnp.float32) / d)
    ang = jnp.arange(s, dtype=jnp.float32)[:, None] * inv_freq[None, :]
    cos = jnp.cos(ang)[None, :, None, :]
    sin = jnp.sin(ang)[None, :, None, :]
    t1, t2 = jnp.split(t.astype(jnp.float32), 2, axis=-1)
    return jnp.concatenate([t1 * cos - t2 * sin, t2 * cos + t1 * sin], axis=-1).astype(t.dtype)

def retention(q, k, v):
    b, s, h, d = q.shape
    dv = v.shape[-1]
    c = RET_CHUNK
    nc = s // c
    dt = v.dtype
    q = apply_rope(q)
    k = apply_rope(k) * (d ** -0.5)
    log_g = jnp.log(1.0 - 2.0 ** (-5.0 - jnp.arange(h, dtype=jnp.float32)))
    idx = jnp.arange(c, dtype=jnp.float32)
    rel = idx[:, None] - idx[None, :]
    intra = jnp.where(rel[None] >= 0, jnp.exp(rel[None] * log_g[:, None, None]), 0.0)
    zeta = jnp.exp((c - 1 - idx)[:, None] * log_g[None, :])
    xi = jnp.exp((idx + 1)[:, None] * log_g[None, :])
    chunk_decay = jnp.exp(c * log_g)
    qc = q.reshape(b, nc, c, h, d)
    kc = k.reshape(b, nc, c, h, d)
    vc = v.reshape(b, nc, c, h, dv)
    scores = jnp.einsum('bcnhd,bcmhd->bchnm', qc, kc) * intra.astype(dt)
    y_intra = jnp.einsum('bchnm,bcmhe->bcnhe', scores, vc)
    kv = jnp.einsum('bcmhd,bcmhe->bchde', kc * zeta.astype(dt)[:, :, None], vc)

    def step(state, kv_c):
        return chunk_decay[:, None, None] * state + kv_c, state

    _, r_prev = lax.scan(step, jnp.zeros((b, h, d, dv), jnp.float32),
                         jnp.moveaxis(kv.astype(jnp.float32), 1, 0))
    r_prev = jnp.moveaxis(r_prev, 0, 1).astype(dt)
    y_inter = jnp.einsum('bcnhd,bchde->bcnhe', qc, r_prev) * xi.astype(dt)[:, :, None]
    y = (y_intra + y_inter).reshape(b, s, h, dv).astype(jnp.float32)
    mu = jnp.mean(y, axis=-1, keepdims=True)
    var = jnp.mean(jnp.square(y - mu), axis=-1, keepdims=True)
    y = (y - mu) * lax.rsqrt(var + NORM_EPS)
    return y.reshape(b, s, h * dv).astype(dt)

def ssd_mixer(xbc, z, dt_raw, conv_w, conv_b, dt_bias, a_log, d_skip, norm_g):
    b, s, _ = xbc.shape
    dtype = xbc.dtype
    L = SSD_CHUNK
    nc = s // L
    G, J, P, N = SSD_GROUPS, SSD_HEADS // SSD_GROUPS, SSD_HEAD_DIM, SSD_STATE
    xbc = lax.conv_general_dilated(xbc, conv_w[:, None, :], window_strides=(1,),
                                   padding=[(SSD_CONV - 1, 0)],
                                   dimension_numbers=('NWC', 'WIO', 'NWC'),
                                   feature_group_count=SSD_CONV_DIM)
    xbc = jax.nn.silu(xbc + conv_b)
    xs, bm, cm = jnp.split(xbc, [GROUP_WIDTH, GROUP_WIDTH + SSD_BC], axis=-1)
    delta = jax.nn.softplus(dt_raw.astype(jnp.float32) + dt_bias.astype(jnp.float32))
    da = (delta * -jnp.exp(a_log.astype(jnp.float32))).reshape(b, nc, L, SSD_HEADS)
    x_heads = xs.reshape(b, s, SSD_HEADS, P)
    xdt = (x_heads * delta[..., None].astype(dtype)).reshape(b, nc, L, G, J, P)
    bc = bm.reshape(b, nc, L, G, N)
    cc = cm.reshape(b, nc, L, G, N)
    a_cs = jnp.cumsum(da, axis=2)
    causal = jnp.tril(jnp.ones((L, L), dtype=bool))[None, None, :, :, None]
    seg = a_cs[:, :, :, None, :] - a_cs[:, :, None, :, :]
    decay_in = jnp.exp(jnp.where(causal, seg, -jnp.inf)).reshape(b, nc, L, L, G, J)
    cb = jnp.einsum('bclgn,bcsgn->bclsg', cc, bc)
    y_diag = jnp.einsum('bclsgj,bcsgjp->bclgjp', cb[..., None] * decay_in.astype(dtype), xdt)
    decay_states = jnp.exp(a_cs[:, :, -1:, :] - a_cs).reshape(b, nc, L, G, J)
    states = jnp.einsum('bclgn,bclgjp->bcgjpn', bc, xdt * decay_states.astype(dtype)[..., None])
    chunk_decay = jnp.exp(a_cs[:, :, -1, :]).reshape(b, nc, G, J)

    def step(state, inp):
        dec, st = inp
        return dec[..., None, None] * state + st, state

    _, prev = lax.scan(step, jnp.zeros((b, G, J, P, N), jnp.float32),
                       (jnp.moveaxis(chunk_decay, 1, 0), jnp.moveaxis(states.astype(jnp.float32), 1, 0)))
    prev = jnp.moveaxis(prev, 0, 1).astype(dtype)
    y_off = jnp.einsum('bclgn,bcgjpn->bclgjp', cc, prev) * jnp.exp(a_cs).reshape(b, nc, L, G, J, 1).astype(dtype)
    y = (y_diag + y_off).reshape(b, s, SSD_HEADS, P) + x_heads * d_skip.astype(dtype)[:, None]
    y = y.reshape(b, s, GROUP_WIDTH) * jax.nn.silu(z)
    y = rmsnorm(y.reshape(b, s, SSD_GROUPS, SSD_NORM_GROUP), norm_g.reshape(SSD_GROUPS, SSD_NORM_GROUP))
    return y.reshape(b, s, GROUP_WIDTH)

def stick_breaking(q, k, v):
    b, s, h, d = q.shape
    nb = s // SB_BLOCK
    scale = d ** -0.5
    key_pos = jnp.arange(s)
    qb = jnp.moveaxis(q.reshape(b, nb, SB_BLOCK, h, d), 1, 0)

    def block(args):
        q_blk, i = args
        logits = jnp.einsum('bthd,bshd->bhts', q_blk, k).astype(jnp.float32) * scale
        q_pos = i * SB_BLOCK + jnp.arange(SB_BLOCK)
        causal = key_pos[None, :] < q_pos[:, None]
        log_beta = jax.nn.log_sigmoid(logits)
        log_1mb = jnp.where(causal, jax.nn.log_sigmoid(-logits), 0.0)
        tail = lax.cumsum(log_1mb, axis=3, reverse=True) - log_1mb
        w = jnp.where(causal, jnp.exp(log_beta + tail), 0.0)
        return jnp.einsum('bhts,bshd->bthd', w.astype(v.dtype), v)

    out = lax.map(block, (qb, jnp.arange(nb)))
    return jnp.moveaxis(out, 0, 1).reshape(b, s, h * d)

def memory_read(q, mem_n, w_mem_kv):
    b, s, h, d = q.shape
    kv = mem_n @ w_mem_kv
    k, v = jnp.split(kv, 2, axis=-1)
    k = k.reshape(b, -1, h, d)
    v = v.reshape(b, -1, h, d)
    logits = jnp.einsum('bshd,bmhd->bhsm', q, k).astype(jnp.float32) * (d ** -0.5)
    p = jax.nn.softmax(logits, axis=-1).astype(v.dtype)
    return jnp.einsum('bhsm,bmhd->bshd', p, v).reshape(b, s, h * d)

def hybrid_layer(x, mem, pre_g, post_g, w_in, conv_w, conv_b, dt_bias, a_log, d_skip,
                 ssd_norm_g, mem_norm_g, w_mem_kv, w_out):
    b, s, _ = x.shape
    hn = rmsnorm(x, pre_g)
    proj = hn @ w_in
    (ret_q, ret_k, ret_v, ret_g, xbc, z, dt_raw,
     sb_q, sb_k, sb_v, sb_g, mem_q, mem_g) = jnp.split(proj, list(np.cumsum(IN_SIZES)[:-1]), axis=-1)
    y_ret = retention(ret_q.reshape(b, s, RET_HEADS, RET_HEAD_DIM),
                      ret_k.reshape(b, s, RET_HEADS, RET_HEAD_DIM),
                      ret_v.reshape(b, s, RET_HEADS, RET_HEAD_DIM)) * jax.nn.silu(ret_g)
    y_ssd = ssd_mixer(xbc, z, dt_raw, conv_w, conv_b, dt_bias, a_log, d_skip, ssd_norm_g)
    y_sb = stick_breaking(sb_q.reshape(b, s, SB_HEADS, SB_HEAD_DIM),
                          sb_k.reshape(b, s, SB_HEADS, SB_HEAD_DIM),
                          sb_v.reshape(b, s, SB_HEADS, SB_HEAD_DIM)) * jax.nn.silu(sb_g)
    y_mem = memory_read(mem_q.reshape(b, s, MEM_HEADS, MEM_HEAD_DIM),
                        rmsnorm(mem, mem_norm_g), w_mem_kv) * jax.nn.silu(mem_g)
    y = jnp.concatenate([y_ret, y_ssd, y_sb, y_mem], axis=-1) @ w_out
    return x + rmsnorm(y, post_g)

def first_inputs(seed: int = 0) -> dict:
    key = jax.random.key(seed)
    ks = jax.random.split(key, 14)
    f32 = jnp.float32

    def gain(k, shape):
        return 1.0 + 0.02 * jax.random.normal(k, shape, f32)

    dt0 = jnp.exp(jax.random.uniform(ks[7], (DEPTH, SSD_HEADS), f32, math.log(DT_MIN), math.log(DT_MAX)))
    return {
        'x': jax.random.normal(ks[0], (BATCH, SEQ, D_MODEL), f32),
        'mem': jax.random.normal(ks[1], (BATCH, N_MEM, D_MODEL), f32),
        'pre_norm_g': gain(ks[2], (DEPTH, D_MODEL)),
        'post_norm_g': gain(ks[3], (DEPTH, D_MODEL)),
        'w_in': jax.random.normal(ks[4], (DEPTH, D_MODEL, D_IN), f32) * D_MODEL ** -0.5,
        'conv_w': jax.random.normal(ks[5], (DEPTH, SSD_CONV, SSD_CONV_DIM), f32) * SSD_CONV ** -0.5,
        'conv_b': 0.02 * jax.random.normal(ks[6], (DEPTH, SSD_CONV_DIM), f32),
        'dt_bias': dt0 + jnp.log(-jnp.expm1(-dt0)),
        'a_log': jnp.log(jax.random.uniform(ks[8], (DEPTH, SSD_HEADS), f32, A_INIT_MIN, A_INIT_MAX)),
        'd_skip': gain(ks[9], (DEPTH, SSD_HEADS)),
        'ssd_norm_g': gain(ks[10], (DEPTH, GROUP_WIDTH)),
        'mem_norm_g': gain(ks[11], (DEPTH, D_MODEL)),
        'w_mem_kv': jax.random.normal(ks[12], (DEPTH, D_MODEL, 2 * GROUP_WIDTH), f32) * D_MODEL ** -0.5,
        'w_out': jax.random.normal(ks[13], (DEPTH, D_MIX, D_MODEL), f32) * D_MIX ** -0.5,
    }

def first_block(x, mem, pre_norm_g, post_norm_g, w_in, conv_w, conv_b, dt_bias, a_log, d_skip,
              ssd_norm_g, mem_norm_g, w_mem_kv, w_out):
    for l in range(DEPTH):
        x = hybrid_layer(x, mem, pre_norm_g[l], post_norm_g[l], w_in[l], conv_w[l], conv_b[l],
                         dt_bias[l], a_log[l], d_skip[l], ssd_norm_g[l], mem_norm_g[l],
                         w_mem_kv[l], w_out[l])
    return x


D_FF = 2816
D_POOL = 256
POOL_WINDOWS = (2, 4, 8, 16)
POOL_GROUP = D_POOL // len(POOL_WINDOWS)
D_CONV = 256
CONV_WIDTH = 3
NA_HEADS = 8
NA_HEAD_DIM = 64
D_NA = NA_HEADS * NA_HEAD_DIM
D_MIX_2 = D_POOL + D_CONV + D_NA
GRID_W = 64
NA_ROWS = 8
NA_COLS = 16
D_IN_2 = D_POOL + 3 * D_CONV + 3 * D_NA
ALPHA = (2.0 * DEPTH) ** 0.25
BETA = (8.0 * DEPTH) ** -0.25
LN_EPS = 1e-5
NEG_INF = -1e30


def layer_norm(x, g, b):
    xf = x.astype(jnp.float32)
    mu = jnp.mean(xf, axis=-1, keepdims=True)
    var = jnp.mean(jnp.square(xf - mu), axis=-1, keepdims=True)
    y = (xf - mu) * lax.rsqrt(var + LN_EPS)
    return (y * g.astype(jnp.float32) + b.astype(jnp.float32)).astype(x.dtype)

def swiglu(x, w_gate, w_up, w_down):
    return (jax.nn.silu(x @ w_gate) * (x @ w_up)) @ w_down

def pool_mixer(u, pool_w, pool_scale):
    bsz, s, _ = u.shape
    ng = len(POOL_WINDOWS)
    uf = u.astype(jnp.float32).reshape(bsz, s, ng, POOL_GROUP)
    cs = jnp.concatenate([jnp.zeros((bsz, 1, ng, POOL_GROUP), jnp.float32),
                          jnp.cumsum(uf, axis=1)], axis=1)
    t = jnp.arange(s)
    outs = []
    for g, w in enumerate(POOL_WINDOWS):
        lo = jnp.clip(t - w // 2, 0, s)
        hi = jnp.clip(t - w // 2 + w, 0, s)
        cnt = (hi - lo).astype(jnp.float32)[None, :, None]
        mean = (cs[:, hi, g] - cs[:, lo, g]) / cnt
        outs.append(mean - uf[:, :, g])
    p = jnp.stack(outs, axis=2).astype(u.dtype)
    y = jnp.einsum('bsgc,gcd->bsgd', p, pool_w) * pool_scale.reshape(ng, POOL_GROUP)
    return y.reshape(bsz, s, D_POOL)

def gated_conv_mixer(gate_b, gate_c, h, conv_w):
    z = gate_c * h
    zp = jnp.pad(z, ((0, 0), (1, 1), (0, 0)))
    y = conv_w[0] * zp[:, :-2] + conv_w[1] * zp[:, 1:-1] + conv_w[2] * zp[:, 2:]
    return gate_b * y

def neighbourhood_attention(q, k, v, rpb):
    bsz, s, _ = q.shape
    rows = s // GRID_W
    kr = min(NA_ROWS, rows)
    shp = (bsz, rows, GRID_W, NA_HEADS, NA_HEAD_DIM)
    q, k, v = q.reshape(shp), k.reshape(shp), v.reshape(shp)
    r = jnp.arange(rows)
    row_start = jnp.clip(r - kr // 2, 0, rows - kr)
    row_idx = row_start[:, None] + jnp.arange(kr)[None, :]
    kb = k[:, row_idx]
    vb = v[:, row_idx]
    c = jnp.arange(GRID_W)
    col_start = jnp.clip(c - NA_COLS // 2, 0, GRID_W - NA_COLS)
    col_valid = (c[None, :] >= col_start[:, None]) & (c[None, :] < col_start[:, None] + NA_COLS)
    dr = row_idx - r[:, None] + (NA_ROWS - 1)
    dc = jnp.clip(c[None, :] - c[:, None], -(NA_COLS - 1), NA_COLS - 1) + (NA_COLS - 1)
    bias = rpb[:, dr[:, None, :, None], dc[None, :, None, :]]
    scores = jnp.einsum('brqhd,brikhd->bhrqik', q, kb).astype(jnp.float32) * (NA_HEAD_DIM ** -0.5)
    scores = scores + bias.astype(jnp.float32)
    scores = jnp.where(col_valid[:, None, :], scores, NEG_INF)
    p = jax.nn.softmax(scores, axis=(-2, -1)).astype(v.dtype)
    o = jnp.einsum('bhrqik,brikhd->brqhd', p, vb)
    return o.reshape(bsz, s, D_NA)

def second_inputs(seed: int = 0) -> dict:
    key = jax.random.key(seed)
    ks = jax.random.split(key, 16)
    L, D, F = DEPTH, D_MODEL, D_FF
    nrm = lambda k, shp: jax.random.normal(k, shp, jnp.float32)
    x = nrm(ks[0], (BATCH, SEQ, D))
    ffn1_w_gate = nrm(ks[1], (L, D, F)) * D ** -0.5
    ffn1_w_up = nrm(ks[2], (L, D, F)) * D ** -0.5
    ffn1_w_down = nrm(ks[3], (L, F, D)) * (BETA * F ** -0.5)
    ffn2_w_gate = nrm(ks[4], (L, D, F)) * D ** -0.5
    ffn2_w_up = nrm(ks[5], (L, D, F)) * D ** -0.5
    ffn2_w_down = nrm(ks[6], (L, F, D)) * (BETA * F ** -0.5)
    col_scale = jnp.concatenate([
        jnp.ones((D_POOL + 2 * D_CONV,), jnp.float32),
        jnp.full((D_CONV,), BETA, jnp.float32),
        jnp.ones((2 * D_NA,), jnp.float32),
        jnp.full((D_NA,), BETA, jnp.float32)])
    w_in = nrm(ks[7], (L, D, D_IN_2)) * D ** -0.5 * col_scale
    pool_w = nrm(ks[8], (L, len(POOL_WINDOWS), POOL_GROUP, POOL_GROUP)) * POOL_GROUP ** -0.5
    pool_scale = 1.0 + 0.1 * nrm(ks[9], (L, D_POOL))
    conv_w = nrm(ks[10], (L, CONV_WIDTH, D_CONV)) * CONV_WIDTH ** -0.5
    rpb = 0.02 * nrm(ks[11], (L, NA_HEADS, 2 * NA_ROWS - 1, 2 * NA_COLS - 1))
    w_out = nrm(ks[12], (L, D_MIX_2, D)) * (BETA * D_MIX_2 ** -0.5)
    ln_g = 1.0 + 0.05 * nrm(ks[13], (L, 3, D))
    ln_b = 0.02 * nrm(ks[14], (L, 3, D))
    return {"x": x,
            "ffn1_w_gate": ffn1_w_gate, "ffn1_w_up": ffn1_w_up, "ffn1_w_down": ffn1_w_down,
            "ffn2_w_gate": ffn2_w_gate, "ffn2_w_up": ffn2_w_up, "ffn2_w_down": ffn2_w_down,
            "w_in": w_in, "pool_w": pool_w, "pool_scale": pool_scale, "conv_w": conv_w,
            "rpb": rpb, "w_out": w_out, "ln_g": ln_g, "ln_b": ln_b}

def second_block(x, ffn1_w_gate, ffn1_w_up, ffn1_w_down, ffn2_w_gate, ffn2_w_up, ffn2_w_down,
              w_in, pool_w, pool_scale, conv_w, rpb, w_out, ln_g, ln_b):
    splits = np.cumsum([D_POOL, D_CONV, D_CONV, D_CONV, D_NA, D_NA])
    for l in range(DEPTH):
        x = layer_norm(ALPHA * x + 0.5 * swiglu(x, ffn1_w_gate[l], ffn1_w_up[l], ffn1_w_down[l]),
                       ln_g[l, 0], ln_b[l, 0])
        proj = x @ w_in[l]
        u, gb, gc, h, q, k, v = jnp.split(proj, splits, axis=-1)
        y_a = pool_mixer(u, pool_w[l], pool_scale[l])
        y_b = gated_conv_mixer(gb, gc, h, conv_w[l])
        y_c = neighbourhood_attention(q, k, v, rpb[l])
        y = jnp.concatenate([y_a, y_b, y_c], axis=-1) @ w_out[l]
        x = layer_norm(ALPHA * x + y, ln_g[l, 1], ln_b[l, 1])
        x = layer_norm(ALPHA * x + 0.5 * swiglu(x, ffn2_w_gate[l], ffn2_w_up[l], ffn2_w_down[l]),
                       ln_g[l, 2], ln_b[l, 2])
    return x


def setup_inputs(seed=0):
    out = dict(first_inputs(seed))
    for name, value in second_inputs(seed + 1).items():
        if name != "x":
            out[name + "_2"] = value
    return out


def reference(
    x, mem, pre_norm_g, post_norm_g, w_in, conv_w, conv_b, dt_bias, a_log, d_skip, ssd_norm_g,
    mem_norm_g, w_mem_kv, w_out, ffn1_w_gate_2, ffn1_w_up_2, ffn1_w_down_2, ffn2_w_gate_2,
    ffn2_w_up_2, ffn2_w_down_2, w_in_2, pool_w_2, pool_scale_2, conv_w_2, rpb_2, w_out_2,
    ln_g_2, ln_b_2,
):
    x = first_block(
        x, mem, pre_norm_g, post_norm_g, w_in, conv_w, conv_b, dt_bias, a_log, d_skip,
        ssd_norm_g, mem_norm_g, w_mem_kv, w_out,
    )
    return second_block(
        x, ffn1_w_gate_2, ffn1_w_up_2, ffn1_w_down_2, ffn2_w_gate_2, ffn2_w_up_2, ffn2_w_down_2,
        w_in_2, pool_w_2, pool_scale_2, conv_w_2, rpb_2, w_out_2, ln_g_2, ln_b_2,
    )


_drawn_inputs = setup_inputs


def setup_inputs(seed=0):
    import zlib

    import numpy as np

    out = dict(_drawn_inputs(seed))
    spreads = {}
    factors = {'d_skip': 4.763,
     'ssd_norm_g': 3.315,
     'mem_norm_g': 8.0,
     'pool_scale_2': 2.943,
     'rpb_2': 8.0}
    for name, (base, spread) in spreads.items():
        noise = np.random.default_rng([zlib.crc32(name.encode()), seed]).standard_normal(out[name].shape)
        drawn = base * np.exp(spread * noise) if base else spread * noise
        out[name] = jnp.asarray(drawn.astype(out[name].dtype))
    for name, factor in factors.items():
        out[name] = (out[name] * factor).astype(out[name].dtype)
    return out
```

```python
from contextlib import ExitStack

import numpy as np

import concourse.bass as bass
from concourse import mybir

F32 = mybir.dt.float32
F32R = mybir.dt.float32r
ALU = mybir.AluOpType
ACT = mybir.ActivationFunctionType
AX = mybir.AxisListType

P = 128
DEPTH = 2
SEQ = 512
D = 1024
TILES = SEQ // P
DCH = D // P
N_MEM = 256
GW = 512
HEADS = 4
HD = 128
SSD_H = 8
D_FF = 2816
EPS = 1e-6
LN_EPS = 1e-5
ALPHA = (2.0 * DEPTH) ** 0.25
SCALE = HD ** -0.5
NEG = -1e30

KB = 4
BC = 512
BLOCK1 = 38
BLOCK2 = 82
UNITS1 = 23
UNITS2 = 2 * (11 + 4) + 5 + 2
FF_HALVES = ((6, (4, 4, 4)), (5, (4, 4, 2)))

NA_H = 8
NA_D = 64
GRID_W = 64
NA_R = 8
CONV2 = 256
LOG_G = np.log(1.0 - 2.0 ** (-5.0 - np.arange(HEADS, dtype=np.float32))).astype(np.float32)
RET_DECAY = [float(x) for x in np.exp(np.float32(P) * LOG_G)]

PRE_G, POST_G, MEM_G, SSD_G, DT_B, A_LOG, D_SKIP = 0, 1024, 2048, 3072, 3584, 3592, 3600
ROW1 = 3608


def constants():
    f = np.float32
    i = np.arange(P)
    inv = f(10000.0) ** (-np.arange(0, HD, 2, dtype=f) / f(HD))
    ang = np.arange(SEQ, dtype=f)[:, None] * inv[None, :].astype(f)
    cos, sin = np.cos(ang).T, np.sin(ang).T
    rot = np.zeros((P, P), f)
    rot[i[64:], i[:64]] = -1.0
    rot[i[:64], i[64:]] = 1.0
    rel = (i[None, :] - i[:, None]).astype(f)
    intra = np.stack([np.where(rel >= 0, np.exp(np.maximum(rel, 0) * g), 0) * f(SCALE) for g in LOG_G], 1)
    xi = np.stack([np.broadcast_to(np.exp((i + 1).astype(f) * g), (P, P)) for g in LOG_G], 1)
    zeta = np.stack([np.exp((P - 1 - i).astype(f) * g) * f(SCALE) for g in LOG_G], 1)
    first = {
        "cos": np.concatenate([cos, cos]), "sin": np.concatenate([sin, sin]), "rot": rot,
        "upto": (i[:, None] <= i[None, :]), "from": (i[:, None] >= i[None, :]), "ones": np.ones((P, P)),
        "upto_neg": np.where(i[:, None] <= i[None, :], 0, NEG), "before": (i[:, None] < i[None, :]),
        "before_neg": np.where(i[:, None] < i[None, :], 0, NEG),
        "intra": intra.reshape(P, -1), "xi": xi.reshape(P, -1), "zeta": zeta,
    }
    cl = i // NA_R
    def mask(qb, kb):
        c, k = 16 * qb + cl[:, None], 16 * kb + cl[None, :]
        lo = np.clip(c - 8, 0, GRID_W - 16)
        return np.where((k >= lo) & (k < lo + 16), 0, NEG)
    masks = np.stack([mask(0, 0), mask(2, 1), mask(1, 1), mask(1, 2), mask(3, 3)], 1)
    assert (mask(0, 1) == mask(1, 2)).all() and (mask(3, 2) == mask(2, 1)).all() and (mask(2, 2) == mask(1, 1)).all()
    sel = np.zeros((P, NA_R, P))
    for k in range(NA_R):
        sel[k - i % NA_R + 7, k, i] = 1.0
    pool = np.zeros((P, 4, 4, 144))
    t = np.arange(SEQ)
    for g, w in enumerate((2, 4, 8, 16)):
        lo, hi = np.clip(t - w // 2, 0, SEQ), np.clip(t - w // 2 + w, 0, SEQ)
        m = ((t[:, None] >= lo[None]) & (t[:, None] < hi[None])) / (hi - lo)[None].astype(f) - np.eye(SEQ)
        for c in range(4):
            for col in range(144):
                tt = 128 * c + col - 8
                if 0 <= tt < SEQ:
                    pool[:, g, c, col] = m[128 * c:128 * c + 128, tt]
    second = {"masks": masks.reshape(P, -1), "pool": pool.reshape(P, -1)}
    return {"ident": np.eye(P)}, first, second, {"sel": sel.reshape(P, -1)[:15]}


def columns(parts):
    at, out = 0, {}
    for name, a in parts.items():
        out[name] = (at, at + a.shape[1])
        at += a.shape[1]
    return out, at


def build(nc, x_in, mem_in, stream, const0, const1, const2, rows1, conv1, w_dt, ln_rows, pool_w, cols2, rpb, sel_in, out):
    c0, c1, c2, _ = constants()
    _, N0 = columns(c0)
    at1, N1 = columns(c1)
    at2, N2 = columns(c2)

    ctx = ExitStack()
    with ctx:
        def sb(name, shape, dt=F32, on=ctx):
            return on.enter_context(nc.sbuf_tensor(name, shape, dt))

        def sem(name):
            return ctx.enter_context(nc.semaphore(name))

        ident = sb("ident", [P, N0])
        x = sb("x", [P, TILES, D])
        xT_hi = sb("xT_hi", [P, DCH, SEQ], F32R)
        xT_lo = sb("xT_lo", [P, DCH, SEQ], F32R)
        raw = sb("raw", [P, 2, KB, BC])
        w_hi = sb("w_hi", [P, 2, KB, BC], F32R)
        w_lo = sb("w_lo", [P, 2, KB, BC], F32R)
        rs_v = sb("rs_v", [P, 16])
        rs_r = sb("rs_r", [P, 16])
        rs_t = sb("rs_t", [P, 16])
        stats = sb("stats", [P, 16, 6])
        mean_var = sb("mean_var", [P, 16, 2])

        one = ExitStack()
        cst = sb("cst", [P, N1], on=one)
        row = sb("row", [P, ROW1], on=one)
        conv = sb("conv", [P, 8, 5], on=one)
        wdt = sb("wdt", [P, 8, 8], on=one)
        wdt_hi = sb("wdt_hi", [P, 8, 8], F32R, on=one)
        wdt_lo = sb("wdt_lo", [P, 8, 8], F32R, on=one)
        fA = sb("fA", [P, 4, 512], on=one)
        fB = sb("fB", [P, 4, 512], on=one)
        tA = sb("tA", [P, 4, 512], on=one)
        tB = sb("tB", [P, 4, 512], on=one)
        mix = sb("mix", [P, 4, 512], on=one)
        y_acc = sb("y_acc", [P, TILES, D], on=one)
        xn = sb("xn", [P, 2, 1024], on=one)
        state = sb("state", [P, 512], on=one)
        mk = y_acc[:, 0, :].rearrange("p (h n) -> p h n", h=4)
        small = sb("small", [P, 12, 32], on=one)
        with ExitStack() as over:
            sA = sb("sA", [P, 2048], on=over)
            sB = sb("sB", [P, 2048], on=over)
        mixT_hi = sb("mixT_hi", [P, 4, SEQ], F32R, on=one)
        mixT_lo = sb("mixT_lo", [P, 4, SEQ], F32R, on=one)
        one.close()

        two = ExitStack()
        lnr = sb("lnr", [P, 2, D], on=two)
        cst2 = sb("cst2", [P, N2], on=two)
        work = sb("work", [P, 3072], on=two)
        poolw = sb("poolw", [P, 2, P], on=two)
        col2 = sb("col2", [P, 2, 4], on=two)
        nmx = sb("nmx", [P, 4, 32], on=two)
        with ExitStack() as over:
            qkv = sb("qkv", [P, 3 * 4 * SEQ], on=over)
            bm = sb("bm", [P, NA_H, 5, P], on=over)
            y2_hi = sb("y2_hi", [P, 8, SEQ], F32R, on=over)
            y2_lo = sb("y2_lo", [P, 8, SEQ], F32R, on=over)
        h_hi = sb("h_hi", [P, 12, SEQ], F32R, on=two)
        h_lo = sb("h_lo", [P, 12, SEQ], F32R, on=two)
        two.close()

        qp, kp, vp = (qkv[:, i * 2048:i * 2048 + 2048].rearrange("p (c t) -> p c t", c=4) for i in range(3))
        sel = bm[:, :, :, :].rearrange("p h a b -> p (h a b)")[:, 0:1024]
        conv_out = lnr[:, 0, :]
        shifted = qkv[:, 0:3072].rearrange("p (h k e) -> p h k e", h=8, k=8)
        raw_rows = work[:, 256:256 + 1984]

        def c1v(name):
            a, b = at1[name]
            return cst[:, a:b]

        def c2v(name):
            a, b = at2[name]
            return cst2[:, a:b]

        I = ident[:, 0:P]
        G = ctx.enter_context(nc.psum_tensor("G", [P, 4, 512], F32))
        A = ctx.enter_context(nc.psum_tensor("A", [P, 4, 512], F32))

        raw_in = [sem("raw_in0"), sem("raw_in1")]
        hi_done = sem("hi_done")
        lo_done = sem("lo_done")
        blk_used = sem("blk_used")
        g_done = [sem(f"g_done{i}") for i in range(3)]
        g_free = [sem(f"g_free{i}") for i in range(4)]
        pe_end, act_end, pool_end = sem("pe_end"), sem("act_end"), sem("pool_end")
        layer_open = sem("layer_open")
        const_in, x_loaded, out_done = sem("const_in"), sem("x_loaded"), sem("out_done")
        const2_in = sem("const2_in")
        stage = {}

        def st(name):
            if name not in stage:
                stage[name] = sem(name)
            return stage[name]

        landed = {n: sem(n) for n in "row_in conv_in wdt_in mem_in ln_in poolw_in col2_in rpb_in sel_in shift_in".split()}

        def param(eng, l, name, k=1, per=1):
            eng.wait_ge(landed[name], l * (16 * per) + 16 * k)

        for n in ("layer_begun layer_left perm_hi perm_lo row_used ln_used rs_in rs_out act_chain dve_chain "
                  "tr_src tr_done tr_hi tr_lo "
                  "ff_s ff_h ff_hi ff_lo half_done "
                  "ev_mem ev_a ev_b ev_c ev_d "
                  "m_log m_nb m_p m_pt m_ptc m_o m_y "
                  "rot_done rot_used ret_ready rz_t rz_used r_s r_sm r_y r_kv r_yu r_st mix_ready "
                  "s_log s_ab s_ln s_sp s_cum s_d s_w s_pv s_pvu "
                  "conv_done conv_silu x_t x_tc dt_p dt_ab dt_ln dt_da dt_cs dt_sub dt_ex dt_al wdt_h wdt_l "
                  "d_bc d_t d_e d_sc d_y d_yu d_st "
                  "b_g b_gc b_bm b_raw p_t p_tc p_y z_y y2h y2l n_s n_m n_p n_pn n_t n_tc n_o n_oh n_ol").split():
            st(n)
        S = stage
        nums = [s.num for s in S.values()]
        STAGES = range(nums[0], nums[-1] + 1)
        assert nums == list(STAGES)

        def bcast(ap, shape):
            return ap.to_broadcast(shape)

        block = ctx.enter_context(nc.Block())

        def perm_view(ap):
            return ap.rearrange("p (r c) -> p c r", c=GRID_W)

        @block.sync
        def _(sp):
            pairs = DEPTH * (BLOCK1 + BLOCK2) // 2
            with sp.Fori(0, pairs) as m:
                for s in range(2):
                    sp.wait_ge(lo_done, 2 * m + s + 1)
                    sp.dma_start(raw[:, s, :, :].rearrange("p k n -> p (k n)"),
                                 stream[bass.ds(2 * m + s, 1)].rearrange("o p n -> (o p) n")).then_inc(raw_in[s], 16)

        @block.tensor
        def _(pe):
            mm = nc.tensor.matmul
            pe.sem_inc(blk_used, 2)

            class Pos:
                pair, off, ubase, u = 0, 0, 0, 0

            def gemm(kbs, jobs):
                c = 0
                for b, nk in enumerate(kbs):
                    s = Pos.off % 2
                    pe.wait_ge(lo_done, 2 * Pos.pair + Pos.off + 3)
                    for n, (bank, emits) in enumerate(jobs):
                        if b == 0:
                            pe.wait_ge(g_free[bank], Pos.ubase + Pos.u + 1)
                        for e, emit in enumerate(emits):
                            for k in range(nk):
                                last = emit(c + k, w_hi[:, s, k, :], w_lo[:, s, k, :],
                                            b == 0 and k == 0 and e == 0, b == len(kbs) - 1 and k == nk - 1)
                        if n == 3:
                            last.then_inc(blk_used, 1)
                        elif b == len(kbs) - 1:
                            last.then_inc(g_done[bank], 1)
                    Pos.off += 1
                    c += nk
                Pos.u += 1

            def results_read():
                for bank in range(4):
                    pe.wait_ge(g_free[bank], Pos.ubase + Pos.u + 1)

            def feat(bank, hi, lo, col, n=SEQ, dst=None):
                o = G[:, bank, 0:n]

                def emit(c, wh, wl, start, stop):
                    a = wh[:, col:col + P]
                    mm(o, a, hi[:, c, 0:n], start=start, stop=False)
                    mm(o, a, lo[:, c, 0:n], start=False, stop=False)
                    return mm(o, wl[:, col:col + P], hi[:, c, 0:n], start=False, stop=stop)
                return emit

            def tok(bank, hi, lo, tile, col=0, n=BC, at=0, own_start=True):
                o = G[:, bank, at:at + n]

                def emit(c, wh, wl, start, stop):
                    a, b = hi[:, c, tile * P:tile * P + P], lo[:, c, tile * P:tile * P + P]
                    k = dict(skip_group_check=True) if n < BC else {}
                    mm(o, a, wh[:, col:col + n], start=start and own_start, stop=False, **k)
                    mm(o, a, wl[:, col:col + n], start=False, stop=False, **k)
                    return mm(o, b, wh[:, col:col + n], start=False, stop=stop, **k)
                return emit

            def feat4(n=SEQ):
                gemm((4, 4), [(o, [feat(o, xT_hi, xT_lo, o * P, n)]) for o in range(4)])

            def tok4(kbs=(4, 4), hi=xT_hi, lo=xT_lo):
                gemm(kbs, [(o, [tok(o, hi, lo, o)]) for o in range(4)])

            class N:
                tr = 0

            def transposes(src, tiles, groups):
                for t in range(tiles):
                    for g in range(groups):
                        if N.tr >= 4:
                            pe.wait_ge(S["tr_lo"], N.tr - 3)
                        pe.wait_ge(S["tr_src"], N.src + t + 1)
                        for c in range(4):
                            last = nc.tensor.transpose(A[:, N.tr % 4, c * P:c * P + P],
                                                       src(t)[:, (4 * g + c) * P:(4 * g + c + 1) * P], I)
                        last.then_inc(S["tr_done"], 1)
                        N.tr += 1
                N.src += tiles

            def mem_attention():
                results_read()
                for q in range(TILES):
                    if q:
                        pe.wait_ge(S["tr_src"], N.src + q)
                    for h in range(HEADS):
                        last = mm(A[:, h // 2, (h % 2) * 256:(h % 2) * 256 + 256], fA[:, h, q * P:q * P + P],
                                  mk[:, h, :], start=True, stop=True)
                    last.then_inc(S["m_log"], 1)
                    pe.wait_ge(S["m_p"], 4 * (q + 1))
                    pm = sA[:, 0:1024]
                    for i in range(8):
                        last = nc.tensor.transpose(A[:, 2 + i // 4, (i % 4) * P:(i % 4 + 1) * P],
                                                   pm[:, i * P:i * P + P], I)
                    last.then_inc(S["m_pt"], 1)
                    pe.wait_ge(S["m_ptc"], q + 1)
                    for h in range(HEADS):
                        for k in range(2):
                            last = mm(A[:, 0, h * P:h * P + P], sB[:, (2 * h + k) * P:(2 * h + k + 1) * P],
                                      tA[:, k, h * P:h * P + P], start=(k == 0), stop=(k == 1))
                    last.then_inc(S["m_o"], 1)

            def retention():
                results_read()
                for i in range(8):
                    if i >= 4:
                        pe.wait_ge(S["rot_used"], i - 3)
                    mm(A[:, i % 4, :], c1v("rot"), (fA if i < 4 else fB)[:, i % 4, :],
                       start=True, stop=True).then_inc(S["rot_done"], 1)
                pe.wait_ge(S["ret_ready"], 1)
                for c in range(3):
                    for h in range(HEADS):
                        last = nc.tensor.transpose(A[:, c, h * P:h * P + P], fB[:, h, c * P:c * P + P], I)
                    last.then_inc(S["rz_t"], 1)
                pe.wait_ge(S["rz_used"], 3)
                for c in range(TILES):
                    for h in range(HEADS):
                        last = mm(A[:, 0, h * P:h * P + P], fB[:, h, c * P:c * P + P], fA[:, h, c * P:c * P + P],
                                  start=True, stop=True)
                    last.then_inc(S["r_s"], 1)
                    if c < 3:
                        if c:
                            pe.wait_ge(S["r_st"], 4 * c)
                        for h in range(HEADS):
                            last = mm(A[:, 2, h * P:h * P + P], sB[:, c * 512 + h * P:c * 512 + h * P + P],
                                      tA[:, c, h * P:h * P + P], start=True, stop=True)
                        last.then_inc(S["r_kv"], 1)
                    pe.wait_ge(S["r_sm"], c + 1)
                    if c:
                        pe.wait_ge(S["r_yu"], c)
                        pe.wait_ge(S["r_st"], 4 * c)
                    for h in range(HEADS):
                        last = mm(A[:, 1, h * P:h * P + P], xn[:, 0, h * P:h * P + P], tA[:, c, h * P:h * P + P],
                                  start=True, stop=(c == 0))
                        if c:
                            last = mm(A[:, 1, h * P:h * P + P], sA[:, h * 512 + c * P:h * 512 + c * P + P],
                                      state[:, h * P:h * P + P], start=False, stop=True)
                    last.then_inc(S["r_y"], 1)

            SB_AT = (0, 512, 1024, 896)

            def stick():
                results_read()
                flat = A[:, :, :].rearrange("p b n -> p (b n)")
                for h in range(HEADS):
                    if h:
                        pe.wait_ge(S["s_d"], h)
                    for i in range(4):
                        n = (4 - i) * P
                        last = mm(flat[:, SB_AT[i]:SB_AT[i] + n], fB[:, h, i * P:i * P + P], fA[:, h, i * P:SEQ],
                                  start=True, stop=True, skip_group_check=True)
                    last.then_inc(S["s_log"], 1)
                    pe.wait_ge(S["s_sp"], h + 1)
                    for i in range(4):
                        for k in range(i, 4):
                            w, n = (k - i) * P, (4 - k) * P
                            last = mm(flat[:, SB_AT[i] + w:SB_AT[i] + w + n], c1v("from" if k == i else "ones"),
                                      sB[:, SB_AT[k]:SB_AT[k] + n], start=(k == i and i != 3), stop=(k == 3),
                                      skip_group_check=True)
                        if i == 1:
                            last = mm(flat[:, SB_AT[3]:SB_AT[3] + P], c1v("from"), sB[:, SB_AT[3]:SB_AT[3] + P],
                                      start=False, stop=True, skip_group_check=True)
                        if i == 2:
                            break
                    last.then_inc(S["s_cum"], 1)
                    pe.wait_ge(S["s_w"], h + 1)
                    if h:
                        pe.wait_ge(S["s_pvu"], h)
                    for j in range(4):
                        for i in range(j + 1):
                            last = mm(A[:, 3, j * P:j * P + P], sA[:, SB_AT[i] + (j - i) * P:SB_AT[i] + (j - i + 1) * P],
                                      tA[:, i, h * P:h * P + P], start=(i == 0), stop=(i == j))
                    last.then_inc(S["s_pv"], 1)

            def ssd():
                pe.wait_ge(S["wdt_l"], 1)
                for t in range(TILES):
                    for k in range(8):
                        o = A[:, 3, 8 * t:8 * t + 8]
                        a, b = xT_hi[:, k, t * P:t * P + P], xT_lo[:, k, t * P:t * P + P]
                        mm(o, a, wdt_hi[:, k, :], start=(k == 0), stop=False)
                        mm(o, a, wdt_lo[:, k, :], start=False, stop=False)
                        last = mm(o, b, wdt_hi[:, k, :], start=False, stop=(k == 7))
                last.then_inc(S["dt_p"], 1)
                pe.wait_ge(S["conv_silu"], 8)
                for c in range(TILES):
                    if c >= 2:
                        pe.wait_ge(S["x_tc"], 2 * (c - 1))
                    b = c % 2
                    for i in range(4):
                        nc.tensor.transpose(A[:, b, i * P:i * P + P], fA[:, i, c * P:c * P + P], I)
                    for i in range(2):
                        if c >= 1 and i == 0:
                            pe.wait_ge(S["x_tc"], 2 * c)
                        last = nc.tensor.transpose(A[:, 2, i * P:i * P + P], fB[:, i, c * P:c * P + P], I)
                    last.then_inc(S["x_t"], 1)
                pe.wait_ge(S["dt_da"], 1)
                pe.wait_ge(S["x_tc"], 8)
                da = small[:, 3, :]
                mm(A[:, 2, 0:32], c1v("upto"), da, start=True, stop=True)
                mm(A[:, 2, 32:64], c1v("ones"), da, start=True, stop=True).then_inc(S["dt_cs"], 1)
                pe.wait_ge(S["dt_ex"], 3)
                pe.wait_ge(S["dt_sub"], 1)
                for c in range(TILES):
                    if c:
                        pe.wait_ge(S["d_yu"], c)
                        pe.wait_ge(S["d_st"], c)
                    for h in range(SSD_H):
                        mm(A[:, h // 4, (h % 4) * P:(h % 4 + 1) * P], bcast(da[:, 8 * c + h:8 * c + h + 1], [P, P]),
                           c1v("upto"), start=True, stop=True)
                    for g in range(2):
                        last = mm(A[:, 2, g * P:g * P + P], fB[:, g, c * P:c * P + P], fB[:, 2 + g, c * P:c * P + P],
                                  start=True, stop=True)
                    last.then_inc(S["d_bc"], 1)
                    pe.wait_ge(S["d_sc"], c + 1)
                    for h in range(SSD_H):
                        last = mm(A[:, 3, h * 64:h * 64 + 64], sB[:, 1024 + h * P:1024 + h * P + P],
                                  fA[:, c, h * 64:h * 64 + 64], start=True, stop=True)
                    if c:
                        for g in range(2):
                            last = mm(A[:, 0, g * 256:g * 256 + 256], fB[:, 2 + g, c * P:c * P + P],
                                      state[:, g * 256:g * 256 + 256], start=True, stop=True)
                    if c < 3:
                        for g in range(2):
                            last = mm(A[:, 1, g * 256:g * 256 + 256], xn[:, c // 2, (c % 2) * 256 + g * P:(c % 2) * 256 + g * P + P],
                                      sA[:, c * 512 + g * 256:c * 512 + g * 256 + 256], start=True, stop=True)
                    last.then_inc(S["d_y"], 1)

            def mixer_out():
                pe.wait_ge(S["tr_src"], N.src + TILES)
                transposes(lambda t: mix[:, t, :], TILES, 1)
                pe.wait_ge(S["tr_lo"], N.tr)
                for half in range(2):
                    tok4(kbs=(4,), hi=mixT_hi, lo=mixT_lo)

            pe.wait_ge(const_in, 16 * 2)
            with pe.Fori(0, DEPTH) as l:
                Pos.l = l
                Pos.pair, Pos.off, Pos.ubase, Pos.u = l * (BLOCK1 // 2), 0, l * UNITS1, 0
                N.tr, N.src = 0, 0
                pe.wait_ge(layer_open, l + 1)
                pe.sem_inc(S["layer_begun"], 1)
                transposes(lambda t: xn[:, t % 2, :], 2, 2)
                pe.wait_ge(S["tr_lo"], N.tr)
                feat4(N_MEM)
                gemm((4, 4), [(o, [tok(o, xT_hi, xT_lo, o // 2, col=(o % 2) * 256, n=256)]) for o in range(4)])
                transposes(lambda t: xn[:, t % 2, :], 4, 2)
                pe.wait_ge(S["tr_lo"], N.tr)
                feat4()
                tok4()
                mem_attention()
                mixer_out()
                feat4()
                feat4()
                tok4()
                tok4()
                retention()
                mixer_out()
                feat4()
                feat4()
                tok4()
                tok4()
                stick()
                mixer_out()
                feat4()
                feat4()
                tok4()
                ssd()
                mixer_out()
                assert Pos.off == BLOCK1 and Pos.u == UNITS1
                pe.sem_inc(pe_end, 1)

            def ffn():
                for n, (units, downs) in enumerate(FF_HALVES):
                    base_pair, base_off, base_u = Pos.pair, Pos.off, Pos.u
                    assert base_off % 2 == 0
                    ub = Pos.ubase
                    with pe.Fori(0, units) as u:
                        Pos.pair, Pos.off, Pos.ubase, Pos.u = base_pair + u, base_off, ub + u, base_u
                        feat4()
                    Pos.pair, Pos.off, Pos.ubase, Pos.u = base_pair, base_off + 2 * units, ub, base_u + units
                    N.ff += 2 * units
                    pe.wait_ge(S["ff_lo"], N.ff)
                    for half in range(2):
                        gemm(downs, [(o, [tok(o, h_hi, h_lo, o)]) for o in range(4)])

            def bias():
                param(pe, Pos.l, "rpb_in")
                param(pe, Pos.l, "sel_in")
                for k in range(NA_R):
                    if k >= 4:
                        pe.wait_ge(S["b_gc"], k - 3)
                    mm(A[:, k % 4, 0:248], sel[0:15, k * P:k * P + P], work[0:15, 0:248],
                       start=True, stop=True).then_inc(S["b_g"], 1)
                pe.wait_ge(S["b_gc"], NA_R)

            def pool_mixer():
                results_read()
                param(pe, Pos.l, "poolw_in")
                for ch in range(2):
                    for gg in range(2):
                        g = 2 * ch + gg
                        for c in range(4):
                            lo, hi = max(0, 128 * c - 8), min(SEQ, 128 * c + 136)
                            o = c2v("pool")[:, (4 * g + c) * 144 + lo - (128 * c - 8):(4 * g + c) * 144 + hi - (128 * c - 8)]
                            last = mm(A[64 * gg:64 * gg + 64, ch, lo:hi], work[:, c * 256 + g * 64:c * 256 + g * 64 + 64], o,
                                      start=(c == 0), stop=(c == 3), skip_group_check=True)
                    last.then_inc(S["p_t"], 1)
                for ch in range(2):
                    pe.wait_ge(S["p_tc"], ch + 1)
                    mm(A[:, 2 + ch, :], poolw[:, ch, :], y2tmp(ch), start=True, stop=True).then_inc(S["p_y"], 1)

            def y2tmp(ch):
                return conv_out[:, ch * 512:ch * 512 + 512]

            def neighbourhood():
                pe.wait_ge(S["b_bm"], 1)
                pe.wait_ge(S["y2l"], 4)
                combos = [(h, j) for h in range(NA_H) for j in range(4)]

                def scores(i):
                    h, j = combos[i]
                    r = 64 * (h % 2)
                    a, b = max(0, j - 1), min(4, j + 2)
                    if i >= 2:
                        pe.wait_ge(S["n_m"], i - 1)
                    mm(A[:, i % 2, 0:(b - a) * P], qp[r:r + 64, h // 2, j * P:j * P + P],
                       kp[r:r + 64, h // 2, a * P:b * P], start=True, stop=True).then_inc(S["n_s"], 1)

                def turn(i):
                    h, j = combos[i]
                    n = min(4, j + 2) - max(0, j - 1)
                    pe.wait_ge(S["n_pn"], i + 1)
                    if i:
                        pe.wait_ge(S["n_tc"], i)
                    for k in range(n):
                        last = nc.tensor.transpose(A[:, 2, k * P:k * P + P],
                                                   work[:, (i % 2) * 384 + k * P:(i % 2) * 384 + k * P + P], I)
                    last.then_inc(S["n_t"], 1)

                def pv(i):
                    h, j = combos[i]
                    r = 64 * (h % 2)
                    a, b = max(0, j - 1), min(4, j + 2)
                    pe.wait_ge(S["n_tc"], i + 1)
                    if i % 8 == 0 and i:
                        pe.wait_ge(S["n_ol"], i // 8)
                    for k in range(a, b):
                        last = mm(A[r:r + 64, 3, j * P:j * P + P], vp[:, k, h * 64:h * 64 + 64],
                                  work[:, 768 + (i % 2) * 384 + (k - a) * P:768 + (i % 2) * 384 + (k - a + 1) * P],
                                  start=(k == a), stop=(k == b - 1), skip_group_check=True)
                    last.then_inc(S["n_o"], 1)

                for i in range(len(combos) + 2):
                    if i < len(combos):
                        scores(i)
                    if 1 <= i <= len(combos):
                        turn(i - 1)
                    if i >= 2:
                        pv(i - 2)

            pe.wait_ge(const2_in, 16)
            with pe.Fori(0, DEPTH) as l:
                Pos.l = l
                Pos.pair, Pos.off = l * (BLOCK2 // 2) + DEPTH * BLOCK1 // 2, 0
                Pos.ubase, Pos.u = l * UNITS2 + DEPTH * UNITS1, 0
                N.tr, N.src, N.ff = 0, 0, 0
                pe.wait_ge(layer_open, l + 1 + DEPTH)
                pe.sem_inc(S["layer_begun"], 1)
                transposes(lambda t: x[:, t, :], 4, 2)
                pe.wait_ge(S["tr_lo"], N.tr)
                ffn()
                bias()
                transposes(lambda t: x[:, t, :], 4, 2)
                pe.wait_ge(S["tr_lo"], N.tr)
                gemm((4, 4), [(b, [tok(b, xT_hi, xT_lo, 2 * b + i, n=256, at=256 * i, own_start=(i == 0)) for i in range(2)])
                              for b in range(2)] +
                     [(2 + i, [feat(2 + i, xT_hi, xT_lo, 256 + i * P)]) for i in range(2)])
                feat4()
                feat4()
                feat4()
                pe.wait_ge(S["perm_hi"], 1)
                pe.wait_ge(S["perm_lo"], 1)
                tok4(hi=y2_hi, lo=y2_lo)
                pool_mixer()
                neighbourhood()
                pe.wait_ge(S["n_ol"], 4)
                for half in range(2):
                    gemm((4, 4), [(o, [tok(o, y2_hi, y2_lo, o)]) for o in range(4)])
                transposes(lambda t: x[:, t, :], 4, 2)
                pe.wait_ge(S["tr_lo"], N.tr)
                ffn()
                assert Pos.off == BLOCK2 and Pos.u == UNITS2, (Pos.off, Pos.u)
                pe.sem_inc(pe_end, 1)

        @block.scalar
        def _(act):
            fn = nc.scalar.activation
            for i in range(4):
                act.sem_inc(g_free[i], 1)
            act.dma_start(ident[:, :], const0).then_inc(const_in, 16)

            class Pos:
                pair, off, end, ubase, u = 0, 0, 0, 0, 0

            class N:
                tr, ch, rs, ff = 0, 0, 0, 0

            def link(ins):
                N.ch += 1
                ins.then_inc(S["act_chain"], 1)
                act.wait_ge(S["act_chain"], N.ch)

            def split(nk=KB):
                s = Pos.off % 2
                act.wait_ge(raw_in[s], (Pos.pair + Pos.off // 2 + 1) * 16)
                act.wait_ge(blk_used, 2 * Pos.pair + Pos.off + 1)
                fn(w_hi[:, s, 0:nk, :], raw[:, s, 0:nk, :], ACT.Copy).then_inc(hi_done, 1)
                Pos.off += 1

            def unit(evac, nxt):
                if nxt:
                    split(nxt[0])
                evac()
                for nk in nxt[1:]:
                    split(nk)
                Pos.u += 1
                Pos.end += len(nxt)

            def done(bank):
                if bank < 3:
                    act.wait_ge(g_done[bank], Pos.ubase + Pos.u + 1)
                else:
                    act.wait_ge(blk_used, 2 * Pos.pair + Pos.end + 2)

            def evac4(dst, func=ACT.Copy, src=None):
                def go():
                    for b in range(4):
                        done(b)
                        fn(dst(b), src(b) if src else G[:, b, :], func).then_inc(g_free[b], 1)
                return go

            def tr_hi(dst, tiles, groups):
                for t in range(tiles):
                    for g in range(groups):
                        act.wait_ge(S["tr_done"], N.tr + 1)
                        fn(dst[:, 4 * g:4 * g + 4, t * P:t * P + P], A[:, N.tr % 4, :].rearrange("p (c t) -> p c t", c=4),
                           ACT.Copy).then_inc(S["tr_hi"], 1)
                        N.tr += 1

            def rsqrt(n):
                N.rs += 1
                act.wait_ge(S["rs_in"], N.rs)
                link(fn(rs_t[:, 0:n], rs_v[:, 0:n], ACT.Ln))
                fn(rs_r[:, 0:n], rs_t[:, 0:n], ACT.Exp, scale=-0.5).then_inc(S["rs_out"], 1)

            def mem_attention():
                for q in range(TILES):
                    act.wait_ge(S["m_nb"], q + 1)
                    act.wait_ge(S["m_log"], q + 1)
                    if q:
                        act.wait_ge(S["m_pt"], q)
                    for h in range(HEADS):
                        fn(sA[:, h * 256:h * 256 + 256], A[:, h // 2, (h % 2) * 256:(h % 2) * 256 + 256], ACT.Exp,
                           bias=small[:, 0, h:h + 1], scale=SCALE, accum_out=small[:, 1, h:h + 1]).then_inc(S["m_p"], 1)

            def stick():
                for h in range(HEADS):
                    act.wait_ge(S["s_ab"], h + 1)
                    link(fn(sB[:, 0:1280], sB[:, 0:1280], ACT.Exp, scale=-1.0))
                    fn(sB[:, 0:1280], sB[:, 0:1280], ACT.Ln, bias=1.0).then_inc(S["s_ln"], 1)
                    act.wait_ge(S["s_d"], h + 1)
                    fn(sA[:, 0:1280], sA[:, 0:1280], ACT.Exp).then_inc(S["s_w"], 1)

            def ssd():
                param(act, Pos.l, "wdt_in")
                fn(wdt_hi[:, :, :], wdt[:, :, :], ACT.Copy).then_inc(S["wdt_h"], 1)
                param(act, Pos.l, "row_in")
                fn(small[:, 11, 0:8], row[:, A_LOG:A_LOG + 8], ACT.Exp).then_inc(S["dt_al"], 1)
                act.wait_ge(S["dt_ab"], 1)
                link(fn(small[:, 1, :], small[:, 1, :], ACT.Exp, scale=-1.0))
                fn(small[:, 1, :], small[:, 1, :], ACT.Ln, bias=1.0).then_inc(S["dt_ln"], 1)
                act.wait_ge(S["dt_sub"], 1)
                fn(small[:, 6, :], small[:, 4, :], ACT.Exp).then_inc(S["dt_ex"], 1)
                fn(small[:, 7, :], small[:, 5, :], ACT.Exp).then_inc(S["dt_ex"], 1)
                fn(small[:, 8, :], small[:, 9, :], ACT.Exp).then_inc(S["dt_ex"], 1)
                for c in range(TILES):
                    act.wait_ge(S["d_t"], c + 1)
                    fn(sB[:, 0:1024], sB[:, 0:1024], ACT.Exp).then_inc(S["d_e"], 1)

            def mixer_out(nxt):
                tr_hi(mixT_hi, TILES, 1)
                unit(lambda: None, (4,))
                unit(lambda: None, nxt)

            act.dma_start(cst[:, :], const1).then_inc(const_in, 16)
            act.wait_ge(const_in, 32)
            act.dma_start(x[:, :, :], x_in.rearrange("a (t p) d -> p (a t) d", p=P)).then_inc(x_loaded, 16)
            act.wait_ge(x_loaded, 16)
            T, K2 = (4, 4), (4, 4)
            with act.Fori(0, DEPTH) as l:
                Pos.l = l
                Pos.pair, Pos.off, Pos.end, Pos.ubase, Pos.u = l * (BLOCK1 // 2), 0, 2, l * UNITS1, 0
                N.tr, N.ch, N.rs = 0, 0, 0
                split()
                split()
                act.wait_ge(layer_open, l + 1)
                act.sem_inc(S["layer_begun"], 1)
                rsqrt(2)
                tr_hi(xT_hi, 2, 2)
                unit(evac4(lambda b: mk[:, b, :], src=lambda b: G[:, b, 0:N_MEM]), K2)
                unit(evac4(lambda b: tA[:, b // 2, (b % 2) * 256:(b % 2) * 256 + 256], src=lambda b: G[:, b, 0:256]), K2)
                rsqrt(4)
                tr_hi(xT_hi, 4, 2)
                unit(evac4(lambda b: fA[:, b, :]), K2)
                unit(evac4(lambda b: tB[:, b, :], ACT.Silu), (4,))
                mem_attention()
                mixer_out(K2)
                unit(evac4(lambda b: fA[:, b, :]), K2)
                unit(evac4(lambda b: fB[:, b, :]), K2)
                unit(evac4(lambda b: tA[:, b, :]), K2)
                unit(evac4(lambda b: tB[:, b, :], ACT.Silu), (4,))
                rsqrt(16)
                mixer_out(K2)
                unit(evac4(lambda b: fA[:, b, :]), K2)
                unit(evac4(lambda b: fB[:, b, :]), K2)
                unit(evac4(lambda b: tA[:, b, :]), K2)
                unit(evac4(lambda b: tB[:, b, :], ACT.Silu), (4,))
                stick()
                mixer_out(K2)

                def silu_conv(buf, base):
                    def go():
                        for b in range(4):
                            act.wait_ge(g_free[b], Pos.ubase + Pos.u + 2)
                            fn(buf[:, b, :], buf[:, b, :], ACT.Silu).then_inc(S["conv_silu"], 1)
                    return go
                unit(silu_conv(fA, 0), K2)
                unit(silu_conv(fB, 4), K2)
                unit(evac4(lambda b: tB[:, b, :], ACT.Silu), (4,))
                ssd()
                rsqrt(8)
                mixer_out(())
                rsqrt(4)
                assert Pos.off == BLOCK1 and Pos.u == UNITS1
                act.sem_inc(act_end, 1)

            def ffn(nxt):
                for n, (units, downs) in enumerate(FF_HALVES):
                    base_pair, base_off, base_u, ub = Pos.pair, Pos.off, Pos.u, Pos.ubase
                    c0 = N.ff
                    with act.Fori(0, units) as u:
                        Pos.pair, Pos.off, Pos.end = base_pair + u, base_off, base_off
                        Pos.ubase, Pos.u = ub + u, base_u
                        split()
                        for i in range(2):
                            done(i)
                            act.wait_ge(g_free[2 + i], ub + u + (base_u + 1))
                            fn(work[:, i * 512:i * 512 + 512], G[:, i, :], ACT.Silu).then_inc(g_free[i], 1)
                        for i in range(2):
                            act.wait_ge(g_free[2 + i], ub + u + (base_u + 2))
                            fn(h_hi[:, bass.ds(2 * u + i, 1), :].rearrange("p o n -> p (o n)"),
                               work[:, 1024 + i * 512:1536 + i * 512], ACT.Copy).then_inc(S["ff_hi"], 1)
                        split()
                    Pos.pair, Pos.off, Pos.end = base_pair, base_off + 2 * units, base_off + 2 * units + 1
                    Pos.ubase, Pos.u = ub, base_u + units
                    N.ff += 2 * units
                    split(downs[2])
                    unit(lambda: None, (4, 4, downs[2]))
                    unit(lambda: None, (4, 4) if n == 0 else nxt)

            act.wait_ge(const2_in, 16)
            with act.Fori(0, DEPTH) as l:
                Pos.l = l
                Pos.pair, Pos.off, Pos.end = l * (BLOCK2 // 2) + DEPTH * BLOCK1 // 2, 0, 2
                Pos.ubase, Pos.u = l * UNITS2 + DEPTH * UNITS1, 0
                N.tr, N.ch, N.rs, N.ff = 0, 0, 0, 0
                split()
                split()
                act.wait_ge(layer_open, l + 1 + DEPTH)
                act.sem_inc(S["layer_begun"], 1)
                tr_hi(xT_hi, 4, 2)
                ffn(K2)
                rsqrt(4)
                for k in range(NA_R):
                    act.wait_ge(S["b_g"], k + 1)
                    fn(raw_rows.rearrange("p (h k e) -> p h k e", h=8, k=8)[:, :, k, :],
                       A[:, k % 4, 0:248].rearrange("p (h e) -> p h e", h=8), ACT.Copy).then_inc(S["b_gc"], 1)
                tr_hi(xT_hi, 4, 2)
                act.wait_ge(S["tr_hi"], N.tr)
                fn(y2_hi[:, :, :].rearrange("p k (c r) -> p k c r", r=NA_R),
                   xT_hi[:, :, :].bitcast(F32).rearrange("p k (r c) -> p k c r", c=GRID_W), ACT.Copy).then_inc(S["perm_hi"], 1)

                def ub():
                    for b in range(2):
                        done(b)
                        act.wait_ge(S["b_bm"], 1)
                        fn(work[:, b * 512:b * 512 + 512], G[:, b, :], ACT.Copy).then_inc(g_free[b], 1)
                    for b in range(2):
                        done(2 + b)
                        fn(work[:, 1024 + b * 512:1536 + b * 512], G[:, 2 + b, :], ACT.Copy).then_inc(g_free[2 + b], 1)
                unit(ub, K2)

                def cz():
                    for b in range(2):
                        done(b)
                        fn(work[:, 2048 + b * 512:2560 + b * 512], G[:, b, :], ACT.Copy).then_inc(g_free[b], 1)
                unit(cz, K2)
                unit(evac4(lambda b: qp[:, b, :].rearrange("p (c r) -> p c r", r=NA_R),
                           src=lambda b: perm_view(G[:, b, :])), K2)
                unit(evac4(lambda b: kp[:, b, :].rearrange("p (c r) -> p c r", r=NA_R),
                           src=lambda b: perm_view(G[:, b, :])), K2)
                unit(evac4(lambda b: vp[:, b, :]), K2)
                for ch in range(2):
                    act.wait_ge(S["p_t"], ch + 1)
                    act.wait_ge(S["z_y"], 2)
                    fn(conv_out[:, ch * 512:ch * 512 + 512], A[:, ch, :], ACT.Copy).then_inc(S["p_tc"], 1)
                param(act, Pos.l, "col2_in")
                for ch in range(2):
                    act.wait_ge(S["p_y"], ch + 1)
                    fn(y2_hi[:, ch, :], A[:, 2 + ch, :], ACT.Copy, scale=col2[:, ch, 3:4]).then_inc(S["y2h"], 1)
                for ch in range(2):
                    fn(y2_hi[:, 2 + ch, :], work[:, 1024 + ch * 512:1536 + ch * 512], ACT.Copy).then_inc(S["y2h"], 1)
                combos = [(h, j) for h in range(NA_H) for j in range(4)]

                def exps(i):
                    h, j = combos[i]
                    n = (min(4, j + 2) - max(0, j - 1)) * P
                    act.wait_ge(S["n_m"], i + 1)
                    if i >= 2:
                        act.wait_ge(S["n_t"], i - 1)
                    w = work[:, (i % 2) * 384:(i % 2) * 384 + n]
                    fn(w, w, ACT.Exp, bias=nmx[:, 0, i:i + 1], accum_out=nmx[:, 1, i:i + 1]).then_inc(S["n_p"], 1)

                def turned(i):
                    h, j = combos[i]
                    n = (min(4, j + 2) - max(0, j - 1)) * P
                    act.wait_ge(S["n_t"], i + 1)
                    if i >= 2:
                        act.wait_ge(S["n_o"], i - 1)
                    fn(work[:, 768 + (i % 2) * 384:768 + (i % 2) * 384 + n], A[:, 2, 0:n], ACT.Copy).then_inc(S["n_tc"], 1)

                def pair_out(i):
                    act.wait_ge(S["n_o"], 8 * i + 8)
                    fn(y2_hi[:, 4 + i, :].rearrange("p (r c) -> p c r", c=GRID_W),
                       A[:, 3, :].rearrange("p (c r) -> p c r", r=NA_R), ACT.Copy).then_inc(S["n_oh"], 1)

                for i in range(len(combos) + 2):
                    if i < len(combos):
                        exps(i)
                    if 1 <= i <= len(combos):
                        turned(i - 1)
                    if i >= 2 and (i - 2) % 8 == 7:
                        pair_out((i - 2) // 8)
                unit(lambda: None, K2)
                unit(lambda: None, K2)
                rsqrt(4)
                tr_hi(xT_hi, 4, 2)
                ffn(())
                rsqrt(4)
                assert Pos.off == BLOCK2 and Pos.u == UNITS2
                act.sem_inc(act_end, 1)

        @block.vector
        def _(dve):
            tt, ts, stt = nc.vector.tensor_tensor, nc.vector.tensor_scalar, nc.vector.scalar_tensor_tensor
            dve.sem_inc(lo_done, 2)

            class Pos:
                pair, off, end, ubase, u = 0, 0, 0, 0, 0

            class N:
                tr, ch, rs, ff, half = 0, 0, 0, 0, 0

            def link(ins):
                N.ch += 1
                ins.then_inc(S["dve_chain"], 1)
                dve.wait_ge(S["dve_chain"], N.ch)

            def split(nk=KB):
                s = Pos.off % 2
                dve.wait_ge(hi_done, 2 * Pos.pair + Pos.off + 1)
                tt(w_lo[:, s, 0:nk, :], raw[:, s, 0:nk, :], w_hi[:, s, 0:nk, :].bitcast(F32),
                   ALU.subtract).then_inc(lo_done, 1)
                Pos.off += 1

            def unit(evac, nxt):
                if nxt:
                    split(nxt[0])
                evac()
                for nk in nxt[1:]:
                    split(nk)
                Pos.u += 1
                Pos.end += len(nxt)

            def done(bank):
                if bank < 3:
                    dve.wait_ge(g_done[bank], Pos.ubase + Pos.u + 1)
                else:
                    dve.wait_ge(blk_used, 2 * Pos.pair + Pos.end + 2)

            def none():
                pass

            def results_read():
                for bank in range(4):
                    dve.wait_ge(g_free[bank], Pos.ubase + Pos.u + 1)

            def tr_lo(dst_hi, dst_lo, tiles, groups, src=None):
                for t in range(tiles):
                    if src:
                        src(t)
                    for g in range(groups):
                        dve.wait_ge(S["tr_hi"], N.tr + 1)
                        tt(dst_lo[:, 4 * g:4 * g + 4, t * P:t * P + P], A[:, N.tr % 4, :].rearrange("p (c t) -> p c t", c=4),
                           dst_hi[:, 4 * g:4 * g + 4, t * P:t * P + P].bitcast(F32), ALU.subtract).then_inc(S["tr_lo"], 1)
                        N.tr += 1

            def rsqrt(n, scale, eps):
                v, r, t = rs_v[:, 0:n], rs_r[:, 0:n], rs_t[:, 0:n]
                N.rs += 1
                ts(v, v, scale, eps, ALU.mult, ALU.add).then_inc(S["rs_in"], 1)
                dve.wait_ge(S["rs_out"], N.rs)
                link(tt(t, r, r, ALU.mult))
                link(tt(t, t, v, ALU.mult))
                link(ts(t, t, -0.5, 1.5, ALU.mult, ALU.add))
                link(tt(r, r, t, ALU.mult))

            def rms_operand(src, tiles, g):
                for t in range(tiles):
                    ins = nc.vector.tensor_tensor_reduce(out=xn[:, 0, :], in0=src(t), in1=src(t), scale=1.0, scalar=0.0,
                                                         op0=ALU.mult, op1=ALU.add, accum_out=rs_v[:, t:t + 1])
                    link(ins)
                rsqrt(tiles, 1.0 / D, EPS)
                base = N.tr

                def normed(t):
                    if t >= 2:
                        dve.wait_ge(S["tr_done"], base + 2 * (t - 1))
                    stt(out=xn[:, t % 2, :], in0=src(t), scalar=rs_r[:, t:t + 1], in1=row[:, g:g + D],
                        op0=ALU.mult, op1=ALU.mult).then_inc(S["tr_src"], 1)
                normed(0)
                tr_lo(xT_hi, xT_lo, tiles, 2, lambda t: normed(t + 1) if t + 1 < tiles else None)

            def heads(ap, n=4):
                return ap.unsqueeze(2).to_broadcast([P, n, P])

            def mem_attention():
                for q in range(TILES):
                    dve.wait_ge(S["m_log"], q + 1)
                    link(nc.vector.tensor_reduce(small[:, 2, 0:4],
                                                 A[:, 0:2, :].rearrange("p b (h n) -> p (b h) n", h=2), AX.X, ALU.max))
                    ts(small[:, 0, 0:4], small[:, 2, 0:4], -SCALE, None, ALU.mult).then_inc(S["m_nb"], 1)
                    dve.wait_ge(S["m_pt"], q + 1)
                    nc.vector.tensor_copy(sB[:, 0:1024], A[:, 2:4, :].rearrange("p b n -> p (b n)")).then_inc(S["m_ptc"], 1)
                    dve.wait_ge(S["m_p"], 4 * (q + 1))
                    link(nc.vector.reciprocal(small[:, 3, 0:4], small[:, 1, 0:4]))
                    dve.wait_ge(S["m_o"], q + 1)
                    m = mix[:, q, :].rearrange("p (h n) -> p h n", h=4)
                    ins = tt(m, A[:, 0, :].rearrange("p (h n) -> p h n", h=4), heads(small[:, 3, 0:4]), ALU.mult)
                    link(ins)
                    if q == 0:
                        results_read()
                    tt(mix[:, q, :], mix[:, q, :], tB[:, q, :], ALU.mult).then_inc(S["tr_src"], 1)

            def mixer_out(first, nxt):
                tr_lo(mixT_hi, mixT_lo, TILES, 1)
                for half in range(2):
                    def add():
                        for b in range(4):
                            done(b)
                            o = y_acc[:, b, half * 512:half * 512 + 512]
                            if first:
                                ins = nc.vector.tensor_copy(o, G[:, b, :])
                            else:
                                ins = tt(o, o, G[:, b, :], ALU.add)
                            ins.then_inc(g_free[b], 1)
                    unit(add, (4,) if half == 0 else nxt)

            def retention():
                for i in range(8):
                    f = (fA if i < 4 else fB)[:, i % 4, :]
                    dve.wait_ge(S["rot_done"], i + 1)
                    tt(xn[:, 1, 0:512], A[:, i % 4, :], c1v("sin"), ALU.mult).then_inc(S["rot_used"], 1)
                    dve.wait_ge(S["rot_used"], i + 1)
                    link(tt(f, f, c1v("cos"), ALU.mult))
                    link(tt(f, f, xn[:, 1, 0:512], ALU.add))
                nc.vector.sem_inc(S["ret_ready"], 1)
                xi = c1v("xi").rearrange("p (h n) -> p h n", h=4)
                for h in range(HEADS):
                    link(tt(sA[:, h * 512:h * 512 + 512].rearrange("p (c n) -> p c n", c=4),
                            fA[:, h, :].rearrange("p (c n) -> p c n", c=4),
                            xi[:, h:h + 1, :].to_broadcast([P, 4, P]), ALU.mult))
                for c in range(3):
                    dve.wait_ge(S["rz_t"], c + 1)
                    ins = tt(sB[:, c * 512:c * 512 + 512].rearrange("p (h n) -> p h n", h=4),
                             A[:, c, :].rearrange("p (h n) -> p h n", h=4), heads(c1v("zeta")), ALU.mult)
                    ins.then_inc(S["rz_used"], 1)
                for c in range(TILES):
                    dve.wait_ge(S["r_s"], c + 1)
                    if c:
                        dve.wait_ge(S["r_y"], c)
                    tt(xn[:, 0, 0:512], A[:, 0, :], c1v("intra"), ALU.mult).then_inc(S["r_sm"], 1)
                    dve.wait_ge(S["r_y"], c + 1)
                    nc.vector.tensor_copy(mix[:, c, :], A[:, 1, :]).then_inc(S["r_yu"], 1)
                    if c < 3:
                        dve.wait_ge(S["r_kv"], c + 1)
                        for h in range(HEADS):
                            o, k = state[:, h * P:h * P + P], A[:, 2, h * P:h * P + P]
                            if c == 0:
                                nc.vector.tensor_copy(o, k).then_inc(S["r_st"], 1)
                            else:
                                stt(out=o, in0=o, scalar=RET_DECAY[h], in1=k, op0=ALU.mult,
                                    op1=ALU.add).then_inc(S["r_st"], 1)
                dve.wait_ge(S["r_yu"], 4)
                m3 = mix[:, :, :].rearrange("p c (h n) -> p (c h) n", h=4)
                for i in range(16):
                    ins = nc.vector.bn_stats(stats[:, i, :], m3[:, i, :])
                link(ins)
                for i in range(16):
                    ins = nc.vector.bn_aggr(mean_var[:, i, :], stats[:, i, :])
                link(ins)
                link(nc.vector.tensor_copy(rs_v[:, 0:16], mean_var[:, :, 1]))
                rsqrt(16, 1.0, EPS)
                link(tt(m3, m3, heads(mean_var[:, :, 0], 16), ALU.subtract))
                link(tt(m3, m3, heads(rs_r[:, 0:16], 16), ALU.mult))
                results_read()
                for t in range(TILES):
                    tt(mix[:, t, :], mix[:, t, :], tB[:, t, :], ALU.mult).then_inc(S["tr_src"], 1)

            SB_AT = (0, 512, 1024, 896)

            def stick():
                flat = A[:, :, :].rearrange("p b n -> p (b n)")[:, 0:1280]
                L, E = sA[:, 0:1280], sB[:, 0:1280]
                for h in range(HEADS):
                    dve.wait_ge(S["s_log"], h + 1)
                    if h:
                        dve.wait_ge(S["s_pv"], h)
                    link(ts(L, flat, SCALE, None, ALU.mult))
                    stt(out=E, in0=L, scalar=-1.0, in1=L, op0=ALU.mult, op1=ALU.max).then_inc(S["s_ab"], 1)
                    dve.wait_ge(S["s_ln"], h + 1)
                    link(stt(out=E, in0=L, scalar=0.0, in1=E, op0=ALU.max, op1=ALU.add))
                    for i in range(4):
                        e = sB[:, SB_AT[i]:SB_AT[i] + P]
                        ins = tt(e, e, c1v("before"), ALU.mult)
                    ins.then_inc(S["s_sp"], 1)
                    dve.wait_ge(S["s_cum"], h + 1)
                    link(tt(L, L, flat, ALU.subtract))
                    for i in range(4):
                        e = sA[:, SB_AT[i]:SB_AT[i] + P]
                        ins = tt(e, e, c1v("before_neg"), ALU.min)
                    ins.then_inc(S["s_d"], 1)
                    dve.wait_ge(S["s_pv"], h + 1)
                    if h == 0:
                        results_read()
                    ins = tt(mix[:, :, h * P:h * P + P], A[:, 3, :].rearrange("p (j n) -> p j n", j=4),
                             tB[:, :, h * P:h * P + P], ALU.mult)
                    ins.then_inc(S["s_pvu"], 1)
                dve.wait_ge(S["s_pvu"], 4)
                nc.vector.sem_inc(S["tr_src"], 4)

            def conv_in(buf, base):
                def go():
                    param(dve, Pos.l, "conv_in")
                    for b in range(4):
                        done(b)
                        f, w = buf[:, b, :], conv[:, base + b, :]
                        link(ts(f, G[:, b, :], w[:, 3:4], w[:, 4:5], ALU.mult, ALU.add))
                        for s in (1, 2, 3):
                            ins = stt(out=f[:, s:], in0=G[:, b, 0:512 - s], scalar=w[:, 3 - s:4 - s], in1=f[:, s:],
                                      op0=ALU.mult, op1=ALU.add)
                            if s < 3:
                                link(ins)
                        ins.then_inc(g_free[b], 1)
                return go

            def per_head(ap, c=None):
                return ap.unsqueeze(2).to_broadcast([P, ap.shape[1], 64])

            def ssd():
                dve.wait_ge(S["wdt_h"], 1)
                tt(wdt_lo[:, :, :], wdt[:, :, :], wdt_hi[:, :, :].bitcast(F32), ALU.subtract).then_inc(S["wdt_l"], 1)
                dve.wait_ge(S["dt_p"], 1)
                u, ab = small[:, 0, :], small[:, 1, :]
                link(tt(u.rearrange("p (t h) -> p t h", h=8), A[:, 3, 0:32].rearrange("p (t h) -> p t h", h=8),
                        row[:, DT_B:DT_B + 8].unsqueeze(1).to_broadcast([P, 4, 8]), ALU.add))
                stt(out=ab, in0=u, scalar=-1.0, in1=u, op0=ALU.mult, op1=ALU.max).then_inc(S["dt_ab"], 1)
                dve.wait_ge(S["dt_ln"], 1)
                dl = small[:, 2, :]
                link(stt(out=dl, in0=u, scalar=0.0, in1=ab, op0=ALU.max, op1=ALU.add))
                dve.wait_ge(S["dt_al"], 1)
                stt(out=small[:, 3, :].rearrange("p (t h) -> p t h", h=8), in0=dl.rearrange("p (t h) -> p t h", h=8),
                    scalar=-1.0, in1=small[:, 11, 0:8].unsqueeze(1).to_broadcast([P, 4, 8]),
                    op0=ALU.mult, op1=ALU.mult).then_inc(S["dt_da"], 1)
                for c in range(TILES):
                    dve.wait_ge(S["x_t"], c + 1)
                    nc.vector.tensor_copy(tA[:, c, :], A[:, c % 2, :]).then_inc(S["x_tc"], 1)
                    nc.vector.tensor_copy(xn[:, c // 2, (c % 2) * 256:(c % 2) * 256 + 256],
                                          A[:, 2, 0:256]).then_inc(S["x_tc"], 1)
                dve.wait_ge(S["x_tc"], 8)
                dve.wait_ge(S["dt_cs"], 1)
                nc.vector.tensor_copy(small[:, 4, :], A[:, 2, 0:32])
                link(nc.vector.tensor_copy(small[:, 5, :], A[:, 2, 32:64]))
                tt(small[:, 9, :], small[:, 5, :], small[:, 4, :], ALU.subtract).then_inc(S["dt_sub"], 1)
                f2 = fA[:, :, :].rearrange("p c (h n) -> p (c h) n", n=64)
                link(tt(f2, tA[:, :, :].rearrange("p c (h n) -> p (c h) n", n=64), per_head(dl), ALU.mult))
                dve.wait_ge(S["dt_ex"], 3)
                link(tt(sA[:, :].rearrange("p (h n) -> p h n", n=64), f2, per_head(small[:, 8, :]), ALU.mult))
                for c in range(TILES):
                    t = sB[:, 0:1024].rearrange("p (h n) -> p h n", n=P)
                    dve.wait_ge(S["d_bc"], c + 1)
                    link(tt(t, A[:, 0:2, :].rearrange("p b (h n) -> p (b h) n", n=P),
                            heads(small[:, 4, 8 * c:8 * c + 8], 8), ALU.subtract))
                    tt(t, t, c1v("upto_neg").unsqueeze(1).to_broadcast([P, 8, P]), ALU.min).then_inc(S["d_t"], 1)
                    dve.wait_ge(S["d_e"], c + 1)
                    for g in range(2):
                        ins = tt(sB[:, 1024 + g * 512:1536 + g * 512].rearrange("p (h n) -> p h n", n=P),
                                 sB[:, g * 512:g * 512 + 512].rearrange("p (h n) -> p h n", n=P),
                                 A[:, 2, g * P:g * P + P].unsqueeze(1).to_broadcast([P, 4, P]), ALU.mult)
                    ins.then_inc(S["d_sc"], 1)
                    dve.wait_ge(S["d_y"], c + 1)
                    m = mix[:, c, :]
                    if c:
                        link(tt(m.rearrange("p (h n) -> p h n", n=64), A[:, 0, :].rearrange("p (h n) -> p h n", n=64),
                                per_head(small[:, 6, 8 * c:8 * c + 8]), ALU.mult))
                        tt(m, m, A[:, 3, :], ALU.add).then_inc(S["d_yu"], 1)
                    else:
                        nc.vector.tensor_copy(m, A[:, 3, :]).then_inc(S["d_yu"], 1)
                    if c == 0:
                        nc.vector.tensor_copy(state[:, :], A[:, 1, :]).then_inc(S["d_st"], 1)
                    elif c < 3:
                        s3 = state[:, :].rearrange("p (h n) -> p h n", n=64)
                        link(tt(s3, s3, per_head(small[:, 7, 8 * c:8 * c + 8]), ALU.mult))
                        tt(state[:, :], state[:, :], A[:, 1, :], ALU.add).then_inc(S["d_st"], 1)
                dve.wait_ge(S["d_yu"], 4)
                results_read()
                for c in range(TILES):
                    xs = tA[:, c, :].rearrange("p (h n) -> p h n", n=64)
                    link(tt(xs, xs, per_head(row[:, D_SKIP:D_SKIP + 8]), ALU.mult))
                m2 = mix[:, :, :].rearrange("p c n -> p (c n)")
                link(tt(m2, m2, tA[:, :, :].rearrange("p c n -> p (c n)"), ALU.add))
                link(tt(m2, m2, tB[:, :, :].rearrange("p c n -> p (c n)"), ALU.mult))
                for i in range(8):
                    g = m2[:, i * 256:i * 256 + 256]
                    link(nc.vector.tensor_tensor_reduce(out=sB[:, 0:256], in0=g, in1=g, scale=1.0, scalar=0.0,
                                                        op0=ALU.mult, op1=ALU.add, accum_out=rs_v[:, i:i + 1]))
                rsqrt(8, 1.0 / 256, EPS)
                for c in range(TILES):
                    for g in range(2):
                        o = mix[:, c, g * 256:g * 256 + 256]
                        ins = stt(out=o, in0=o, scalar=rs_r[:, 2 * c + g:2 * c + g + 1],
                                  in1=row[:, SSD_G + g * 256:SSD_G + g * 256 + 256], op0=ALU.mult, op1=ALU.mult)
                    ins.then_inc(S["tr_src"], 1)

            def end_layer(n):
                dve.wait_ge(pe_end, n)
                dve.wait_ge(act_end, n)
                dve.wait_ge(pool_end, n)
                nc.vector.sem_inc(S["layer_left"], 1)
                nc.vector.sem_clear(STAGES)
                nc.vector.memset(rs_t[:, 0:2], 0.0).then_inc(layer_open, 1)

            nc.vector.sem_inc(layer_open, 1)
            dve.wait_ge(const_in, 32)
            dve.wait_ge(x_loaded, 16)
            K2 = (4, 4)
            with dve.Fori(0, DEPTH) as l:
                Pos.l = l
                Pos.pair, Pos.off, Pos.end, Pos.ubase, Pos.u = l * (BLOCK1 // 2), 0, 2, l * UNITS1, 0
                N.tr, N.ch, N.rs = 0, 0, 0
                split()
                split()
                param(dve, Pos.l, "mem_in")
                param(dve, Pos.l, "row_in")
                mem_t = sA[:, :].rearrange("p (t d) -> p t d", t=2)
                rms_operand(lambda t: mem_t[:, t, :], 2, MEM_G)
                unit(none, K2)
                unit(none, K2)
                dve.wait_ge(blk_used, 2 * Pos.pair + 4 + 2)
                rms_operand(lambda t: x[:, t, :], 4, PRE_G)
                unit(none, K2)
                split(4)
                Pos.u, Pos.end = Pos.u + 1, Pos.end + 1
                mem_attention()
                mixer_out(True, K2)
                for _ in range(3):
                    unit(none, K2)
                split(4)
                Pos.u, Pos.end = Pos.u + 1, Pos.end + 1
                retention()
                mixer_out(False, K2)
                for _ in range(3):
                    unit(none, K2)
                split(4)
                Pos.u, Pos.end = Pos.u + 1, Pos.end + 1
                stick()
                mixer_out(False, K2)
                unit(conv_in(fA, 0), K2)
                unit(conv_in(fB, 4), K2)
                unit(none, (4,))
                ssd()
                mixer_out(False, ())
                for b in range(4):
                    dve.wait_ge(g_free[b], Pos.ubase + Pos.u + 1)
                for t in range(4):
                    link(nc.vector.tensor_tensor_reduce(out=xn[:, 0, :], in0=y_acc[:, t, :], in1=y_acc[:, t, :],
                                                        scale=1.0, scalar=0.0, op0=ALU.mult, op1=ALU.add,
                                                        accum_out=rs_v[:, t:t + 1]))
                rsqrt(4, 1.0 / D, EPS)
                for t in range(4):
                    ins = stt(out=y_acc[:, t, :], in0=y_acc[:, t, :], scalar=rs_r[:, t:t + 1], in1=row[:, POST_G:POST_G + D],
                              op0=ALU.mult, op1=ALU.mult)
                link(ins)
                x2, y2 = x[:, :, :].rearrange("p t d -> p (t d)"), y_acc[:, :, :].rearrange("p t d -> p (t d)")
                link(tt(x2, x2, y2, ALU.add))
                nc.vector.sem_inc(S["row_used"], 1)
                assert Pos.off == BLOCK1 and Pos.u == UNITS1
                end_layer(l + 1)

            def x_operand():
                nc.vector.sem_inc(S["tr_src"], 4)
                tr_lo(xT_hi, xT_lo, 4, 2)
                for t in range(4):
                    ins = ts(x[:, t, :], x[:, t, :], ALPHA, None, ALU.mult)
                link(ins)

            def add_half(scale, half):
                def go():
                    for b in range(4):
                        done(b)
                        o = x[:, b, half * 512:half * 512 + 512]
                        ins = stt(out=o, in0=G[:, b, :], scalar=scale, in1=o, op0=ALU.mult, op1=ALU.add)
                        ins.then_inc(g_free[b], 1)
                return go

            def ffn(nxt):
                for n, (units, downs) in enumerate(FF_HALVES):
                    base_pair, base_off, base_u, ub = Pos.pair, Pos.off, Pos.u, Pos.ubase
                    c0 = N.ff
                    with dve.Fori(0, units) as u:
                        Pos.pair, Pos.off, Pos.end = base_pair + u, base_off, base_off
                        Pos.ubase, Pos.u = ub + u, base_u
                        split()
                        for i in range(2):
                            done(2 + i)
                            dve.wait_ge(g_free[i], ub + u + base_u + 2)
                            ins = tt(work[:, 1024 + i * 512:1536 + i * 512], work[:, i * 512:i * 512 + 512],
                                     G[:, 2 + i, :], ALU.mult)
                            ins.then_inc(g_free[2 + i], 1)
                        for i in range(2):
                            dve.wait_ge(S["ff_hi"], 2 * u + (c0 + i + 1))
                            a = bass.ds(2 * u + i, 1)
                            tt(h_lo[:, a, :].rearrange("p o n -> p (o n)"), work[:, 1024 + i * 512:1536 + i * 512],
                               h_hi[:, a, :].rearrange("p o n -> p (o n)").bitcast(F32), ALU.subtract).then_inc(S["ff_lo"], 1)
                        split()
                    Pos.pair, Pos.off, Pos.end = base_pair, base_off + 2 * units, base_off + 2 * units + 1
                    Pos.ubase, Pos.u = ub, base_u + units
                    N.ff += 2 * units
                    split(downs[2])
                    unit(add_half(0.5, 0), (4, 4, downs[2]))
                    unit(add_half(0.5, 1), (4, 4) if n == 0 else nxt)

            def layer_norm(i):
                results_read()
                if i == 0:
                    nc.vector.sem_inc(S["half_done"], 1)
                for t in range(4):
                    for s in range(2):
                        ins = nc.vector.bn_stats(stats[:, 2 * t + s, :], x[:, t, s * 512:s * 512 + 512])
                link(ins)
                for t in range(4):
                    ins = nc.vector.bn_aggr(mean_var[:, t, :], stats[:, 2 * t:2 * t + 2, :].rearrange("p a b -> p (a b)"))
                link(ins)
                link(nc.vector.tensor_copy(rs_v[:, 0:4], mean_var[:, 0:4, 1]))
                rsqrt(4, 1.0, LN_EPS)
                param(dve, Pos.l, "ln_in", i + 1, 3)
                for t in range(4):
                    link(ts(x[:, t, :], x[:, t, :], mean_var[:, t, 0:1], rs_r[:, t:t + 1], ALU.subtract, ALU.mult))
                for t in range(4):
                    link(tt(x[:, t, :], x[:, t, :], lnr[:, 0, :], ALU.mult))
                for t in range(4):
                    link(tt(x[:, t, :], x[:, t, :], lnr[:, 1, :], ALU.add))
                nc.vector.sem_inc(S["ln_used"], 1)

            dve.wait_ge(const2_in, 16)
            with dve.Fori(0, DEPTH) as l:
                Pos.l = l
                Pos.pair, Pos.off, Pos.end = l * (BLOCK2 // 2) + DEPTH * BLOCK1 // 2, 0, 2
                Pos.ubase, Pos.u = l * UNITS2 + DEPTH * UNITS1, 0
                N.tr, N.ch, N.rs, N.ff, N.half = 0, 0, 0, 0, 0
                split()
                split()
                x_operand()
                ffn(K2)
                layer_norm(0)
                x_operand()
                dve.wait_ge(S["tr_lo"], N.tr)
                nc.vector.tensor_copy(y2_lo[:, :, :].rearrange("p k (c r) -> p k c r", r=NA_R),
                                      xT_lo[:, :, :].bitcast(F32).rearrange("p k (r c) -> p k c r", c=GRID_W)
                                      ).then_inc(S["perm_lo"], 1)
                param(dve, Pos.l, "shift_in", 16, 16)
                masks = c2v("masks").rearrange("p (m c r) -> p m c r", m=5, c=16)
                for h in range(NA_H):
                    for m, off in enumerate((16, 0, 16, 32, 16)):
                        ins = tt(bm[:, h, m, :].rearrange("p (c r) -> p c r", c=16),
                                 shifted[:, h, :, off:off + 16].rearrange("p k e -> p e k"), masks[:, m], ALU.add)
                ins.then_inc(S["b_bm"], 1)
                unit(none, K2)

                def conv_z():
                    for b in range(2):
                        done(2 + b)
                        dve.wait_ge(g_free[b], Pos.ubase + Pos.u + 2)
                        z = work[:, 2048 + b * 512:2560 + b * 512]
                        tt(z, z, G[:, 2 + b, :], ALU.mult).then_inc(g_free[2 + b], 1)
                unit(conv_z, K2)
                param(dve, Pos.l, "col2_in")
                results_read()
                for b in range(2):
                    z = work[:, 2048 + b * 512:2560 + b * 512]
                    o = conv_out[:, b * 512:b * 512 + 512]
                    gb = work[:, 1024 + b * 512:1536 + b * 512]
                    link(ts(o, z, col2[:, b, 1:2], None, ALU.mult))
                    link(stt(out=o[:, 1:], in0=z[:, 0:511], scalar=col2[:, b, 0:1], in1=o[:, 1:], op0=ALU.mult, op1=ALU.add))
                    link(stt(out=o[:, 0:511], in0=z[:, 1:], scalar=col2[:, b, 2:3], in1=o[:, 0:511], op0=ALU.mult, op1=ALU.add))
                    tt(gb, gb, o, ALU.mult).then_inc(S["z_y"], 1)
                for _ in range(3):
                    unit(none, K2)
                for ch in range(2):
                    dve.wait_ge(S["y2h"], ch + 1)
                    stt(out=y2_lo[:, ch, :], in0=A[:, 2 + ch, :], scalar=col2[:, ch, 3:4], in1=y2_hi[:, ch, :].bitcast(F32),
                        op0=ALU.mult, op1=ALU.subtract).then_inc(S["y2l"], 1)
                for ch in range(2):
                    dve.wait_ge(S["y2h"], ch + 3)
                    tt(y2_lo[:, 2 + ch, :], work[:, 1024 + ch * 512:1536 + ch * 512], y2_hi[:, 2 + ch, :].bitcast(F32),
                       ALU.subtract).then_inc(S["y2l"], 1)
                combos = [(h, j) for h in range(NA_H) for j in range(4)]

                def biased(i):
                    h, j = combos[i]
                    nb = min(4, j + 2) - max(0, j - 1)
                    n = nb * P
                    dve.wait_ge(S["n_s"], i + 1)
                    if i == 0:
                        dve.wait_ge(S["y2l"], 4)
                        dve.wait_ge(S["y2h"], 4)
                    if i >= 2:
                        dve.wait_ge(S["n_t"], i - 1)
                    w = work[:, (i % 2) * 384:(i % 2) * 384 + n]
                    b = {0: bm[:, h, 0:4:3, :], 1: bm[:, h, 1:4, :], 2: bm[:, h, 1:4, :], 3: bm[:, h, 1:5:3, :]}[j]
                    link(stt(out=w.rearrange("p (b n) -> p b n", n=P),
                             in0=A[:, i % 2, 0:n].rearrange("p (b n) -> p b n", n=P), scalar=NA_D ** -0.5, in1=b,
                             op0=ALU.mult, op1=ALU.add))
                    link(nc.vector.tensor_reduce(nmx[:, 2, i:i + 1], w, AX.X, ALU.max))
                    ts(nmx[:, 0, i:i + 1], nmx[:, 2, i:i + 1], -1.0, None, ALU.mult).then_inc(S["n_m"], 1)

                def normed(i):
                    h, j = combos[i]
                    n = (min(4, j + 2) - max(0, j - 1)) * P
                    dve.wait_ge(S["n_p"], i + 1)
                    link(nc.vector.reciprocal(nmx[:, 3, i:i + 1], nmx[:, 1, i:i + 1]))
                    w = work[:, (i % 2) * 384:(i % 2) * 384 + n]
                    ts(w, w, nmx[:, 3, i:i + 1], None, ALU.mult).then_inc(S["n_pn"], 1)

                def pair_out(i):
                    dve.wait_ge(S["n_oh"], i + 1)
                    tt(y2_lo[:, 4 + i, :].rearrange("p (r c) -> p c r", c=GRID_W), A[:, 3, :].rearrange("p (c r) -> p c r", r=NA_R),
                       y2_hi[:, 4 + i, :].bitcast(F32).rearrange("p (r c) -> p c r", c=GRID_W),
                       ALU.subtract).then_inc(S["n_ol"], 1)

                for i in range(len(combos) + 2):
                    if i < len(combos):
                        biased(i)
                    if 1 <= i <= len(combos):
                        normed(i - 1)
                    if i >= 2 and (i - 2) % 8 == 7:
                        pair_out((i - 2) // 8)
                unit(add_half(1.0, 0), K2)
                unit(add_half(1.0, 1), K2)
                layer_norm(1)
                x_operand()
                ffn(())
                layer_norm(2)
                assert Pos.off == BLOCK2 and Pos.u == UNITS2
                end_layer(l + 1 + DEPTH)

        @block.gpsimd
        def _(pool):
            with pool.Fori(0, DEPTH) as l:
                pool.wait_ge(layer_open, l + 1)
                pool.sem_inc(S["layer_begun"], 1)
                pool.dma_start(sA[:, :].rearrange("p (t d) -> p t d", t=2),
                               mem_in.rearrange("a (t p) d -> p (a t) d", p=P)).then_inc(landed["mem_in"], 16)
                pool.dma_start(row[:, :], rows1[bass.ds(l, 1)].to_broadcast([P, ROW1])).then_inc(landed["row_in"], 16)
                pool.dma_start(conv[:, :, :].rearrange("p a b -> p (a b)"),
                               conv1[bass.ds(l, 1)].rearrange("o p n -> (o p) n")).then_inc(landed["conv_in"], 16)
                pool.dma_start(wdt[:, :, :].rearrange("p a b -> p (a b)"),
                               w_dt[bass.ds(l, 1)].rearrange("o p n -> (o p) n")).then_inc(landed["wdt_in"], 16)
                param(pool, l, "conv_in")
                param(pool, l, "wdt_in")
                pool.wait_ge(S["row_used"], 1)
                pool.sem_inc(pool_end, 1)
            pool.wait_ge(layer_open, DEPTH + 1)
            pool.dma_start(cst2[:, :], const2).then_inc(const2_in, 16)
            pool.wait_ge(const2_in, 16)
            with pool.Fori(0, DEPTH) as l:
                pool.wait_ge(layer_open, l + 1 + DEPTH)
                pool.sem_inc(S["layer_begun"], 1)
                def load_ln(i):
                    pool.dma_start(lnr[:, :, :].rearrange("p a b -> p (a b)"),
                                   ln_rows[bass.ds(l, 1), i, :].to_broadcast([P, 2 * D])).then_inc(landed["ln_in"], 16)
                load_ln(0)
                pool.dma_start(poolw[:, :, :].rearrange("p a b -> p (a b)"),
                               pool_w[bass.ds(l, 1)].rearrange("o p n -> (o p) n")).then_inc(landed["poolw_in"], 16)
                pool.dma_start(col2[:, :, :].rearrange("p a b -> p (a b)"),
                               cols2[bass.ds(l, 1)].rearrange("o p n -> (o p) n")).then_inc(landed["col2_in"], 16)
                pool.wait_ge(S["half_done"], 1)
                pool.dma_start(work[0:15, 0:248], rpb[bass.ds(l, 1)].rearrange("o p n -> (o p) n")).then_inc(landed["rpb_in"], 16)
                pool.dma_start(sel[0:15, :], sel_in).then_inc(landed["sel_in"], 16)
                pool.memset(qkv[:, 0:3072], 0.0).then_inc(S["b_raw"], 1)
                pool.wait_ge(S["b_raw"], 1)
                pool.wait_ge(S["b_gc"], NA_R)
                for c in range(16):
                    pool.dma_start(shifted[8 * c:8 * c + 8, :, :, c + 1:c + 32],
                                   raw_rows[8 * c:8 * c + 8, :].rearrange("p (h k e) -> p h k e", h=8, k=8)
                                   ).then_inc(landed["shift_in"], 16)
                param(pool, l, "shift_in", 16, 16)
                pool.sem_inc(S["layer_begun"], 1)
                pool.wait_ge(S["y2l"], 4)
                load_ln(1)
                pool.wait_ge(S["ln_used"], 2)
                load_ln(2)
                pool.wait_ge(S["ln_used"], 3)
                pool.sem_inc(pool_end, 1)
            pool.wait_ge(layer_open, 2 * DEPTH + 1)
            pool.dma_start(out.rearrange("a (t p) d -> p (a t) d", p=P), x[:, :, :]).then_inc(out_done, 16)
            pool.wait_ge(out_done, 16)


def weight_stream(v):
    out = []

    def add(w, col, rows=None):
        r0, r1 = rows or (0, w.shape[0])
        for r in range(r0, r1, KB * P):
            b = w[r:min(r + KB * P, r1), col:col + BC]
            b = b.reshape(-1, P, BC).transpose(1, 0, 2)
            if b.shape[1] < KB:
                b = np.concatenate([b, np.zeros((P, KB - b.shape[1], BC), b.dtype)], axis=1)
            out.append(b.reshape(P, KB * BC))

    for l in range(DEPTH):
        w, wo, kv = v["w_in"][l], v["w_out"][l], v["w_mem_kv"][l]

        def mixer(cols, first_row):
            for c in cols:
                add(w, c)
            for half in range(2):
                add(wo, half * BC, (first_row, first_row + GW))
        add(kv, 0)
        add(kv, GW)
        mixer((5640, 6152), 1536)
        mixer((0, 512, 1024, 1536), 0)
        mixer((3592, 4104, 4616, 5128), 1024)
        mixer((2048, 2560, 3072), 512)
    for l in range(DEPTH):
        def ffn(name):
            g, u, d = (v[f"{name}_w_{p}_2"][l] for p in ("gate", "up", "down"))
            gu = np.stack([g.reshape(D, 11, 256), u.reshape(D, 11, 256)], axis=2).reshape(D, -1)
            at = 0
            for units, downs in FF_HALVES:
                for i in range(at, at + units):
                    add(gu, i * BC)
                for half in range(2):
                    add(d, half * BC, (at * 256, (at + units) * 256))
                at += units
        ffn("ffn1")
        for c in range(5):
            add(v["w_in_2"][l], c * BC)
        for half in range(2):
            add(v["w_out_2"][l], half * BC)
        ffn("ffn2")
    return np.stack(out)


def kernel(**inputs):
    import concourse.bacc as bacc
    from concourse.bass_utils import run_bass_kernel_spmd

    v = {k: np.ascontiguousarray(a) for k, a in inputs.items()}
    f = np.float32
    c0, c1, c2, c3 = (np.concatenate([a.astype(f) for a in c.values()], axis=1) for c in constants())
    rows1 = np.concatenate([v["pre_norm_g"], v["post_norm_g"], v["mem_norm_g"], v["ssd_norm_g"], v["dt_bias"],
                            v["a_log"], v["d_skip"]], axis=1)
    conv1 = np.concatenate([v["conv_w"], v["conv_b"][:, None]], axis=1).reshape(DEPTH, 5, 8, P)
    conv1 = conv1.transpose(0, 3, 2, 1).reshape(DEPTH, P, 40)
    w_dt = v["w_in"][:, :, 3584:3592].reshape(DEPTH, 8, P, 8).transpose(0, 2, 1, 3).reshape(DEPTH, P, 64)
    ln_rows = np.stack([v["ln_g_2"], v["ln_b_2"]], axis=2).reshape(DEPTH, 3, 2 * D)
    pool_w = np.zeros((DEPTH, P, 2, P), f)
    for g in range(4):
        a = 64 * (g % 2)
        pool_w[:, a:a + 64, g // 2, a:a + 64] = v["pool_w_2"][:, g]
    cols2 = np.concatenate([v["conv_w_2"], v["pool_scale_2"][:, None]], axis=1).reshape(DEPTH, 4, 2, P)
    cols2 = cols2.transpose(0, 3, 2, 1).reshape(DEPTH, P, 8)
    rpb = v["rpb_2"].transpose(0, 2, 1, 3).reshape(DEPTH, 15, NA_H * 31)

    arrays = {"in_x": v["x"], "in_mem": v["mem"], "in_stream": weight_stream(v), "in_const0": c0, "in_const1": c1,
              "in_const2": c2, "in_rows1": rows1, "in_conv1": conv1, "in_w_dt": w_dt, "in_ln_rows": ln_rows,
              "in_pool_w": pool_w.reshape(DEPTH, P, 2 * P), "in_cols2": cols2, "in_rpb": rpb, "in_sel": c3}
    arrays = {k: np.ascontiguousarray(a) for k, a in arrays.items()}
    nc = bacc.Bacc("TRN2", target_bir_lowering=False, num_devices=1)
    args = [nc.dram_tensor(k, a.shape, mybir.dt.from_np(a.dtype), kind="ExternalInput").ap() for k, a in arrays.items()]
    out = nc.dram_tensor("out_0", (1, SEQ, D), F32, kind="ExternalOutput").ap()
    build(nc, *args, out)
    r = run_bass_kernel_spmd(nc, [arrays], core_ids=[0])
    return r.results[0]["out_0"]
```

```python
from contextlib import ExitStack

import numpy as np

import concourse.bass as bass
from concourse import mybir

F32 = mybir.dt.float32
F32R = mybir.dt.float32r
ALU = mybir.AluOpType
ACT = mybir.ActivationFunctionType
AX = mybir.AxisListType

P = 128
DEPTH = 2
SEQ = 512
D = 1024
TILES = SEQ // P
DCH = D // P
N_MEM = 256
GW = 512
HEADS = 4
HD = 128
SSD_H = 8
D_FF = 2816
EPS = 1e-6
LN_EPS = 1e-5
ALPHA = (2.0 * DEPTH) ** 0.25
SCALE = HD ** -0.5
NEG = -1e30
LN_EXP = "natural_log_exp_and_others"

KB = 4
BC = 512
BLOCK1 = 38
BLOCK2 = 82
UNITS1 = 23
UNITS2 = 2 * (11 + 4) + 5 + 2
FF_HALVES = ((6, (4, 4, 4)), (5, (4, 4, 2)))

NA_H = 8
NA_D = 64
GRID_W = 64
NA_R = 8
CONV2 = 256
LOG_G = np.log(1.0 - 2.0 ** (-5.0 - np.arange(HEADS, dtype=np.float32))).astype(np.float32)
RET_DECAY = [float(x) for x in np.exp(np.float32(P) * LOG_G)]

PRE_G, POST_G, MEM_G, SSD_G, DT_B, A_LOG, D_SKIP = 0, 1024, 2048, 3072, 3584, 3592, 3600
ROW1 = 3608


def constants():
    f = np.float32
    i = np.arange(P)
    inv = f(10000.0) ** (-np.arange(0, HD, 2, dtype=f) / f(HD))
    ang = np.arange(SEQ, dtype=f)[:, None] * inv[None, :].astype(f)
    cos, sin = np.cos(ang).T, np.sin(ang).T
    rot = np.zeros((P, P), f)
    rot[i[64:], i[:64]] = -1.0
    rot[i[:64], i[64:]] = 1.0
    rel = (i[None, :] - i[:, None]).astype(f)
    intra = np.stack([np.where(rel >= 0, np.exp(np.maximum(rel, 0) * g), 0) * f(SCALE) for g in LOG_G], 1)
    xi = np.stack([np.broadcast_to(np.exp((i + 1).astype(f) * g), (P, P)) for g in LOG_G], 1)
    zeta = np.stack([np.exp((P - 1 - i).astype(f) * g) * f(SCALE) for g in LOG_G], 1)
    first = {
        "cos": np.concatenate([cos, cos]), "sin": np.concatenate([sin, sin]), "rot": rot,
        "upto": (i[:, None] <= i[None, :]), "from": (i[:, None] >= i[None, :]), "ones": np.ones((P, P)),
        "upto_neg": np.where(i[:, None] <= i[None, :], 0, NEG), "before": (i[:, None] < i[None, :]),
        "before_neg": np.where(i[:, None] < i[None, :], 0, NEG),
        "intra": intra.reshape(P, -1), "xi": xi.reshape(P, -1), "zeta": zeta,
    }
    cl = i // NA_R
    def mask(qb, kb):
        c, k = 16 * qb + cl[:, None], 16 * kb + cl[None, :]
        lo = np.clip(c - 8, 0, GRID_W - 16)
        return np.where((k >= lo) & (k < lo + 16), 0, NEG)
    masks = np.stack([mask(0, 0), mask(2, 1), mask(1, 1), mask(1, 2), mask(3, 3)], 1)
    assert (mask(0, 1) == mask(1, 2)).all() and (mask(3, 2) == mask(2, 1)).all() and (mask(2, 2) == mask(1, 1)).all()
    sel = np.zeros((P, NA_R, P))
    for k in range(NA_R):
        sel[k - i % NA_R + 7, k, i] = 1.0
    pool = np.zeros((P, 4, 4, 144))
    t = np.arange(SEQ)
    for g, w in enumerate((2, 4, 8, 16)):
        lo, hi = np.clip(t - w // 2, 0, SEQ), np.clip(t - w // 2 + w, 0, SEQ)
        m = ((t[:, None] >= lo[None]) & (t[:, None] < hi[None])) / (hi - lo)[None].astype(f) - np.eye(SEQ)
        for c in range(4):
            for col in range(144):
                tt = 128 * c + col - 8
                if 0 <= tt < SEQ:
                    pool[:, g, c, col] = m[128 * c:128 * c + 128, tt]
    second = {"masks": masks.reshape(P, -1), "pool": pool.reshape(P, -1)}
    return {"ident": np.eye(P)}, first, second, {"sel": sel.reshape(P, -1)[:15]}


def columns(parts):
    at, out = 0, {}
    for name, a in parts.items():
        out[name] = (at, at + a.shape[1])
        at += a.shape[1]
    return out, at


def build(nc, x_in, mem_in, stream, const0, const1, const2, rows1, conv1, w_dt, ln_rows, pool_w, cols2, rpb, sel_in, out):
    c0, c1, c2, _ = constants()
    _, N0 = columns(c0)
    at1, N1 = columns(c1)
    at2, N2 = columns(c2)

    ctx = ExitStack()
    with ctx:
        def sb(name, shape, dt=F32, on=ctx):
            return on.enter_context(nc.sbuf_tensor(name, shape, dt))

        def sem(name):
            return ctx.enter_context(nc.semaphore(name))

        ident = sb("ident", [P, N0])
        x = sb("x", [P, TILES, D])
        xT_hi = sb("xT_hi", [P, DCH, SEQ], F32R)
        xT_lo = sb("xT_lo", [P, DCH, SEQ], F32R)
        raw = sb("raw", [P, 2, KB, BC])
        w_hi = sb("w_hi", [P, 2, KB, BC], F32R)
        w_lo = sb("w_lo", [P, 2, KB, BC], F32R)
        rs_v = sb("rs_v", [P, 16])
        rs_r = sb("rs_r", [P, 16])
        rs_t = sb("rs_t", [P, 16])
        stats = sb("stats", [P, 16, 6])
        mean_var = sb("mean_var", [P, 16, 2])

        one = ExitStack()
        cst = sb("cst", [P, N1], on=one)
        row = sb("row", [P, ROW1], on=one)
        conv = sb("conv", [P, 8, 5], on=one)
        wdt = sb("wdt", [P, 8, 8], on=one)
        wdt_hi = sb("wdt_hi", [P, 8, 8], F32R, on=one)
        wdt_lo = sb("wdt_lo", [P, 8, 8], F32R, on=one)
        fA = sb("fA", [P, 4, 512], on=one)
        fB = sb("fB", [P, 4, 512], on=one)
        tA = sb("tA", [P, 4, 512], on=one)
        tB = sb("tB", [P, 4, 512], on=one)
        mix = sb("mix", [P, 4, 512], on=one)
        y_acc = sb("y_acc", [P, TILES, D], on=one)
        xn = sb("xn", [P, 2, 1024], on=one)
        state = sb("state", [P, 512], on=one)
        mk = y_acc[:, 0, :].rearrange("p (h n) -> p h n", h=4)
        mem_t = fA[:, :, :].rearrange("p c n -> p (c n)").rearrange("p (t d) -> p t d", t=2)
        small = sb("small", [P, 12, 32], on=one)
        with ExitStack() as over:
            sA = sb("sA", [P, 2048], on=over)
            sB = sb("sB", [P, 2048], on=over)
        mixT_hi = sb("mixT_hi", [P, 4, SEQ], F32R, on=one)
        mixT_lo = sb("mixT_lo", [P, 4, SEQ], F32R, on=one)
        one.close()

        two = ExitStack()
        lnr = sb("lnr", [P, 2, D], on=two)
        cst2 = sb("cst2", [P, N2], on=two)
        work = sb("work", [P, 3072], on=two)
        poolw = sb("poolw", [P, 2, P], on=two)
        col2 = sb("col2", [P, 2, 4], on=two)
        nmx = sb("nmx", [P, 4, 32], on=two)
        with ExitStack() as over:
            qkv = sb("qkv", [P, 3 * 4 * SEQ], on=over)
            bm = sb("bm", [P, NA_H, 5, P], on=over)
            y2_hi = sb("y2_hi", [P, 8, SEQ], F32R, on=over)
            y2_lo = sb("y2_lo", [P, 8, SEQ], F32R, on=over)
        h_hi = sb("h_hi", [P, 12, SEQ], F32R, on=two)
        h_lo = sb("h_lo", [P, 12, SEQ], F32R, on=two)
        two.close()

        qp, kp, vp = (qkv[:, i * 2048:i * 2048 + 2048].rearrange("p (c t) -> p c t", c=4) for i in range(3))
        sel = bm[:, :, :, :].rearrange("p h a b -> p (h a b)")[:, 0:1024]
        conv_out = lnr[:, 0, :]
        shifted = qkv[:, 0:3072].rearrange("p (h k e) -> p h k e", h=8, k=8)
        raw_rows = work[:, 256:256 + 1984]

        def p_slot(i):
            return work[:, (i % 3) * 384:(i % 3) * 384 + 384]

        def pt_slot(i):
            return work[:, (3 + i % 2) * 384:(3 + i % 2) * 384 + 384]

        def c1v(name):
            a, b = at1[name]
            return cst[:, a:b]

        def c2v(name):
            a, b = at2[name]
            return cst2[:, a:b]

        I = ident[:, 0:P]
        G = ctx.enter_context(nc.psum_tensor("G", [P, 4, 512], F32))
        A = ctx.enter_context(nc.psum_tensor("A", [P, 4, 512], F32))

        raw_in = [sem("raw_in0"), sem("raw_in1")]
        hi_done = sem("hi_done")
        lo_done = sem("lo_done")
        blk_used = sem("blk_used")
        g_done = [sem(f"g_done{i}") for i in range(3)]
        g_free = [sem(f"g_free{i}") for i in range(4)]
        pe_end, act_end, pool_end = sem("pe_end"), sem("act_end"), sem("pool_end")
        layer_open = sem("layer_open")
        const_in, x_loaded, out_done = sem("const_in"), sem("x_loaded"), sem("out_done")
        const1_in = sem("const1_in")
        const2_in = sem("const2_in")
        stage = {}

        def st(name):
            if name not in stage:
                stage[name] = sem(name)
            return stage[name]

        landed = {n: sem(n) for n in "row_in conv_in wdt_in mem_in ln_in poolw_in col2_in rpb_in sel_in shift_in".split()}

        def param(eng, l, name, k=1, per=1):
            eng.wait_ge(landed[name], l * (16 * per) + 16 * k)

        for n in ("layer_begun layer_left perm_hi perm_lo row_used ln_bias ln_std ln_gain y_scaled x_added rs_in rs_out act_chain dve_chain "
                  "tr_src tr_done tr_hi tr_lo "
                  "ff_s ff_h ff_hi ff_lo half_done "
                  "ev_mem ev_a ev_b ev_c ev_d "
                  "m_log m_nb m_p m_pt m_ptc m_o m_y "
                  "rot_done rot_used ret_ready rz_t rz_used r_s r_sm r_y r_kv r_yu r_st mix_ready "
                  "s_log s_ab s_ln s_sp s_cum s_d s_w s_pv s_pvu "
                  "conv_done conv_silu x_t x_tc dt_p dt_ab dt_ln dt_da dt_cs dt_sub dt_ex dt_al wdt_h wdt_l "
                  "dt_row dt_t d_skip d_in d_kv d_bc d_t d_e d_sc d_y d_yu d_st "
                  "b_g b_gc b_bm b_raw p_t p_tc p_y z_y y2h y2l n_s n_m n_p n_pn n_t n_tc n_o n_oh n_ol").split():
            st(n)
        S = stage
        nums = [s.num for s in S.values()]
        STAGES = range(nums[0], nums[-1] + 1)
        assert nums == list(STAGES)

        def bcast(ap, shape):
            return ap.to_broadcast(shape)

        block = ctx.enter_context(nc.Block())

        def perm_view(ap):
            return ap.rearrange("p (r c) -> p c r", c=GRID_W)

        @block.sync
        def _(sp):
            pairs = DEPTH * (BLOCK1 + BLOCK2) // 2
            with sp.Fori(0, pairs) as m:
                for s in range(2):
                    sp.wait_ge(lo_done, 2 * m + s + 1)
                    sp.dma_start(raw[:, s, :, :].rearrange("p k n -> p (k n)"),
                                 stream[bass.ds(2 * m + s, 1)].rearrange("o p n -> (o p) n")).then_inc(raw_in[s], 16)

        @block.tensor
        def _(pe):
            mm = nc.tensor.matmul
            pe.sem_inc(blk_used, 2)

            class Pos:
                pair, off, ubase, u = 0, 0, 0, 0

            def gemm_steps(kbs, jobs):
                c = 0
                for b, nk in enumerate(kbs):
                    s = Pos.off % 2
                    pe.wait_ge(lo_done, 2 * Pos.pair + Pos.off + 3)
                    for n, (bank, emits) in enumerate(jobs):
                        if b == 0:
                            pe.wait_ge(g_free[bank], Pos.ubase + Pos.u + 1)
                        for e, emit in enumerate(emits):
                            for k in range(nk):
                                last = emit(c + k, w_hi[:, s, k, :], w_lo[:, s, k, :],
                                            b == 0 and k == 0 and e == 0, b == len(kbs) - 1 and k == nk - 1)
                        if n == 3:
                            last.then_inc(blk_used, 1)
                        elif b == len(kbs) - 1:
                            last.then_inc(g_done[bank], 1)
                        if n == len(jobs) - 1:
                            Pos.off += 1
                            c += nk
                            if b == len(kbs) - 1:
                                Pos.u += 1
                        yield

            def gemm(kbs, jobs):
                for _ in gemm_steps(kbs, jobs):
                    pass

            def results_read():
                for bank in range(4):
                    pe.wait_ge(g_free[bank], Pos.ubase + Pos.u + 1)

            def feat(bank, hi, lo, col, n=SEQ, dst=None):
                o = G[:, bank, 0:n]

                def emit(c, wh, wl, start, stop):
                    a = wh[:, col:col + P]
                    mm(o, a, hi[:, c, 0:n], start=start, stop=False)
                    mm(o, a, lo[:, c, 0:n], start=False, stop=False)
                    return mm(o, wl[:, col:col + P], hi[:, c, 0:n], start=False, stop=stop)
                return emit

            def tok(bank, hi, lo, tile, col=0, n=BC, at=0, own_start=True):
                o = G[:, bank, at:at + n]

                def emit(c, wh, wl, start, stop):
                    a, b = hi[:, c, tile * P:tile * P + P], lo[:, c, tile * P:tile * P + P]
                    k = dict(skip_group_check=True) if n < BC else {}
                    mm(o, a, wh[:, col:col + n], start=start and own_start, stop=False, **k)
                    mm(o, a, wl[:, col:col + n], start=False, stop=False, **k)
                    return mm(o, b, wh[:, col:col + n], start=False, stop=stop, **k)
                return emit

            def feat4(n=SEQ):
                gemm((4, 4), [(o, [feat(o, xT_hi, xT_lo, o * P, n)]) for o in range(4)])

            def tok4(kbs=(4, 4), hi=xT_hi, lo=xT_lo):
                gemm(kbs, [(o, [tok(o, hi, lo, o)]) for o in range(4)])

            def gate_steps():
                return gemm_steps((4, 4), [(o, [tok(o, xT_hi, xT_lo, o)]) for o in range(4)])

            def advance(steps, n):
                for _ in range(n):
                    next(steps)

            def finished(steps):
                assert next(steps, "end") == "end"

            class N:
                tr = 0

            def transposes(src, tiles, groups):
                for t in range(tiles):
                    for g in range(groups):
                        if N.tr >= 4:
                            pe.wait_ge(S["tr_lo"], N.tr - 3)
                        pe.wait_ge(S["tr_src"], N.src + t + 1)
                        for c in range(4):
                            last = nc.tensor.transpose(A[:, N.tr % 4, c * P:c * P + P],
                                                       src(t)[:, (4 * g + c) * P:(4 * g + c + 1) * P], I)
                        last.then_inc(S["tr_done"], 1)
                        N.tr += 1
                N.src += tiles

            def mem_attention():
                results_read()
                gate = gate_steps()
                for q in range(TILES):
                    if q:
                        pe.wait_ge(S["m_y"], q)
                    for h in range(HEADS):
                        last = mm(A[:, h // 2, (h % 2) * 256:(h % 2) * 256 + 256], fA[:, h, q * P:q * P + P],
                                  mk[:, h, :], start=True, stop=True)
                    last.then_inc(S["m_log"], 1)
                    advance(gate, (2, 2, 1, 0)[q])
                    pe.wait_ge(S["m_p"], 4 * (q + 1))
                    pm = sA[:, 0:1024]
                    for i in range(8):
                        last = nc.tensor.transpose(A[:, 2 + i // 4, (i % 4) * P:(i % 4 + 1) * P],
                                                   pm[:, i * P:i * P + P], I)
                    last.then_inc(S["m_pt"], 1)
                    advance(gate, (1, 1, 1, 0)[q])
                    pe.wait_ge(S["m_ptc"], q + 1)
                    for h in range(HEADS):
                        for k in range(2):
                            last = mm(A[:, 0, h * P:h * P + P], sB[:, (2 * h + k) * P:(2 * h + k + 1) * P],
                                      tA[:, k, h * P:h * P + P], start=(k == 0), stop=(k == 1))
                    last.then_inc(S["m_o"], 1)
                finished(gate)

            def retention():
                results_read()
                pe.wait_ge(const1_in, 16)
                gate = gate_steps()
                for i in range(8):
                    if i >= 4:
                        advance(gate, 1)
                        pe.wait_ge(S["rot_used"], i - 3)
                    mm(A[:, i % 4, :], c1v("rot"), (fA if i < 4 else fB)[:, i % 4, :],
                       start=True, stop=True).then_inc(S["rot_done"], 1)
                pe.wait_ge(S["ret_ready"], 1)
                for c in range(3):
                    for h in range(HEADS):
                        last = nc.tensor.transpose(A[:, c, h * P:h * P + P], fB[:, h, c * P:c * P + P], I)
                    last.then_inc(S["rz_t"], 1)
                pe.wait_ge(S["rz_used"], 3)
                for c in range(TILES):
                    for h in range(HEADS):
                        last = mm(A[:, 0, h * P:h * P + P], fB[:, h, c * P:c * P + P], fA[:, h, c * P:c * P + P],
                                  start=True, stop=True)
                    last.then_inc(S["r_s"], 1)
                    if c < 3:
                        if c:
                            pe.wait_ge(S["r_st"], 4 * c)
                        for h in range(HEADS):
                            last = mm(A[:, 2, h * P:h * P + P], sB[:, c * 512 + h * P:c * 512 + h * P + P],
                                      tA[:, c, h * P:h * P + P], start=True, stop=True)
                        last.then_inc(S["r_kv"], 1)
                    advance(gate, 1 if c < 2 else 0)
                    pe.wait_ge(S["r_sm"], c + 1)
                    if c:
                        pe.wait_ge(S["r_yu"], c)
                        pe.wait_ge(S["r_st"], 4 * c)
                    for h in range(HEADS):
                        last = mm(A[:, 1, h * P:h * P + P], xn[:, 0, h * P:h * P + P], tA[:, c, h * P:h * P + P],
                                  start=True, stop=(c == 0))
                        if c:
                            last = mm(A[:, 1, h * P:h * P + P], sA[:, h * 512 + c * P:h * 512 + c * P + P],
                                      state[:, h * P:h * P + P], start=False, stop=True)
                    last.then_inc(S["r_y"], 1)
                advance(gate, 2)
                finished(gate)

            SB_AT = (0, 512, 1024, 896)

            def stick():
                results_read()
                gate = gate_steps()
                flat = A[:, :, :].rearrange("p b n -> p (b n)")
                for h in range(HEADS):
                    if h:
                        pe.wait_ge(S["s_d"], h)
                    for i in range(4):
                        n = (4 - i) * P
                        last = mm(flat[:, SB_AT[i]:SB_AT[i] + n], fB[:, h, i * P:i * P + P], fA[:, h, i * P:SEQ],
                                  start=True, stop=True, skip_group_check=True)
                    last.then_inc(S["s_log"], 1)
                    advance(gate, (2, 2, 1, 0)[h])
                    pe.wait_ge(S["s_sp"], h + 1)
                    for i in range(4):
                        for k in range(i, 4):
                            w, n = (k - i) * P, (4 - k) * P
                            last = mm(flat[:, SB_AT[i] + w:SB_AT[i] + w + n], c1v("from" if k == i else "ones"),
                                      sB[:, SB_AT[k]:SB_AT[k] + n], start=(k == i and i != 3), stop=(k == 3),
                                      skip_group_check=True)
                        if i == 1:
                            last = mm(flat[:, SB_AT[3]:SB_AT[3] + P], c1v("from"), sB[:, SB_AT[3]:SB_AT[3] + P],
                                      start=False, stop=True, skip_group_check=True)
                        if i == 2:
                            break
                    last.then_inc(S["s_cum"], 1)
                    advance(gate, (1, 1, 1, 0)[h])
                    pe.wait_ge(S["s_w"], h + 1)
                    if h:
                        pe.wait_ge(S["s_pvu"], h)
                    for j in range(4):
                        for i in range(j + 1):
                            last = mm(A[:, 3, j * P:j * P + P], sA[:, SB_AT[i] + (j - i) * P:SB_AT[i] + (j - i + 1) * P],
                                      tA[:, i, h * P:h * P + P], start=(i == 0), stop=(i == j))
                    last.then_inc(S["s_pv"], 1)
                finished(gate)

            def ssd():
                pe.wait_ge(S["wdt_l"], 1)
                for k in range(8):
                    o = A[0:8, 3, :]
                    mm(o, wdt_hi[:, k, :], xT_hi[:, k, :], start=(k == 0), stop=False)
                    mm(o, wdt_hi[:, k, :], xT_lo[:, k, :], start=False, stop=False)
                    last = mm(o, wdt_lo[:, k, :], xT_hi[:, k, :], start=False, stop=(k == 7))
                last.then_inc(S["dt_p"], 1)
                feat4()
                pe.wait_ge(S["dt_row"], 1)
                for t in range(TILES):
                    last = nc.tensor.transpose(A[:, 2, 8 * t:8 * t + 8], xn[0:8, 1, 512 + t * P:512 + t * P + P],
                                               ident[0:8, 0:8])
                last.then_inc(S["dt_t"], 1)
                feat4()
                pe.wait_ge(S["dt_da"], 1)
                da = small[:, 3, :]
                mm(A[:, 2, 0:32], c1v("upto"), da, start=True, stop=True)
                mm(A[:, 2, 32:64], c1v("ones"), da, start=True, stop=True).then_inc(S["dt_cs"], 1)
                gate = gate_steps()
                advance(gate, 5)
                pe.wait_ge(S["conv_silu"], 8)
                for c in range(TILES):
                    if c >= 2:
                        pe.wait_ge(S["x_tc"], 2 * (c - 1))
                    b = c % 2
                    for i in range(4):
                        nc.tensor.transpose(A[:, b, i * P:i * P + P], fA[:, i, c * P:c * P + P], I)
                    for i in range(2):
                        if c >= 1 and i == 0:
                            pe.wait_ge(S["x_tc"], 2 * c)
                        elif i == 0:
                            pe.wait_ge(S["dt_sub"], 1)
                        last = nc.tensor.transpose(A[:, 2, i * P:i * P + P], fB[:, i, c * P:c * P + P], I)
                    last.then_inc(S["x_t"], 1)
                pe.wait_ge(S["x_tc"], 8)
                for c in range(TILES):
                    if c:
                        pe.wait_ge(S["d_in"], c)
                        pe.wait_ge(S["d_st"], c)
                    for h in range(SSD_H):
                        mm(A[:, h // 4, (h % 4) * P:(h % 4 + 1) * P], bcast(da[:, 8 * c + h:8 * c + h + 1], [P, P]),
                           c1v("upto"), start=True, stop=True)
                    for g in range(2):
                        last = mm(A[:, 2, g * P:g * P + P], fB[:, g, c * P:c * P + P], fB[:, 2 + g, c * P:c * P + P],
                                  start=True, stop=True)
                    last.then_inc(S["d_bc"], 1)
                    advance(gate, (2, 1, 0, 0)[c])
                    pe.wait_ge(S["d_t"], c + 1)
                    if c:
                        for g in range(2):
                            last = mm(A[:, 0, g * 256:g * 256 + 256], fB[:, 2 + g, c * P:c * P + P],
                                      state[:, g * 256:g * 256 + 256], start=True, stop=True)
                    if c < 3:
                        for g in range(2):
                            last = mm(A[:, 1, g * 256:g * 256 + 256], xn[:, c // 2, (c % 2) * 256 + g * P:(c % 2) * 256 + g * P + P],
                                      sA[:, c * 512 + g * 256:c * 512 + g * 256 + 256], start=True, stop=True)
                    last.then_inc(S["d_kv"], 1)
                    pe.wait_ge(S["d_sc"], c + 1)
                    if c:
                        pe.wait_ge(S["d_yu"], c)
                    for h in range(SSD_H):
                        last = mm(A[:, 3, h * 64:h * 64 + 64], sB[:, 1024 + h * P:1024 + h * P + P],
                                  fA[:, c, h * 64:h * 64 + 64], start=True, stop=True)
                    last.then_inc(S["d_y"], 1)
                finished(gate)

            def mixer_out():
                transposes(lambda t: mix[:, t, :], TILES, 1)
                pe.wait_ge(S["tr_lo"], N.tr)
                for half in range(2):
                    tok4(kbs=(4,), hi=mixT_hi, lo=mixT_lo)

            pe.wait_ge(const_in, 16)
            with pe.Fori(0, DEPTH) as l:
                Pos.l = l
                Pos.pair, Pos.off, Pos.ubase, Pos.u = l * (BLOCK1 // 2), 0, l * UNITS1, 0
                N.tr, N.src = 0, 0
                pe.wait_ge(layer_open, l + 1)
                pe.sem_inc(S["layer_begun"], 1)
                transposes(lambda t: xn[:, t % 2, :], 2, 2)
                pe.wait_ge(S["tr_lo"], N.tr)
                feat4(N_MEM)
                gemm((4, 4), [(o, [tok(o, xT_hi, xT_lo, o // 2, col=(o % 2) * 256, n=256)]) for o in range(4)])
                transposes(lambda t: xn[:, t % 2, :], 4, 2)
                pe.wait_ge(S["tr_lo"], N.tr)
                feat4()
                mem_attention()
                mixer_out()
                feat4()
                feat4()
                tok4()
                retention()
                mixer_out()
                feat4()
                feat4()
                tok4()
                stick()
                mixer_out()
                ssd()
                mixer_out()
                assert Pos.off == BLOCK1 and Pos.u == UNITS1
                pe.sem_inc(pe_end, 1)

            def ffn():
                for n, (units, downs) in enumerate(FF_HALVES):
                    base_pair, base_off, base_u = Pos.pair, Pos.off, Pos.u
                    assert base_off % 2 == 0
                    ub = Pos.ubase
                    with pe.Fori(0, units) as u:
                        Pos.pair, Pos.off, Pos.ubase, Pos.u = base_pair + u, base_off, ub + u, base_u
                        feat4()
                    Pos.pair, Pos.off, Pos.ubase, Pos.u = base_pair, base_off + 2 * units, ub, base_u + units
                    N.ff += 2 * units
                    pe.wait_ge(S["ff_lo"], N.ff)
                    for half in range(2):
                        gemm(downs, [(o, [tok(o, h_hi, h_lo, o)]) for o in range(4)])

            def bias():
                param(pe, Pos.l, "rpb_in")
                param(pe, Pos.l, "sel_in")
                for k in range(NA_R):
                    if k >= 4:
                        pe.wait_ge(S["b_gc"], k - 3)
                    mm(A[:, k % 4, 0:248], sel[0:15, k * P:k * P + P], work[0:15, 0:248],
                       start=True, stop=True).then_inc(S["b_g"], 1)
                pe.wait_ge(S["b_gc"], NA_R)

            def pool_mixer():
                results_read()
                param(pe, Pos.l, "poolw_in")
                pe.wait_ge(const2_in, 16)
                for ch in range(2):
                    for gg in range(2):
                        g = 2 * ch + gg
                        for c in range(4):
                            lo, hi = max(0, 128 * c - 8), min(SEQ, 128 * c + 136)
                            o = c2v("pool")[:, (4 * g + c) * 144 + lo - (128 * c - 8):(4 * g + c) * 144 + hi - (128 * c - 8)]
                            last = mm(A[64 * gg:64 * gg + 64, ch, lo:hi], work[:, c * 256 + g * 64:c * 256 + g * 64 + 64], o,
                                      start=(c == 0), stop=(c == 3), skip_group_check=True)
                    last.then_inc(S["p_t"], 1)
                for ch in range(2):
                    pe.wait_ge(S["p_tc"], ch + 1)
                    mm(A[:, 2 + ch, :], poolw[:, ch, :], y2tmp(ch), start=True, stop=True).then_inc(S["p_y"], 1)

            def y2tmp(ch):
                return conv_out[:, ch * 512:ch * 512 + 512]

            def neighbourhood():
                pe.wait_ge(S["b_bm"], 1)
                pe.wait_ge(S["y2l"], 4)
                combos = [(h, j) for h in range(NA_H) for j in range(4)]

                def scores(i):
                    h, j = combos[i]
                    r = 64 * (h % 2)
                    a, b = max(0, j - 1), min(4, j + 2)
                    if i >= 2:
                        pe.wait_ge(S["n_m"], i - 1)
                    mm(A[:, i % 2, 0:(b - a) * P], qp[r:r + 64, h // 2, j * P:j * P + P],
                       kp[r:r + 64, h // 2, a * P:b * P], start=True, stop=True).then_inc(S["n_s"], 1)

                def turn(i):
                    h, j = combos[i]
                    n = min(4, j + 2) - max(0, j - 1)
                    pe.wait_ge(S["n_pn"], i + 1)
                    if i:
                        pe.wait_ge(S["n_tc"], i)
                    for k in range(n):
                        last = nc.tensor.transpose(A[:, 2, k * P:k * P + P], p_slot(i)[:, k * P:k * P + P], I)
                    last.then_inc(S["n_t"], 1)

                def pv(i):
                    h, j = combos[i]
                    r = 64 * (h % 2)
                    a, b = max(0, j - 1), min(4, j + 2)
                    pe.wait_ge(S["n_tc"], i + 1)
                    if i % 8 == 0 and i:
                        pe.wait_ge(S["n_ol"], i // 8)
                    for k in range(a, b):
                        last = mm(A[r:r + 64, 3, j * P:j * P + P], vp[:, k, h * 64:h * 64 + 64],
                                  pt_slot(i)[:, (k - a) * P:(k - a + 1) * P],
                                  start=(k == a), stop=(k == b - 1), skip_group_check=True)
                    last.then_inc(S["n_o"], 1)

                for i in range(len(combos) + 3):
                    if i < len(combos):
                        scores(i)
                    if 2 <= i < len(combos) + 2:
                        turn(i - 2)
                    if i >= 3:
                        pv(i - 3)

            with pe.Fori(0, DEPTH) as l:
                Pos.l = l
                Pos.pair, Pos.off = l * (BLOCK2 // 2) + DEPTH * BLOCK1 // 2, 0
                Pos.ubase, Pos.u = l * UNITS2 + DEPTH * UNITS1, 0
                N.tr, N.src, N.ff = 0, 0, 0
                pe.wait_ge(layer_open, l + 1 + DEPTH)
                pe.sem_inc(S["layer_begun"], 1)
                transposes(lambda t: x[:, t, :], 4, 2)
                pe.wait_ge(S["tr_lo"], N.tr)
                ffn()
                bias()
                transposes(lambda t: x[:, t, :], 4, 2)
                pe.wait_ge(S["tr_lo"], N.tr)
                gemm((4, 4), [(b, [tok(b, xT_hi, xT_lo, 2 * b + i, n=256, at=256 * i, own_start=(i == 0)) for i in range(2)])
                              for b in range(2)] +
                     [(2 + i, [feat(2 + i, xT_hi, xT_lo, 256 + i * P)]) for i in range(2)])
                feat4()
                feat4()
                feat4()
                pe.wait_ge(S["perm_hi"], 1)
                pe.wait_ge(S["perm_lo"], 1)
                tok4(hi=y2_hi, lo=y2_lo)
                pool_mixer()
                neighbourhood()
                pe.wait_ge(S["n_ol"], 4)
                for half in range(2):
                    gemm((4, 4), [(o, [tok(o, y2_hi, y2_lo, o)]) for o in range(4)])
                transposes(lambda t: x[:, t, :], 4, 2)
                pe.wait_ge(S["tr_lo"], N.tr)
                ffn()
                assert Pos.off == BLOCK2 and Pos.u == UNITS2, (Pos.off, Pos.u)
                pe.sem_inc(pe_end, 1)

        @block.scalar
        def _(act):
            fn = nc.scalar.activation
            for i in range(4):
                act.sem_inc(g_free[i], 1)
            act.dma_start(ident[:, :], const0).then_inc(const_in, 16)

            class Pos:
                pair, off, end, ubase, u = 0, 0, 0, 0, 0

            class N:
                tr, ch, rs, ff = 0, 0, 0, 0

            def link(ins):
                N.ch += 1
                ins.then_inc(S["act_chain"], 1)
                act.wait_ge(S["act_chain"], N.ch)

            def split(nk=KB):
                s = Pos.off % 2
                act.wait_ge(raw_in[s], (Pos.pair + Pos.off // 2 + 1) * 16)
                act.wait_ge(blk_used, 2 * Pos.pair + Pos.off + 1)
                fn(w_hi[:, s, 0:nk, :], raw[:, s, 0:nk, :], ACT.Copy).then_inc(hi_done, 1)
                Pos.off += 1

            def unit(evac, nxt):
                if nxt:
                    split(nxt[0])
                evac()
                for nk in nxt[1:]:
                    split(nk)
                Pos.u += 1
                Pos.end += len(nxt)

            def done(bank):
                if bank < 3:
                    act.wait_ge(g_done[bank], Pos.ubase + Pos.u + 1)
                else:
                    act.wait_ge(blk_used, 2 * Pos.pair + Pos.end + 2)

            def evac4(dst, func=ACT.Copy, src=None):
                def go():
                    for b in range(4):
                        done(b)
                        fn(dst(b), src(b) if src else G[:, b, :], func).then_inc(g_free[b], 1)
                return go

            def gate_out():
                evac4(lambda b: tB[:, b, :], ACT.Silu)()
                Pos.u, Pos.end = Pos.u + 1, Pos.end + 1

            def tr_hi(dst, tiles, groups):
                for t in range(tiles):
                    for g in range(groups):
                        act.wait_ge(S["tr_done"], N.tr + 1)
                        fn(dst[:, 4 * g:4 * g + 4, t * P:t * P + P], A[:, N.tr % 4, :].rearrange("p (c t) -> p c t", c=4),
                           ACT.Copy).then_inc(S["tr_hi"], 1)
                        N.tr += 1

            def rsqrt(n, at=0):
                N.rs += 1
                act.preload_act_table_set(LN_EXP)
                act.wait_ge(S["rs_in"], N.rs)
                link(fn(rs_t[:, at:at + n], rs_v[:, at:at + n], ACT.Ln))
                fn(rs_r[:, at:at + n], rs_t[:, at:at + n], ACT.Exp, scale=-0.5).then_inc(S["rs_out"], 1)

            def layer_norm(i):
                for a in (0, 2):
                    rsqrt(2, a)
                    act.wait_ge(S["ln_bias"], 2 * i + a // 2 + 1)
                    for t in (a, a + 1):
                        fn(x[:, t, :], x[:, t, :], ACT.Identity, scale=rs_r[:, t:t + 1],
                           bias=nmx[:, 0, t:t + 1]).then_inc(S["ln_std"], 1)

            def mem_attention():
                for q in range(TILES):
                    if q == 3:
                        split()
                    act.wait_ge(S["m_nb"], q + 1)
                    act.wait_ge(S["m_log"], q + 1)
                    if q:
                        act.wait_ge(S["m_pt"], q)
                    for h in range(HEADS):
                        fn(sA[:, h * 256:h * 256 + 256], A[:, h // 2, (h % 2) * 256:(h % 2) * 256 + 256], ACT.Exp,
                           bias=small[:, 0, h:h + 1], scale=SCALE, accum_out=small[:, 1, h:h + 1]).then_inc(S["m_p"], 1)
                gate_out()

            def stick():
                act.preload_act_table_set(LN_EXP)
                for h in range(HEADS):
                    if h == 3:
                        split()
                    act.wait_ge(S["s_ab"], h + 1)
                    link(fn(sB[:, 0:1280], sB[:, 0:1280], ACT.Exp, scale=-1.0))
                    fn(sB[:, 0:1280], sB[:, 0:1280], ACT.Ln, bias=1.0).then_inc(S["s_ln"], 1)
                    act.wait_ge(S["s_d"], h + 1)
                    fn(sA[:, 0:1280], sA[:, 0:1280], ACT.Exp).then_inc(S["s_w"], 1)
                gate_out()

            def silu_conv(buf):
                def go():
                    for b in range(4):
                        act.wait_ge(g_free[b], Pos.ubase + Pos.u + 2)
                        fn(buf[:, b, :], buf[:, b, :], ACT.Silu).then_inc(S["conv_silu"], 1)
                return go

            def ssd():
                unit(silu_conv(fA), (4, 4))
                act.preload_act_table_set(LN_EXP)
                param(act, Pos.l, "row_in")
                fn(small[:, 11, 0:8], row[:, A_LOG:A_LOG + 8], ACT.Exp).then_inc(S["dt_al"], 1)
                act.wait_ge(S["dt_ab"], 1)
                link(fn(small[:, 1, :], small[:, 1, :], ACT.Exp, scale=-1.0))
                fn(small[:, 1, :], small[:, 1, :], ACT.Ln, bias=1.0).then_inc(S["dt_ln"], 1)
                unit(silu_conv(fB), (4, 4))
                act.preload_act_table_set(LN_EXP)
                act.wait_ge(S["dt_sub"], 1)
                fn(small[:, 6, :], small[:, 4, :], ACT.Exp).then_inc(S["dt_ex"], 1)
                fn(small[:, 7, :], small[:, 5, :], ACT.Exp).then_inc(S["dt_ex"], 1)
                fn(small[:, 8, :], small[:, 9, :], ACT.Exp).then_inc(S["dt_ex"], 1)
                for c in range(TILES):
                    if c == 2:
                        split()
                    if c == 3:
                        gate_out()
                        act.preload_act_table_set(LN_EXP)
                    act.wait_ge(S["d_t"], c + 1)
                    fn(sB[:, 0:1024], sB[:, 0:1024], ACT.Exp).then_inc(S["d_e"], 1)

            def mixer_out(nxt):
                tr_hi(mixT_hi, TILES, 1)
                unit(lambda: None, (4,))
                unit(lambda: None, nxt)

            act.dma_start(x[:, :, :], x_in.rearrange("a (t p) d -> p (a t) d", p=P)).then_inc(x_loaded, 16)
            act.dma_start(cst[:, :], const1).then_inc(const1_in, 16)
            T, K2 = (4, 4), (4, 4)
            with act.Fori(0, DEPTH) as l:
                Pos.l = l
                Pos.pair, Pos.off, Pos.end, Pos.ubase, Pos.u = l * (BLOCK1 // 2), 0, 2, l * UNITS1, 0
                N.tr, N.ch, N.rs = 0, 0, 0
                split()
                split()
                act.wait_ge(layer_open, l + 1)
                act.sem_inc(S["layer_begun"], 1)
                rsqrt(2)
                tr_hi(xT_hi, 2, 2)
                rsqrt(4)
                unit(evac4(lambda b: mk[:, b, :], src=lambda b: G[:, b, 0:N_MEM]), K2)
                unit(evac4(lambda b: tA[:, b // 2, (b % 2) * 256:(b % 2) * 256 + 256], src=lambda b: G[:, b, 0:256]), K2)
                tr_hi(xT_hi, 4, 2)
                unit(evac4(lambda b: fA[:, b, :]), K2)
                mem_attention()
                mixer_out(K2)
                unit(evac4(lambda b: fA[:, b, :]), K2)
                unit(evac4(lambda b: fB[:, b, :]), K2)
                unit(evac4(lambda b: tA[:, b, :]), K2)
                split()
                rsqrt(16)
                gate_out()
                mixer_out(K2)
                unit(evac4(lambda b: fA[:, b, :]), K2)
                unit(evac4(lambda b: fB[:, b, :]), K2)
                unit(evac4(lambda b: tA[:, b, :]), K2)
                stick()
                param(act, Pos.l, "wdt_in")
                fn(wdt_hi[:, :, :], wdt[:, :, :], ACT.Copy).then_inc(S["wdt_h"], 1)
                mixer_out(K2)
                ssd()
                rsqrt(8)
                mixer_out(())
                rsqrt(4)
                assert Pos.off == BLOCK1 and Pos.u == UNITS1
                act.sem_inc(act_end, 1)

            def ffn(nxt):
                for n, (units, downs) in enumerate(FF_HALVES):
                    base_pair, base_off, base_u, ub = Pos.pair, Pos.off, Pos.u, Pos.ubase
                    c0 = N.ff
                    with act.Fori(0, units) as u:
                        Pos.pair, Pos.off, Pos.end = base_pair + u, base_off, base_off
                        Pos.ubase, Pos.u = ub + u, base_u
                        split()
                        for i in range(2):
                            done(i)
                            act.wait_ge(g_free[2 + i], ub + u + (base_u + 1))
                            fn(work[:, i * 512:i * 512 + 512], G[:, i, :], ACT.Silu).then_inc(g_free[i], 1)
                        for i in range(2):
                            act.wait_ge(g_free[2 + i], ub + u + (base_u + 2))
                            fn(h_hi[:, bass.ds(2 * u + i, 1), :].rearrange("p o n -> p (o n)"),
                               work[:, 1024 + i * 512:1536 + i * 512], ACT.Copy).then_inc(S["ff_hi"], 1)
                        split()
                    Pos.pair, Pos.off, Pos.end = base_pair, base_off + 2 * units, base_off + 2 * units + 1
                    Pos.ubase, Pos.u = ub, base_u + units
                    N.ff += 2 * units
                    split(downs[2])
                    unit(lambda: None, (4, 4, downs[2]))
                    unit(lambda: None, (4, 4) if n == 0 else nxt)

            with act.Fori(0, DEPTH) as l:
                Pos.l = l
                Pos.pair, Pos.off, Pos.end = l * (BLOCK2 // 2) + DEPTH * BLOCK1 // 2, 0, 2
                Pos.ubase, Pos.u = l * UNITS2 + DEPTH * UNITS1, 0
                N.tr, N.ch, N.rs, N.ff = 0, 0, 0, 0
                split()
                split()
                act.wait_ge(layer_open, l + 1 + DEPTH)
                act.sem_inc(S["layer_begun"], 1)
                tr_hi(xT_hi, 4, 2)
                ffn(K2)
                layer_norm(0)
                for k in range(NA_R):
                    act.wait_ge(S["b_g"], k + 1)
                    fn(raw_rows.rearrange("p (h k e) -> p h k e", h=8, k=8)[:, :, k, :],
                       A[:, k % 4, 0:248].rearrange("p (h e) -> p h e", h=8), ACT.Copy).then_inc(S["b_gc"], 1)
                tr_hi(xT_hi, 4, 2)
                act.wait_ge(S["tr_hi"], N.tr)
                fn(y2_hi[:, :, :].rearrange("p k (c r) -> p k c r", r=NA_R),
                   xT_hi[:, :, :].bitcast(F32).rearrange("p k (r c) -> p k c r", c=GRID_W), ACT.Copy).then_inc(S["perm_hi"], 1)

                def ub():
                    for b in range(2):
                        done(b)
                        param(act, Pos.l, "shift_in", 16, 16)
                        fn(work[:, b * 512:b * 512 + 512], G[:, b, :], ACT.Copy).then_inc(g_free[b], 1)
                    for b in range(2):
                        done(2 + b)
                        fn(work[:, 1024 + b * 512:1536 + b * 512], G[:, 2 + b, :], ACT.Copy).then_inc(g_free[2 + b], 1)
                unit(ub, K2)

                def cz():
                    for b in range(2):
                        done(b)
                        fn(work[:, 2048 + b * 512:2560 + b * 512], G[:, b, :], ACT.Copy).then_inc(g_free[b], 1)
                unit(cz, K2)
                act.wait_ge(S["b_bm"], 1)
                unit(evac4(lambda b: qp[:, b, :].rearrange("p (c r) -> p c r", r=NA_R),
                           src=lambda b: perm_view(G[:, b, :])), K2)
                unit(evac4(lambda b: kp[:, b, :].rearrange("p (c r) -> p c r", r=NA_R),
                           src=lambda b: perm_view(G[:, b, :])), K2)
                unit(evac4(lambda b: vp[:, b, :]), K2)
                for ch in range(2):
                    act.wait_ge(S["p_t"], ch + 1)
                    act.wait_ge(S["z_y"], 2)
                    fn(conv_out[:, ch * 512:ch * 512 + 512], A[:, ch, :], ACT.Copy).then_inc(S["p_tc"], 1)
                param(act, Pos.l, "col2_in")
                for ch in range(2):
                    act.wait_ge(S["p_y"], ch + 1)
                    fn(y2_hi[:, ch, :], A[:, 2 + ch, :], ACT.Copy, scale=col2[:, ch, 3:4]).then_inc(S["y2h"], 1)
                for ch in range(2):
                    fn(y2_hi[:, 2 + ch, :], work[:, 1024 + ch * 512:1536 + ch * 512], ACT.Copy).then_inc(S["y2h"], 1)
                combos = [(h, j) for h in range(NA_H) for j in range(4)]

                def exps(i):
                    h, j = combos[i]
                    n = (min(4, j + 2) - max(0, j - 1)) * P
                    act.wait_ge(S["n_m"], i + 1)
                    w = p_slot(i)[:, 0:n]
                    fn(w, w, ACT.Exp, bias=nmx[:, 0, i:i + 1], accum_out=nmx[:, 1, i:i + 1]).then_inc(S["n_p"], 1)

                def turned(i):
                    h, j = combos[i]
                    n = (min(4, j + 2) - max(0, j - 1)) * P
                    act.wait_ge(S["n_t"], i + 1)
                    if i >= 2:
                        act.wait_ge(S["n_o"], i - 1)
                    fn(pt_slot(i)[:, 0:n], A[:, 2, 0:n], ACT.Copy).then_inc(S["n_tc"], 1)

                def pair_out(i):
                    act.wait_ge(S["n_o"], 8 * i + 8)
                    fn(y2_hi[:, 4 + i, :].rearrange("p (r c) -> p c r", c=GRID_W),
                       A[:, 3, :].rearrange("p (c r) -> p c r", r=NA_R), ACT.Copy).then_inc(S["n_oh"], 1)

                for i in range(len(combos) + 3):
                    if 2 <= i < len(combos) + 2:
                        turned(i - 2)
                    if i < len(combos):
                        exps(i)
                    if i >= 3 and (i - 3) % 8 == 7:
                        pair_out((i - 3) // 8)
                unit(lambda: None, K2)
                unit(lambda: None, K2)
                layer_norm(1)
                tr_hi(xT_hi, 4, 2)
                ffn(())
                layer_norm(2)
                assert Pos.off == BLOCK2 and Pos.u == UNITS2
                act.sem_inc(act_end, 1)

        @block.vector
        def _(dve):
            tt, ts, stt = nc.vector.tensor_tensor, nc.vector.tensor_scalar, nc.vector.scalar_tensor_tensor
            dve.sem_inc(lo_done, 2)

            class Pos:
                pair, off, end, ubase, u = 0, 0, 0, 0, 0

            class N:
                tr, ch, rs, ff, half = 0, 0, 0, 0, 0

            def link(ins):
                N.ch += 1
                ins.then_inc(S["dve_chain"], 1)
                dve.wait_ge(S["dve_chain"], N.ch)

            def split(nk=KB):
                s = Pos.off % 2
                dve.wait_ge(hi_done, 2 * Pos.pair + Pos.off + 1)
                tt(w_lo[:, s, 0:nk, :], raw[:, s, 0:nk, :], w_hi[:, s, 0:nk, :].bitcast(F32),
                   ALU.subtract).then_inc(lo_done, 1)
                Pos.off += 1

            def unit(evac, nxt):
                if nxt:
                    split(nxt[0])
                evac()
                for nk in nxt[1:]:
                    split(nk)
                Pos.u += 1
                Pos.end += len(nxt)

            def done(bank):
                if bank < 3:
                    dve.wait_ge(g_done[bank], Pos.ubase + Pos.u + 1)
                else:
                    dve.wait_ge(blk_used, 2 * Pos.pair + Pos.end + 2)

            def none():
                pass

            def results_read():
                for bank in range(4):
                    dve.wait_ge(g_free[bank], Pos.ubase + Pos.u + 1)

            def tr_lo(dst_hi, dst_lo, tiles, groups, src=None):
                for t in range(tiles):
                    if src:
                        src(t)
                    for g in range(groups):
                        dve.wait_ge(S["tr_hi"], N.tr + 1)
                        tt(dst_lo[:, 4 * g:4 * g + 4, t * P:t * P + P], A[:, N.tr % 4, :].rearrange("p (c t) -> p c t", c=4),
                           dst_hi[:, 4 * g:4 * g + 4, t * P:t * P + P].bitcast(F32), ALU.subtract).then_inc(S["tr_lo"], 1)
                        N.tr += 1

            def rsqrt(n, scale, eps):
                ts(rs_v[:, 0:n], rs_v[:, 0:n], scale, eps, ALU.mult, ALU.add).then_inc(S["rs_in"], 1)
                newton(n)

            def newton(n, at=0):
                v, r, t = rs_v[:, at:at + n], rs_r[:, at:at + n], rs_t[:, at:at + n]
                N.rs += 1
                dve.wait_ge(S["rs_out"], N.rs)
                link(tt(t, r, r, ALU.mult))
                link(tt(t, t, v, ALU.mult))
                link(ts(t, t, -0.5, 1.5, ALU.mult, ALU.add))
                link(tt(r, r, t, ALU.mult))

            def rms_operand(src, tiles, g, meanwhile):
                for t in range(tiles):
                    ins = nc.vector.tensor_tensor_reduce(out=xn[:, 0, :], in0=src(t), in1=src(t), scale=1.0, scalar=0.0,
                                                         op0=ALU.mult, op1=ALU.add, accum_out=rs_v[:, t:t + 1])
                    link(ins)
                rsqrt(tiles, 1.0 / D, EPS)
                base = N.tr

                def normed(t):
                    if t >= 2:
                        dve.wait_ge(S["tr_done"], base + 2 * (t - 1))
                    stt(out=xn[:, t % 2, :], in0=src(t), scalar=rs_r[:, t:t + 1], in1=row[:, g:g + D],
                        op0=ALU.mult, op1=ALU.mult).then_inc(S["tr_src"], 1)
                normed(0)
                normed(1)
                meanwhile()
                tr_lo(xT_hi, xT_lo, tiles, 2, lambda t: normed(t + 1) if 1 <= t < tiles - 1 else None)

            def heads(ap, n=4):
                return ap.unsqueeze(2).to_broadcast([P, n, P])

            def gate_split():
                split()
                Pos.u, Pos.end = Pos.u + 1, Pos.end + 1

            def mem_attention():
                for q in range(TILES):
                    if q == 3:
                        gate_split()
                    dve.wait_ge(S["m_log"], q + 1)
                    link(nc.vector.tensor_reduce(small[:, 2, 0:4],
                                                 A[:, 0:2, :].rearrange("p b (h n) -> p (b h) n", h=2), AX.X, ALU.max))
                    ts(small[:, 0, 0:4], small[:, 2, 0:4], -SCALE, None, ALU.mult).then_inc(S["m_nb"], 1)
                    dve.wait_ge(S["m_pt"], q + 1)
                    nc.vector.tensor_copy(sB[:, 0:1024], A[:, 2:4, :].rearrange("p b n -> p (b n)")).then_inc(S["m_ptc"], 1)
                    dve.wait_ge(S["m_p"], 4 * (q + 1))
                    link(nc.vector.reciprocal(small[:, 3, 0:4], small[:, 1, 0:4]))
                    dve.wait_ge(S["m_o"], q + 1)
                    m = mix[:, q, :].rearrange("p (h n) -> p h n", h=4)
                    tt(m, A[:, 0, :].rearrange("p (h n) -> p h n", h=4), heads(small[:, 3, 0:4]),
                       ALU.mult).then_inc(S["m_y"], 1)
                dve.wait_ge(S["m_y"], TILES)
                gated()

            def gated():
                results_read()
                for t in range(TILES):
                    tt(mix[:, t, :], mix[:, t, :], tB[:, t, :], ALU.mult).then_inc(S["tr_src"], 1)

            def mixer_out(first, nxt):
                tr_lo(mixT_hi, mixT_lo, TILES, 1)
                for half in range(2):
                    def add():
                        for b in range(4):
                            done(b)
                            o = y_acc[:, b, half * 512:half * 512 + 512]
                            if first:
                                ins = nc.vector.tensor_copy(o, G[:, b, :])
                            else:
                                ins = tt(o, o, G[:, b, :], ALU.add)
                            ins.then_inc(g_free[b], 1)
                            if half and not nxt:
                                dve.wait_ge(g_free[b], Pos.ubase + Pos.u + 2)
                                link(nc.vector.tensor_tensor_reduce(
                                    out=xn[:, 0, :], in0=y_acc[:, b, :], in1=y_acc[:, b, :], scale=1.0, scalar=0.0,
                                    op0=ALU.mult, op1=ALU.add, accum_out=rs_v[:, b:b + 1]))
                    unit(add, (4,) if half == 0 else nxt)

            def retention():
                dve.wait_ge(const1_in, 16)
                for i in range(8):
                    f = (fA if i < 4 else fB)[:, i % 4, :]
                    dve.wait_ge(S["rot_done"], i + 1)
                    tt(xn[:, 1, 0:512], A[:, i % 4, :], c1v("sin"), ALU.mult).then_inc(S["rot_used"], 1)
                    dve.wait_ge(S["rot_used"], i + 1)
                    link(tt(f, f, c1v("cos"), ALU.mult))
                    link(tt(f, f, xn[:, 1, 0:512], ALU.add))
                nc.vector.sem_inc(S["ret_ready"], 1)
                xi = c1v("xi").rearrange("p (h n) -> p h n", h=4)
                for h in range(HEADS):
                    link(tt(sA[:, h * 512:h * 512 + 512].rearrange("p (c n) -> p c n", c=4),
                            fA[:, h, :].rearrange("p (c n) -> p c n", c=4),
                            xi[:, h:h + 1, :].to_broadcast([P, 4, P]), ALU.mult))
                for c in range(3):
                    dve.wait_ge(S["rz_t"], c + 1)
                    ins = tt(sB[:, c * 512:c * 512 + 512].rearrange("p (h n) -> p h n", h=4),
                             A[:, c, :].rearrange("p (h n) -> p h n", h=4), heads(c1v("zeta")), ALU.mult)
                    ins.then_inc(S["rz_used"], 1)
                for c in range(TILES):
                    dve.wait_ge(S["r_s"], c + 1)
                    if c:
                        dve.wait_ge(S["r_y"], c)
                    tt(xn[:, 0, 0:512], A[:, 0, :], c1v("intra"), ALU.mult).then_inc(S["r_sm"], 1)
                    dve.wait_ge(S["r_y"], c + 1)
                    nc.vector.tensor_copy(mix[:, c, :], A[:, 1, :]).then_inc(S["r_yu"], 1)
                    if c < 3:
                        dve.wait_ge(S["r_kv"], c + 1)
                        for h in range(HEADS):
                            o, k = state[:, h * P:h * P + P], A[:, 2, h * P:h * P + P]
                            if c == 0:
                                nc.vector.tensor_copy(o, k).then_inc(S["r_st"], 1)
                            else:
                                stt(out=o, in0=o, scalar=RET_DECAY[h], in1=k, op0=ALU.mult,
                                    op1=ALU.add).then_inc(S["r_st"], 1)
                gate_split()
                dve.wait_ge(S["r_yu"], 4)
                m3 = mix[:, :, :].rearrange("p c (h n) -> p (c h) n", h=4)
                for i in range(16):
                    ins = nc.vector.bn_stats(stats[:, i, :], m3[:, i, :])
                link(ins)
                for i in range(16):
                    ins = nc.vector.bn_aggr(mean_var[:, i, :], stats[:, i, :])
                link(ins)
                link(nc.vector.tensor_copy(rs_v[:, 0:16], mean_var[:, :, 1]))
                rsqrt(16, 1.0, EPS)
                link(tt(m3, m3, heads(mean_var[:, :, 0], 16), ALU.subtract))
                link(tt(m3, m3, heads(rs_r[:, 0:16], 16), ALU.mult))
                gated()

            SB_AT = (0, 512, 1024, 896)

            def stick():
                flat = A[:, :, :].rearrange("p b n -> p (b n)")[:, 0:1280]
                L, E = sA[:, 0:1280], sB[:, 0:1280]
                for h in range(HEADS):
                    if h == 3:
                        gate_split()
                    dve.wait_ge(S["s_log"], h + 1)
                    if h:
                        dve.wait_ge(S["s_pv"], h)
                    link(ts(L, flat, SCALE, None, ALU.mult))
                    stt(out=E, in0=L, scalar=-1.0, in1=L, op0=ALU.mult, op1=ALU.max).then_inc(S["s_ab"], 1)
                    dve.wait_ge(S["s_ln"], h + 1)
                    link(stt(out=E, in0=L, scalar=0.0, in1=E, op0=ALU.max, op1=ALU.add))
                    for i in range(4):
                        e = sB[:, SB_AT[i]:SB_AT[i] + P]
                        ins = tt(e, e, c1v("before"), ALU.mult)
                    ins.then_inc(S["s_sp"], 1)
                    dve.wait_ge(S["s_cum"], h + 1)
                    link(tt(L, L, flat, ALU.subtract))
                    for i in range(4):
                        e = sA[:, SB_AT[i]:SB_AT[i] + P]
                        ins = tt(e, e, c1v("before_neg"), ALU.min)
                    ins.then_inc(S["s_d"], 1)
                    dve.wait_ge(S["s_pv"], h + 1)
                    nc.vector.tensor_copy(mix[:, :, h * P:h * P + P],
                                          A[:, 3, :].rearrange("p (j n) -> p j n", j=4)).then_inc(S["s_pvu"], 1)
                dve.wait_ge(S["s_pvu"], 4)
                gated()

            def conv_in(buf, base):
                def go():
                    param(dve, Pos.l, "conv_in")
                    for b in range(4):
                        done(b)
                        f, w = buf[:, b, :], conv[:, base + b, :]
                        link(ts(f, G[:, b, :], w[:, 3:4], w[:, 4:5], ALU.mult, ALU.add))
                        for s in (1, 2, 3):
                            ins = stt(out=f[:, s:], in0=G[:, b, 0:512 - s], scalar=w[:, 3 - s:4 - s], in1=f[:, s:],
                                      op0=ALU.mult, op1=ALU.add)
                            if s < 3:
                                link(ins)
                        ins.then_inc(g_free[b], 1)
                return go

            def per_head(ap, c=None):
                return ap.unsqueeze(2).to_broadcast([P, ap.shape[1], 64])

            def ssd():
                dve.wait_ge(S["dt_p"], 1)
                nc.vector.tensor_copy(xn[0:8, 1, 512:1024], A[0:8, 3, :]).then_inc(S["dt_row"], 1)
                unit(conv_in(fA, 0), (4, 4))
                dve.wait_ge(S["dt_t"], 1)
                u, ab = small[:, 0, :], small[:, 1, :]
                link(tt(u.rearrange("p (t h) -> p t h", h=8), A[:, 2, 0:32].rearrange("p (t h) -> p t h", h=8),
                        row[:, DT_B:DT_B + 8].unsqueeze(1).to_broadcast([P, 4, 8]), ALU.add))
                stt(out=ab, in0=u, scalar=-1.0, in1=u, op0=ALU.mult, op1=ALU.max).then_inc(S["dt_ab"], 1)
                dve.wait_ge(S["dt_ln"], 1)
                dl = small[:, 2, :]
                link(stt(out=dl, in0=u, scalar=0.0, in1=ab, op0=ALU.max, op1=ALU.add))
                dve.wait_ge(S["dt_al"], 1)
                stt(out=small[:, 3, :].rearrange("p (t h) -> p t h", h=8), in0=dl.rearrange("p (t h) -> p t h", h=8),
                    scalar=-1.0, in1=small[:, 11, 0:8].unsqueeze(1).to_broadcast([P, 4, 8]),
                    op0=ALU.mult, op1=ALU.mult).then_inc(S["dt_da"], 1)
                unit(conv_in(fB, 4), (4, 4))
                dve.wait_ge(S["dt_cs"], 1)
                nc.vector.tensor_copy(small[:, 4, :], A[:, 2, 0:32])
                link(nc.vector.tensor_copy(small[:, 5, :], A[:, 2, 32:64]))
                tt(small[:, 9, :], small[:, 5, :], small[:, 4, :], ALU.subtract).then_inc(S["dt_sub"], 1)
                for c in range(TILES):
                    dve.wait_ge(S["x_t"], c + 1)
                    nc.vector.tensor_copy(tA[:, c, :], A[:, c % 2, :]).then_inc(S["x_tc"], 1)
                    nc.vector.tensor_copy(xn[:, c // 2, (c % 2) * 256:(c % 2) * 256 + 256],
                                          A[:, 2, 0:256]).then_inc(S["x_tc"], 1)
                dve.wait_ge(S["x_tc"], 8)

                def weighted(c):
                    f2 = fA[:, c, :].rearrange("p (h n) -> p h n", n=64)
                    link(tt(f2, tA[:, c, :].rearrange("p (h n) -> p h n", n=64), per_head(dl[:, 8 * c:8 * c + 8]), ALU.mult))
                    if c < 3:
                        link(tt(sA[:, c * 512:c * 512 + 512].rearrange("p (h n) -> p h n", n=64), f2,
                                per_head(small[:, 8, 8 * c:8 * c + 8]), ALU.mult))

                def gated_squares(c):
                    m = mix[:, c, :]
                    link(tt(m, m, tB[:, c, :], ALU.mult))
                    for g in range(2):
                        v = m[:, g * 256:g * 256 + 256]
                        link(nc.vector.tensor_tensor_reduce(out=sB[:, 512 + g * 256:768 + g * 256], in0=v, in1=v, scale=1.0,
                                                            scalar=0.0, op0=ALU.mult, op1=ALU.add,
                                                            accum_out=rs_v[:, 2 * c + g:2 * c + g + 1]))
                dve.wait_ge(S["dt_ex"], 3)
                weighted(0)
                for c in range(TILES):
                    if c == 2:
                        gate_split()
                    t = sB[:, 0:1024].rearrange("p (h n) -> p h n", n=P)
                    dve.wait_ge(S["d_bc"], c + 1)
                    link(tt(t, A[:, 0:2, :].rearrange("p b (h n) -> p (b h) n", n=P),
                            heads(small[:, 4, 8 * c:8 * c + 8], 8), ALU.subtract))
                    tt(t, t, c1v("upto_neg").unsqueeze(1).to_broadcast([P, 8, P]), ALU.min).then_inc(S["d_t"], 1)
                    dve.wait_ge(S["d_e"], c + 1)
                    if c:
                        dve.wait_ge(S["d_y"], c)
                    for g in range(2):
                        ins = tt(sB[:, 1024 + g * 512:1536 + g * 512].rearrange("p (h n) -> p h n", n=P),
                                 sB[:, g * 512:g * 512 + 512].rearrange("p (h n) -> p h n", n=P),
                                 A[:, 2, g * P:g * P + P].unsqueeze(1).to_broadcast([P, 4, P]), ALU.mult)
                    ins.then_inc(S["d_sc"], 1)
                    m, part = mix[:, c, :], sB[:, 0:512]
                    dve.wait_ge(S["d_kv"], c + 1)
                    dve.wait_ge(S["d_skip"], c + 1)
                    if c:
                        dve.wait_ge(S["d_sc"], c + 1)
                        tt(part.rearrange("p (h n) -> p h n", n=64), A[:, 0, :].rearrange("p (h n) -> p h n", n=64),
                           per_head(small[:, 6, 8 * c:8 * c + 8]), ALU.mult).then_inc(S["d_in"], 1)
                    else:
                        nc.vector.sem_inc(S["d_in"], 1)
                    if c == 0:
                        nc.vector.tensor_copy(state[:, :], A[:, 1, :]).then_inc(S["d_st"], 1)
                    elif c < 3:
                        s3 = state[:, :].rearrange("p (h n) -> p h n", n=64)
                        link(tt(s3, s3, per_head(small[:, 7, 8 * c:8 * c + 8]), ALU.mult))
                        tt(state[:, :], state[:, :], A[:, 1, :], ALU.add).then_inc(S["d_st"], 1)
                    if c:
                        dve.wait_ge(S["d_in"], c + 1)
                        link(tt(m, m, part, ALU.add))
                    if c < 3:
                        weighted(c + 1)
                    else:
                        results_read()
                        for k in range(3):
                            gated_squares(k)
                    dve.wait_ge(S["d_y"], c + 1)
                    link(tt(m, m, A[:, 3, :], ALU.add))
                    nc.vector.sem_inc(S["d_yu"], 1)
                gated_squares(3)
                rsqrt(8, 1.0 / 256, EPS)
                for c in range(TILES):
                    for g in range(2):
                        o = mix[:, c, g * 256:g * 256 + 256]
                        ins = stt(out=o, in0=o, scalar=rs_r[:, 2 * c + g:2 * c + g + 1],
                                  in1=row[:, SSD_G + g * 256:SSD_G + g * 256 + 256], op0=ALU.mult, op1=ALU.mult)
                    ins.then_inc(S["tr_src"], 1)

            def end_layer(n):
                dve.wait_ge(pe_end, n)
                dve.wait_ge(act_end, n)
                dve.wait_ge(pool_end, n)
                nc.vector.sem_inc(S["layer_left"], 1)
                nc.vector.sem_clear(STAGES)
                nc.vector.memset(rs_t[:, 0:2], 0.0).then_inc(layer_open, 1)

            nc.vector.sem_inc(layer_open, 1)
            K2 = (4, 4)
            with dve.Fori(0, DEPTH) as l:
                Pos.l = l
                Pos.pair, Pos.off, Pos.end, Pos.ubase, Pos.u = l * (BLOCK1 // 2), 0, 2, l * UNITS1, 0
                N.tr, N.ch, N.rs = 0, 0, 0
                param(dve, Pos.l, "mem_in")
                param(dve, Pos.l, "row_in")

                def first_splits():
                    split()
                    split()
                rms_operand(lambda t: mem_t[:, t, :], 2, MEM_G, first_splits)
                dve.wait_ge(x_loaded, 16)

                def memory_units():
                    unit(none, K2)
                    unit(none, K2)
                rms_operand(lambda t: x[:, t, :], 4, PRE_G, memory_units)
                unit(none, K2)
                mem_attention()
                mixer_out(True, K2)
                for _ in range(3):
                    unit(none, K2)
                retention()
                mixer_out(False, K2)
                for _ in range(3):
                    unit(none, K2)
                stick()
                dve.wait_ge(S["wdt_h"], 1)
                tt(wdt_lo[:, :, :], wdt[:, :, :], wdt_hi[:, :, :].bitcast(F32), ALU.subtract).then_inc(S["wdt_l"], 1)
                mixer_out(False, K2)
                ssd()
                mixer_out(False, ())
                rsqrt(4, 1.0 / D, EPS)
                for t in range(4):
                    stt(out=y_acc[:, t, :], in0=y_acc[:, t, :], scalar=rs_r[:, t:t + 1], in1=row[:, POST_G:POST_G + D],
                        op0=ALU.mult, op1=ALU.mult).then_inc(S["y_scaled"], 1)
                nc.vector.sem_inc(S["row_used"], 1)
                for t in (2, 3):
                    dve.wait_ge(S["y_scaled"], t + 1)
                    tt(x[:, t, :], x[:, t, :], y_acc[:, t, :], ALU.add).then_inc(S["x_added"], 1)
                dve.wait_ge(S["x_added"], 4)
                assert Pos.off == BLOCK1 and Pos.u == UNITS1
                end_layer(l + 1)

            def add_half(scale, half, eps=None):
                def go():
                    for b in range(4):
                        done(b)
                        o = x[:, b, half * 512:half * 512 + 512]
                        if scale == 1.0:
                            ins = tt(o, o, G[:, b, :], ALU.add)
                        else:
                            ins = stt(out=o, in0=o, scalar=scale, in1=G[:, b, :], op0=ALU.mult, op1=ALU.add)
                        ins.then_inc(g_free[b], 1)
                        if eps is None:
                            continue
                        dve.wait_ge(g_free[b], Pos.ubase + Pos.u + 2)
                        ins = nc.vector.bn_stats(stats[:, 2 * b + half, :], o)
                        if half and b % 2:
                            link(ins)
                            for t in (b - 1, b):
                                ins = nc.vector.bn_aggr(mean_var[:, t, :],
                                                        stats[:, 2 * t:2 * t + 2, :].rearrange("p a b -> p (a b)"))
                            link(ins)
                            ts(rs_v[:, b - 1:b + 1], mean_var[:, b - 1:b + 1, 1], eps, None, ALU.add).then_inc(S["rs_in"], 1)
                return go

            def ffn(nxt):
                for n, (units, downs) in enumerate(FF_HALVES):
                    base_pair, base_off, base_u, ub = Pos.pair, Pos.off, Pos.u, Pos.ubase
                    c0 = N.ff
                    with dve.Fori(0, units) as u:
                        Pos.pair, Pos.off, Pos.end = base_pair + u, base_off, base_off
                        Pos.ubase, Pos.u = ub + u, base_u
                        split()
                        for i in range(2):
                            done(2 + i)
                            dve.wait_ge(g_free[i], ub + u + base_u + 2)
                            ins = tt(work[:, 1024 + i * 512:1536 + i * 512], work[:, i * 512:i * 512 + 512],
                                     G[:, 2 + i, :], ALU.mult)
                            ins.then_inc(g_free[2 + i], 1)
                        for i in range(2):
                            dve.wait_ge(S["ff_hi"], 2 * u + (c0 + i + 1))
                            a = bass.ds(2 * u + i, 1)
                            tt(h_lo[:, a, :].rearrange("p o n -> p (o n)"), work[:, 1024 + i * 512:1536 + i * 512],
                               h_hi[:, a, :].rearrange("p o n -> p (o n)").bitcast(F32), ALU.subtract).then_inc(S["ff_lo"], 1)
                        split()
                    Pos.pair, Pos.off, Pos.end = base_pair, base_off + 2 * units, base_off + 2 * units + 1
                    Pos.ubase, Pos.u = ub, base_u + units
                    N.ff += 2 * units
                    split(downs[2])
                    scale, eps = (2.0 * ALPHA, None) if n == 0 else (1.0, 4.0 * LN_EPS)
                    unit(add_half(scale, 0, eps), (4, 4, downs[2]))
                    unit(add_half(scale, 1, eps), (4, 4) if n == 0 else nxt)

            def layer_norm(i):
                if i == 0:
                    nc.vector.sem_inc(S["half_done"], 1)
                for a in (0, 2):
                    newton(2, a)
                    stt(out=nmx[:, 0, a:a + 2], in0=mean_var[:, a:a + 2, 0], scalar=-1.0, in1=rs_r[:, a:a + 2],
                        op0=ALU.mult, op1=ALU.mult).then_inc(S["ln_bias"], 1)
                    if a == 0:
                        param(dve, Pos.l, "ln_in", i + 1, 3)
                    for t in (a, a + 1):
                        dve.wait_ge(S["ln_std"], 4 * i + t + 1)
                        tt(x[:, t, :], x[:, t, :], lnr[:, 0, :], ALU.mult).then_inc(S["ln_gain"], 1)

            with dve.Fori(0, DEPTH) as l:
                Pos.l = l
                Pos.pair, Pos.off, Pos.end = l * (BLOCK2 // 2) + DEPTH * BLOCK1 // 2, 0, 2
                Pos.ubase, Pos.u = l * UNITS2 + DEPTH * UNITS1, 0
                N.tr, N.ch, N.rs, N.ff, N.half = 0, 0, 0, 0, 0
                nc.vector.sem_inc(S["tr_src"], 4)
                split()
                split()
                tr_lo(xT_hi, xT_lo, 4, 2)
                ffn(K2)
                layer_norm(0)
                tr_lo(xT_hi, xT_lo, 4, 2)
                dve.wait_ge(S["tr_lo"], N.tr)
                nc.vector.tensor_copy(y2_lo[:, :, :].rearrange("p k (c r) -> p k c r", r=NA_R),
                                      xT_lo[:, :, :].bitcast(F32).rearrange("p k (r c) -> p k c r", c=GRID_W)
                                      ).then_inc(S["perm_lo"], 1)
                param(dve, Pos.l, "shift_in", 16, 16)
                dve.wait_ge(const2_in, 16)
                masks = c2v("masks").rearrange("p (m c r) -> p m c r", m=5, c=16)
                for h in range(NA_H):
                    for m, off in enumerate((16, 0, 16, 32, 16)):
                        ins = tt(bm[:, h, m, :].rearrange("p (c r) -> p c r", c=16),
                                 shifted[:, h, :, off:off + 16].rearrange("p k e -> p e k"), masks[:, m], ALU.add)
                ins.then_inc(S["b_bm"], 1)
                unit(none, K2)

                def conv_z():
                    for b in range(2):
                        done(2 + b)
                        dve.wait_ge(g_free[b], Pos.ubase + Pos.u + 2)
                        z = work[:, 2048 + b * 512:2560 + b * 512]
                        tt(z, z, G[:, 2 + b, :], ALU.mult).then_inc(g_free[2 + b], 1)
                unit(conv_z, K2)
                param(dve, Pos.l, "col2_in")
                results_read()
                for b in range(2):
                    z = work[:, 2048 + b * 512:2560 + b * 512]
                    o = conv_out[:, b * 512:b * 512 + 512]
                    gb = work[:, 1024 + b * 512:1536 + b * 512]
                    link(ts(o, z, col2[:, b, 1:2], None, ALU.mult))
                    link(stt(out=o[:, 1:], in0=z[:, 0:511], scalar=col2[:, b, 0:1], in1=o[:, 1:], op0=ALU.mult, op1=ALU.add))
                    link(stt(out=o[:, 0:511], in0=z[:, 1:], scalar=col2[:, b, 2:3], in1=o[:, 0:511], op0=ALU.mult, op1=ALU.add))
                    tt(gb, gb, o, ALU.mult).then_inc(S["z_y"], 1)
                for _ in range(3):
                    unit(none, K2)
                for ch in range(2):
                    dve.wait_ge(S["y2h"], ch + 1)
                    stt(out=y2_lo[:, ch, :], in0=A[:, 2 + ch, :], scalar=col2[:, ch, 3:4], in1=y2_hi[:, ch, :].bitcast(F32),
                        op0=ALU.mult, op1=ALU.subtract).then_inc(S["y2l"], 1)
                for ch in range(2):
                    dve.wait_ge(S["y2h"], ch + 3)
                    tt(y2_lo[:, 2 + ch, :], work[:, 1024 + ch * 512:1536 + ch * 512], y2_hi[:, 2 + ch, :].bitcast(F32),
                       ALU.subtract).then_inc(S["y2l"], 1)
                combos = [(h, j) for h in range(NA_H) for j in range(4)]

                def biased(i):
                    h, j = combos[i]
                    nb = min(4, j + 2) - max(0, j - 1)
                    n = nb * P
                    dve.wait_ge(S["n_s"], i + 1)
                    if i == 0:
                        dve.wait_ge(S["y2l"], 4)
                        dve.wait_ge(S["y2h"], 4)
                    if i >= 3:
                        dve.wait_ge(S["n_t"], i - 2)
                    w = p_slot(i)[:, 0:n]
                    b = {0: bm[:, h, 0:4:3, :], 1: bm[:, h, 1:4, :], 2: bm[:, h, 1:4, :], 3: bm[:, h, 1:5:3, :]}[j]
                    link(stt(out=w.rearrange("p (b n) -> p b n", n=P),
                             in0=A[:, i % 2, 0:n].rearrange("p (b n) -> p b n", n=P), scalar=NA_D ** -0.5, in1=b,
                             op0=ALU.mult, op1=ALU.add))
                    link(nc.vector.tensor_reduce(nmx[:, 2, i:i + 1], w, AX.X, ALU.max))
                    ts(nmx[:, 0, i:i + 1], nmx[:, 2, i:i + 1], -1.0, None, ALU.mult).then_inc(S["n_m"], 1)

                def normed(i):
                    h, j = combos[i]
                    n = (min(4, j + 2) - max(0, j - 1)) * P
                    dve.wait_ge(S["n_p"], i + 1)
                    link(nc.vector.reciprocal(nmx[:, 3, i:i + 1], nmx[:, 1, i:i + 1]))
                    w = p_slot(i)[:, 0:n]
                    ts(w, w, nmx[:, 3, i:i + 1], None, ALU.mult).then_inc(S["n_pn"], 1)

                def pair_out(i):
                    dve.wait_ge(S["n_oh"], i + 1)
                    tt(y2_lo[:, 4 + i, :].rearrange("p (r c) -> p c r", c=GRID_W), A[:, 3, :].rearrange("p (c r) -> p c r", r=NA_R),
                       y2_hi[:, 4 + i, :].bitcast(F32).rearrange("p (r c) -> p c r", c=GRID_W),
                       ALU.subtract).then_inc(S["n_ol"], 1)

                for i in range(len(combos) + 3):
                    if i < len(combos):
                        biased(i)
                    if 1 <= i <= len(combos):
                        normed(i - 1)
                    if i >= 3 and (i - 3) % 8 == 7:
                        pair_out((i - 3) // 8)
                unit(add_half(ALPHA, 0, LN_EPS), K2)
                unit(add_half(ALPHA, 1, LN_EPS), K2)
                layer_norm(1)
                tr_lo(xT_hi, xT_lo, 4, 2)
                ffn(())
                layer_norm(2)
                assert Pos.off == BLOCK2 and Pos.u == UNITS2
                end_layer(l + 1 + DEPTH)

        @block.gpsimd
        def _(pool):
            def load_mem():
                pool.dma_start(mem_t,
                               mem_in.rearrange("a (t p) d -> p (a t) d", p=P)).then_inc(landed["mem_in"], 16)
            load_mem()
            with pool.Fori(0, DEPTH) as l:
                pool.wait_ge(layer_open, l + 1)
                pool.sem_inc(S["layer_begun"], 1)
                pool.dma_start(row[:, :], rows1[bass.ds(l, 1)].to_broadcast([P, ROW1])).then_inc(landed["row_in"], 16)
                pool.dma_start(conv[:, :, :].rearrange("p a b -> p (a b)"),
                               conv1[bass.ds(l, 1)].rearrange("o p n -> (o p) n")).then_inc(landed["conv_in"], 16)
                pool.dma_start(wdt[:, :, :].rearrange("p a b -> p (a b)"),
                               w_dt[bass.ds(l, 1)].rearrange("o p n -> (o p) n")).then_inc(landed["wdt_in"], 16)
                param(pool, l, "conv_in")
                param(pool, l, "wdt_in")
                param(pool, l, "row_in")
                for c in range(TILES):
                    pool.wait_ge(S["x_tc"], 2 * c + 1)
                    nc.gpsimd.tensor_tensor(mix[:, c, :].rearrange("p (h n) -> p h n", n=64),
                                            tA[:, c, :].rearrange("p (h n) -> p h n", n=64),
                                            row[:, D_SKIP:D_SKIP + 8].unsqueeze(2).to_broadcast([P, 8, 64]),
                                            ALU.mult).then_inc(S["d_skip"], 1)
                pool.wait_ge(S["d_y"], 4)
                load_mem()
                for t in range(2):
                    pool.wait_ge(S["y_scaled"], t + 1)
                    nc.gpsimd.tensor_tensor(x[:, t, :], x[:, t, :], y_acc[:, t, :], ALU.add).then_inc(S["x_added"], 1)
                pool.wait_ge(S["row_used"], 1)
                param(pool, l + 1, "mem_in")
                pool.sem_inc(pool_end, 1)
            pool.wait_ge(layer_open, DEPTH + 1)
            pool.dma_start(cst2[:, :], const2).then_inc(const2_in, 16)
            with pool.Fori(0, DEPTH) as l:
                pool.wait_ge(layer_open, l + 1 + DEPTH)
                pool.sem_inc(S["layer_begun"], 1)
                def load_ln(i):
                    pool.dma_start(lnr[:, :, :].rearrange("p a b -> p (a b)"),
                                   ln_rows[bass.ds(l, 1), i, :].to_broadcast([P, 2 * D])).then_inc(landed["ln_in"], 16)

                def add_bias(i):
                    param(pool, l, "ln_in", i + 1, 3)
                    for t in range(TILES):
                        pool.wait_ge(S["ln_gain"], 4 * i + t + 1)
                        nc.gpsimd.tensor_tensor(x[:, t, :], x[:, t, :], lnr[:, 1, :], ALU.add).then_inc(S["tr_src"], 1)
                    pool.wait_ge(S["tr_src"], 4 * (i + 2))
                load_ln(0)
                pool.dma_start(poolw[:, :, :].rearrange("p a b -> p (a b)"),
                               pool_w[bass.ds(l, 1)].rearrange("o p n -> (o p) n")).then_inc(landed["poolw_in"], 16)
                pool.dma_start(col2[:, :, :].rearrange("p a b -> p (a b)"),
                               cols2[bass.ds(l, 1)].rearrange("o p n -> (o p) n")).then_inc(landed["col2_in"], 16)
                pool.wait_ge(S["half_done"], 1)
                pool.dma_start(work[0:15, 0:248], rpb[bass.ds(l, 1)].rearrange("o p n -> (o p) n")).then_inc(landed["rpb_in"], 16)
                pool.dma_start(sel[0:15, :], sel_in).then_inc(landed["sel_in"], 16)
                add_bias(0)
                pool.memset(qkv[:, 0:3072], 0.0).then_inc(S["b_raw"], 1)
                pool.wait_ge(S["b_raw"], 1)
                pool.wait_ge(S["b_gc"], NA_R)
                for c in range(16):
                    pool.dma_start(shifted[8 * c:8 * c + 8, :, :, c + 1:c + 32],
                                   raw_rows[8 * c:8 * c + 8, :].rearrange("p (h k e) -> p h k e", h=8, k=8)
                                   ).then_inc(landed["shift_in"], 16)
                param(pool, l, "shift_in", 16, 16)
                pool.sem_inc(S["layer_begun"], 1)
                pool.wait_ge(S["y2l"], 4)
                load_ln(1)
                add_bias(1)
                load_ln(2)
                add_bias(2)
                pool.sem_inc(pool_end, 1)
            pool.wait_ge(layer_open, 2 * DEPTH + 1)
            pool.dma_start(out.rearrange("a (t p) d -> p (a t) d", p=P), x[:, :, :]).then_inc(out_done, 16)
            pool.wait_ge(out_done, 16)


def weight_stream(v):
    out = []

    def add(w, col, rows=None):
        r0, r1 = rows or (0, w.shape[0])
        for r in range(r0, r1, KB * P):
            b = w[r:min(r + KB * P, r1), col:col + BC]
            b = b.reshape(-1, P, BC).transpose(1, 0, 2)
            if b.shape[1] < KB:
                b = np.concatenate([b, np.zeros((P, KB - b.shape[1], BC), b.dtype)], axis=1)
            out.append(b.reshape(P, KB * BC))

    for l in range(DEPTH):
        w, wo, kv = v["w_in"][l], v["w_out"][l], v["w_mem_kv"][l]

        def mixer(cols, first_row):
            for c in cols:
                add(w, c)
            for half in range(2):
                add(wo, half * BC, (first_row, first_row + GW))
        add(kv, 0)
        add(kv, GW)
        mixer((5640, 6152), 1536)
        mixer((0, 512, 1024, 1536), 0)
        mixer((3592, 4104, 4616, 5128), 1024)
        mixer((2048, 2560, 3072), 512)
    for l in range(DEPTH):
        def ffn(name):
            g, u, d = (v[f"{name}_w_{p}_2"][l] for p in ("gate", "up", "down"))
            gu = np.stack([g.reshape(D, 11, 256), u.reshape(D, 11, 256)], axis=2).reshape(D, -1)
            at = 0
            for units, downs in FF_HALVES:
                for i in range(at, at + units):
                    add(gu, i * BC)
                for half in range(2):
                    add(d, half * BC, (at * 256, (at + units) * 256))
                at += units
        ffn("ffn1")
        for c in range(5):
            add(v["w_in_2"][l], c * BC)
        for half in range(2):
            add(v["w_out_2"][l], half * BC)
        ffn("ffn2")
    return np.stack(out)


def kernel(**inputs):
    import concourse.bacc as bacc
    from concourse.bass_utils import run_bass_kernel_spmd

    v = {k: np.ascontiguousarray(a) for k, a in inputs.items()}
    f = np.float32
    c0, c1, c2, c3 = (np.concatenate([a.astype(f) for a in c.values()], axis=1) for c in constants())
    rows1 = np.concatenate([v["pre_norm_g"], v["post_norm_g"], v["mem_norm_g"], v["ssd_norm_g"], v["dt_bias"],
                            v["a_log"], v["d_skip"]], axis=1)
    conv1 = np.concatenate([v["conv_w"], v["conv_b"][:, None]], axis=1).reshape(DEPTH, 5, 8, P)
    conv1 = conv1.transpose(0, 3, 2, 1).reshape(DEPTH, P, 40)
    w_dt = v["w_in"][:, :, 3584:3592].reshape(DEPTH, 8, P, 8).transpose(0, 2, 1, 3).reshape(DEPTH, P, 64)
    ln_rows = np.stack([v["ln_g_2"], v["ln_b_2"]], axis=2).reshape(DEPTH, 3, 2 * D)
    pool_w = np.zeros((DEPTH, P, 2, P), f)
    for g in range(4):
        a = 64 * (g % 2)
        pool_w[:, a:a + 64, g // 2, a:a + 64] = v["pool_w_2"][:, g]
    cols2 = np.concatenate([v["conv_w_2"], v["pool_scale_2"][:, None]], axis=1).reshape(DEPTH, 4, 2, P)
    cols2 = cols2.transpose(0, 3, 2, 1).reshape(DEPTH, P, 8)
    rpb = v["rpb_2"].transpose(0, 2, 1, 3).reshape(DEPTH, 15, NA_H * 31)

    arrays = {"in_x": v["x"], "in_mem": v["mem"], "in_stream": weight_stream(v), "in_const0": c0, "in_const1": c1,
              "in_const2": c2, "in_rows1": rows1, "in_conv1": conv1, "in_w_dt": w_dt, "in_ln_rows": ln_rows,
              "in_pool_w": pool_w.reshape(DEPTH, P, 2 * P), "in_cols2": cols2, "in_rpb": rpb, "in_sel": c3}
    arrays = {k: np.ascontiguousarray(a) for k, a in arrays.items()}
    nc = bacc.Bacc("TRN2", target_bir_lowering=False, num_devices=1)
    args = [nc.dram_tensor(k, a.shape, mybir.dt.from_np(a.dtype), kind="ExternalInput").ap() for k, a in arrays.items()]
    out = nc.dram_tensor("out_0", (1, SEQ, D), F32, kind="ExternalOutput").ap()
    build(nc, *args, out)
    r = run_bass_kernel_spmd(nc, [arrays], core_ids=[0])
    return r.results[0]["out_0"]
```

```python
from contextlib import ExitStack

import numpy as np

import concourse.bass as bass
from concourse import mybir

F32 = mybir.dt.float32
F32R = mybir.dt.float32r
ALU = mybir.AluOpType
ACT = mybir.ActivationFunctionType
AX = mybir.AxisListType

P = 128
DEPTH = 2
SEQ = 512
D = 1024
TILES = SEQ // P
DCH = D // P
N_MEM = 256
GW = 512
HEADS = 4
HD = 128
SSD_H = 8
D_FF = 2816
EPS = 1e-6
LN_EPS = 1e-5
ALPHA = (2.0 * DEPTH) ** 0.25
SCALE = HD ** -0.5
NEG = -1e30
LN_EXP = "natural_log_exp_and_others"

KB = 4
BC = 512
BLOCK1 = 38
BLOCK2 = 82
UNITS1 = 23
C_H_STEPS = range(1, 33)
UNITS2 = 2 * (11 + 4) + 5 + 2
FF_HALVES = ((6, (4, 4, 4)), (5, (4, 4, 2)))

NA_H = 8
NA_D = 64
GRID_W = 64
NA_R = 8
CONV2 = 256
LOG_G = np.log(1.0 - 2.0 ** (-5.0 - np.arange(HEADS, dtype=np.float32))).astype(np.float32)
RET_DECAY = [float(x) for x in np.exp(np.float32(P) * LOG_G)]

PRE_G, POST_G, MEM_G, SSD_G, DT_B, A_LOG, D_SKIP = 0, 1024, 2048, 3072, 3584, 3592, 3600
ROW1 = 3608


def constants():
    f = np.float32
    i = np.arange(P)
    inv = f(10000.0) ** (-np.arange(0, HD, 2, dtype=f) / f(HD))
    ang = np.arange(SEQ, dtype=f)[:, None] * inv[None, :].astype(f)
    cos, sin = np.cos(ang).T, np.sin(ang).T
    rot = np.zeros((P, P), f)
    rot[i[64:], i[:64]] = -1.0
    rot[i[:64], i[64:]] = 1.0
    rel = (i[None, :] - i[:, None]).astype(f)
    intra = np.stack([np.where(rel >= 0, np.exp(np.maximum(rel, 0) * g), 0) * f(SCALE) for g in LOG_G], 1)
    xi = np.stack([np.broadcast_to(np.exp((i + 1).astype(f) * g), (P, P)) for g in LOG_G], 1)
    zeta = np.stack([np.exp((P - 1 - i).astype(f) * g) * f(SCALE) for g in LOG_G], 1)
    first = {
        "cos": np.concatenate([cos, cos]), "sin": np.concatenate([sin, sin]), "rot": rot,
        "upto": (i[:, None] <= i[None, :]), "minus_from": -1.0 * (i[:, None] >= i[None, :]), "minus_ones": -np.ones((P, P)),
        "upto_neg": np.where(i[:, None] <= i[None, :], 0, NEG), "before": (i[:, None] < i[None, :]),
        "before_neg": np.where(i[:, None] < i[None, :], 0, NEG),
        "intra": intra.reshape(P, -1), "xi": xi.reshape(P, -1), "zeta": zeta,
    }
    cl = i // NA_R
    def mask(qb, kb):
        c, k = 16 * qb + cl[:, None], 16 * kb + cl[None, :]
        lo = np.clip(c - 8, 0, GRID_W - 16)
        return np.where((k >= lo) & (k < lo + 16), 0, NEG)
    masks = np.stack([mask(0, 0), mask(2, 1), mask(1, 1), mask(1, 2), mask(3, 3)], 1)
    assert (mask(0, 1) == mask(1, 2)).all() and (mask(3, 2) == mask(2, 1)).all() and (mask(2, 2) == mask(1, 1)).all()
    sel = np.zeros((P, NA_R, P))
    for k in range(NA_R):
        sel[k - i % NA_R + 7, k, i] = 1.0
    pool = np.zeros((P, 4, 4, 144))
    t = np.arange(SEQ)
    for g, w in enumerate((2, 4, 8, 16)):
        lo, hi = np.clip(t - w // 2, 0, SEQ), np.clip(t - w // 2 + w, 0, SEQ)
        m = ((t[:, None] >= lo[None]) & (t[:, None] < hi[None])) / (hi - lo)[None].astype(f) - np.eye(SEQ)
        for c in range(4):
            for col in range(144):
                tt = 128 * c + col - 8
                if 0 <= tt < SEQ:
                    pool[:, g, c, col] = m[128 * c:128 * c + 128, tt]
    second = {"masks": masks.reshape(P, -1), "pool": pool.reshape(P, -1)}
    return {"ident": np.eye(P)}, first, second, {"sel": sel.reshape(P, -1)[:15]}


def columns(parts):
    at, out = 0, {}
    for name, a in parts.items():
        out[name] = (at, at + a.shape[1])
        at += a.shape[1]
    return out, at


def build(nc, x_in, mem_in, stream, const0, const1, const2, rows1, conv1, w_dt, ln_rows, pool_w, cols2, rpb, sel_in, out):
    c0, c1, c2, _ = constants()
    _, N0 = columns(c0)
    at1, N1 = columns(c1)
    at2, N2 = columns(c2)

    ctx = ExitStack()
    with ctx:
        def sb(name, shape, dt=F32, on=ctx):
            return on.enter_context(nc.sbuf_tensor(name, shape, dt))

        def sem(name):
            return ctx.enter_context(nc.semaphore(name))

        ident = sb("ident", [P, N0])
        x = sb("x", [P, TILES, D])
        xT_hi = sb("xT_hi", [P, DCH, SEQ], F32R)
        xT_lo = sb("xT_lo", [P, DCH, SEQ], F32R)
        raw = sb("raw", [P, 2, KB, BC])
        w_hi = sb("w_hi", [P, 2, KB, BC], F32R)
        w_lo = sb("w_lo", [P, 2, KB, BC], F32R)
        rs_v = sb("rs_v", [P, 16])
        rs_r = sb("rs_r", [P, 16])
        rs_t = sb("rs_t", [P, 16])
        stats = sb("stats", [P, 16, 6])
        mean_var = sb("mean_var", [P, 16, 2])

        one = ExitStack()
        cst = sb("cst", [P, N1], on=one)
        row = sb("row", [P, ROW1], on=one)
        conv = sb("conv", [P, 8, 5], on=one)
        wdt = sb("wdt", [P, 8, 8], on=one)
        wdt_hi = sb("wdt_hi", [P, 8, 8], F32R, on=one)
        wdt_lo = sb("wdt_lo", [P, 8, 8], F32R, on=one)
        fA = sb("fA", [P, 4, 512], on=one)
        fB = sb("fB", [P, 4, 512], on=one)
        tA = sb("tA", [P, 4, 512], on=one)
        tB = sb("tB", [P, 4, 512], on=one)
        mix = sb("mix", [P, 4, 512], on=one)
        y_acc = sb("y_acc", [P, TILES, D], on=one)
        xn = sb("xn", [P, 2, 1024], on=one)
        state = sb("state", [P, 512], on=one)
        mk = y_acc[:, 0, :].rearrange("p (h n) -> p h n", h=4)
        mem_t = fA[:, :, :].rearrange("p c n -> p (c n)").rearrange("p (t d) -> p t d", t=2)
        small = sb("small", [P, 12, 32], on=one)
        with ExitStack() as over:
            sA = sb("sA", [P, 2048], on=over)
            sB = sb("sB", [P, 2048], on=over)
        mixT_hi = sb("mixT_hi", [P, 4, SEQ], F32R, on=one)
        mixT_lo = sb("mixT_lo", [P, 4, SEQ], F32R, on=one)
        one.close()

        two = ExitStack()
        lnr = sb("lnr", [P, 2, D], on=two)
        cst2 = sb("cst2", [P, N2], on=two)
        work = sb("work", [P, 3072], on=two)
        poolw = sb("poolw", [P, 2, P], on=two)
        col2 = sb("col2", [P, 2, 4], on=two)
        nmx = sb("nmx", [P, 4, 32], on=two)
        with ExitStack() as over:
            qkv = sb("qkv", [P, 3 * 4 * SEQ], on=over)
            bm = sb("bm", [P, NA_H, 5, P], on=over)
            y2_hi = sb("y2_hi", [P, 8, SEQ], F32R, on=over)
            y2_lo = sb("y2_lo", [P, 8, SEQ], F32R, on=over)
        h_hi = sb("h_hi", [P, 12, SEQ], F32R, on=two)
        h_lo = sb("h_lo", [P, 12, SEQ], F32R, on=two)
        two.close()

        qp, kp, vp = (qkv[:, i * 2048:i * 2048 + 2048].rearrange("p (c t) -> p c t", c=4) for i in range(3))
        sel = work[:, 2048:3072]
        conv_out = lnr[:, 0, :]
        shifted = qkv[:, 0:3072].rearrange("p (h k e) -> p h k e", h=8, k=8)
        raw_rows = work[:, 0:1984]
        rpb_rows = poolw[:, :, :].rearrange("p a b -> p (a b)")

        gate_b = work[:, 1920:2944]

        def p_slot(i):
            return work[:, (i % 3) * 384:(i % 3) * 384 + 384]

        def pt_slot(i):
            return work[:, (3 + i % 2) * 384:(3 + i % 2) * 384 + 384]

        def c1v(name):
            a, b = at1[name]
            return cst[:, a:b]

        def c2v(name):
            a, b = at2[name]
            return cst2[:, a:b]

        I = ident[:, 0:P]
        G = ctx.enter_context(nc.psum_tensor("G", [P, 4, 512], F32))
        A = ctx.enter_context(nc.psum_tensor("A", [P, 4, 512], F32))

        raw_in = [sem("raw_in0"), sem("raw_in1")]
        hi_done = sem("hi_done")
        lo_done = sem("lo_done")
        blk_used = sem("blk_used")
        g_done = [sem(f"g_done{i}") for i in range(3)]
        g_free = [sem(f"g_free{i}") for i in range(4)]
        pe_end, act_end, pool_end = sem("pe_end"), sem("act_end"), sem("pool_end")
        layer_open = sem("layer_open")
        const_in, x_loaded, out_done = sem("const_in"), sem("x_loaded"), sem("out_done")
        const1_in = sem("const1_in")
        const2_in = sem("const2_in")
        stage = {}

        def st(name):
            if name not in stage:
                stage[name] = sem(name)
            return stage[name]

        landed = {n: sem(n) for n in "row_in mem_g_in conv_in wdt_in mem_in ln_in poolw_in col2_in rpb_in sel_in shift_in".split()}

        def param(eng, l, name, k=1, per=1):
            eng.wait_ge(landed[name], l * (16 * per) + 16 * k)

        for n in ("layer_begun layer_left perm_hi perm_lo row_used ln_bias ln_std ln_gain ln_even ln_odd y_scaled x_added rs_in rs_out act_chain dve_chain "
                  "tr_src tr_done tr_hi tr_lo "
                  "ff_hi ff_lo half_done "
                  "m_log m_nb m_p m_pt m_ptc m_o m_y "
                  "rot_done rot_used rot_cos ret_ready rz_t rz_used r_s r_sm r_y r_kv r_yu r_st "
                  "s_log s_ln s_sp s_cum s_w s_pv s_pvu "
                  "conv_silu x_t x_tc dt_p dt_ab dt_ln dt_da dt_cs dt_sub dt_ex dt_al wdt_h wdt_l "
                  "dt_row dt_t d_skip d_in d_kv d_bc d_t d_e d_sc d_y d_yu d_st "
                  "b_g b_gc b_bm b_raw p_t p_tc p_y z_y y2h y2l n_s n_m n_p n_pn n_t n_tc n_o n_oh n_ol").split():
            st(n)
        S = stage
        nums = [s.num for s in S.values()]
        STAGES = range(nums[0], nums[-1] + 1)
        assert nums == list(STAGES)

        def bcast(ap, shape):
            return ap.to_broadcast(shape)

        block = ctx.enter_context(nc.Block())

        def perm_view(ap):
            return ap.rearrange("p (r c) -> p c r", c=GRID_W)

        @block.sync
        def _(sp):
            pairs = DEPTH * (BLOCK1 + BLOCK2) // 2
            with sp.Fori(0, pairs) as m:
                for s in range(2):
                    sp.wait_ge(lo_done, 2 * m + s + 1)
                    sp.dma_start(raw[:, s, :, :].rearrange("p k n -> p (k n)"),
                                 stream[bass.ds(2 * m + s, 1)].rearrange("o p n -> (o p) n")).then_inc(raw_in[s], 16)

        @block.tensor
        def _(pe):
            mm = nc.tensor.matmul
            pe.sem_inc(blk_used, 2)

            class Pos:
                pair, off, ubase, u = 0, 0, 0, 0

            def gemm_steps(kbs, jobs, operand_ready=None, fine=False):
                c = 0
                for b, nk in enumerate(kbs):
                    s = Pos.off % 2
                    pe.wait_ge(lo_done, 2 * Pos.pair + Pos.off + 3)
                    if operand_ready:
                        operand_ready(c + nk)
                    for n, (bank, emits) in enumerate(jobs):
                        if b == 0:
                            pe.wait_ge(g_free[bank], Pos.ubase + Pos.u + 1)
                        for e, emit in enumerate(emits):
                            for k in range(nk):
                                last = emit(c + k, w_hi[:, s, k, :], w_lo[:, s, k, :],
                                            b == 0 and k == 0 and e == 0, b == len(kbs) - 1 and k == nk - 1)
                                if fine and k < nk - 1:
                                    yield
                        if n == 3:
                            last.then_inc(blk_used, 1)
                        elif b == len(kbs) - 1:
                            last.then_inc(g_done[bank], 1)
                        if n == len(jobs) - 1:
                            Pos.off += 1
                            c += nk
                            if b == len(kbs) - 1:
                                Pos.u += 1
                        yield

            def gemm(kbs, jobs, operand_ready=None):
                for _ in gemm_steps(kbs, jobs, operand_ready):
                    pass

            def results_read():
                for bank in range(4):
                    pe.wait_ge(g_free[bank], Pos.ubase + Pos.u + 1)

            def feat(bank, hi, lo, col, n=SEQ, dst=None):
                o = G[:, bank, 0:n]

                def emit(c, wh, wl, start, stop):
                    a = wh[:, col:col + P]
                    mm(o, a, hi[:, c, 0:n], start=start, stop=False)
                    mm(o, a, lo[:, c, 0:n], start=False, stop=False)
                    return mm(o, wl[:, col:col + P], hi[:, c, 0:n], start=False, stop=stop)
                return emit

            def tok(bank, hi, lo, tile, col=0, n=BC, at=0, own_start=True):
                o = G[:, bank, at:at + n]

                def emit(c, wh, wl, start, stop):
                    a, b = hi[:, c, tile * P:tile * P + P], lo[:, c, tile * P:tile * P + P]
                    k = dict(skip_group_check=True) if n < BC else {}
                    mm(o, a, wh[:, col:col + n], start=start and own_start, stop=False, **k)
                    mm(o, a, wl[:, col:col + n], start=False, stop=False, **k)
                    return mm(o, b, wh[:, col:col + n], start=False, stop=stop, **k)
                return emit

            def feat4(n=SEQ):
                gemm((4, 4), [(o, [feat(o, xT_hi, xT_lo, o * P, n)]) for o in range(4)])

            def tok4(kbs=(4, 4), hi=xT_hi, lo=xT_lo):
                gemm(kbs, [(o, [tok(o, hi, lo, o)]) for o in range(4)])

            def token_steps():
                return gemm_steps((4, 4), [(o, [tok(o, xT_hi, xT_lo, o)]) for o in range(4)])

            def advance(steps, n):
                for _ in range(n):
                    next(steps)

            def finished(steps):
                assert next(steps, "end") == "end"

            class N:
                tr = 0

            def transposes(src, tiles, groups, norm=None):
                for t in range(tiles):
                    for g in range(groups):
                        if N.tr >= 4:
                            pe.wait_ge(S["tr_lo"], N.tr - 3)
                        if norm is not None:
                            pe.wait_ge(S["ln_odd" if t % 2 else "ln_even"], 2 * norm + t // 2 + 1)
                        else:
                            pe.wait_ge(S["tr_src"], N.src + t + 1)
                        for c in range(4):
                            last = nc.tensor.transpose(A[:, N.tr % 4, c * P:c * P + P],
                                                       src(t)[:, (4 * g + c) * P:(4 * g + c + 1) * P], I)
                        last.then_inc(S["tr_done"], 1)
                        N.tr += 1
                N.src += tiles

            def mem_attention():
                results_read()
                gate = token_steps()
                for q in range(TILES):
                    if q:
                        pe.wait_ge(S["m_y"], q)
                    for h in range(HEADS):
                        last = mm(A[:, h // 2, (h % 2) * 256:(h % 2) * 256 + 256], fA[:, h, q * P:q * P + P],
                                  mk[:, h, :], start=True, stop=True)
                    last.then_inc(S["m_log"], 1)
                    advance(gate, (2, 1, 1, 1)[q])
                    pe.wait_ge(S["m_p"], 4 * (q + 1))
                    pm = sA[:, 0:1024]
                    for i in range(8):
                        last = nc.tensor.transpose(A[:, 2 + i // 4, (i % 4) * P:(i % 4 + 1) * P],
                                                   pm[:, i * P:i * P + P], I)
                    last.then_inc(S["m_pt"], 1)
                    advance(gate, (1, 1, 1, 0)[q])
                    pe.wait_ge(S["m_ptc"], q + 1)
                    for h in range(HEADS):
                        for k in range(2):
                            last = mm(A[:, 0, h * P:h * P + P], sB[:, (2 * h + k) * P:(2 * h + k + 1) * P],
                                      tA[:, k, h * P:h * P + P], start=(k == 0), stop=(k == 1))
                    last.then_inc(S["m_o"], 1)
                finished(gate)

            def retention():
                results_read()
                pe.wait_ge(const1_in, 16)
                gate = token_steps()
                for i in range(8):
                    if i >= 4:
                        advance(gate, 1)
                        pe.wait_ge(S["rot_used"], i - 3)
                    mm(A[:, i % 4, :], c1v("rot"), (fA if i < 4 else fB)[:, i % 4, :],
                       start=True, stop=True).then_inc(S["rot_done"], 1)
                pe.wait_ge(S["ret_ready"], 1)
                for c in range(3):
                    for h in range(HEADS):
                        last = nc.tensor.transpose(A[:, c, h * P:h * P + P], fB[:, h, c * P:c * P + P], I)
                    last.then_inc(S["rz_t"], 1)
                advance(gate, 1)
                pe.wait_ge(S["rz_used"], 3)
                for c in range(TILES):
                    for h in range(HEADS):
                        last = mm(A[:, 0, h * P:h * P + P], fB[:, h, c * P:c * P + P], fA[:, h, c * P:c * P + P],
                                  start=True, stop=True)
                    last.then_inc(S["r_s"], 1)
                    if c < 3:
                        if c:
                            pe.wait_ge(S["r_st"], 4 * c)
                        for h in range(HEADS):
                            last = mm(A[:, 2, h * P:h * P + P], sB[:, c * 512 + h * P:c * 512 + h * P + P],
                                      tA[:, c, h * P:h * P + P], start=True, stop=True)
                        last.then_inc(S["r_kv"], 1)
                    pe.wait_ge(S["r_sm"], c + 1)
                    if c:
                        pe.wait_ge(S["r_yu"], c)
                        pe.wait_ge(S["r_st"], 4 * c)
                    for h in range(HEADS):
                        last = mm(A[:, 1, h * P:h * P + P], xn[:, 0, h * P:h * P + P], tA[:, c, h * P:h * P + P],
                                  start=True, stop=(c == 0))
                        if c:
                            last = mm(A[:, 1, h * P:h * P + P], sA[:, h * 512 + c * P:h * 512 + c * P + P],
                                      state[:, h * P:h * P + P], start=False, stop=True)
                    last.then_inc(S["r_y"], 1)
                advance(gate, 3)
                finished(gate)

            SB_AT = (0, 512, 1024, 896)

            def stick():
                results_read()
                values, gate = token_steps(), token_steps()
                flat = A[:, :, :].rearrange("p b n -> p (b n)")
                for h in range(HEADS):
                    if h:
                        pe.wait_ge(S["s_w"], h)
                    for i in range(4):
                        n = (4 - i) * P
                        last = mm(flat[:, SB_AT[i]:SB_AT[i] + n], fB[:, h, i * P:i * P + P], fA[:, h, i * P:SEQ],
                                  start=(i != 3), stop=True, skip_group_check=True)
                    last.then_inc(S["s_log"], 1)
                    advance(values, (5, 0, 0, 0)[h])
                    advance(gate, (0, 2, 2, 1)[h])
                    pe.wait_ge(S["s_sp"], h + 1)
                    for i in range(4):
                        for k in range(i, 4):
                            w, n = (k - i) * P, (4 - k) * P
                            mm(flat[:, SB_AT[i] + w:SB_AT[i] + w + n], c1v("minus_from" if k == i else "minus_ones"),
                               sB[:, SB_AT[k]:SB_AT[k] + n], start=False, stop=False, skip_group_check=True)
                        last = mm(flat[:, SB_AT[i]:SB_AT[i] + P], I, c1v("before_neg"), start=False, stop=True,
                                  skip_group_check=True)
                    last.then_inc(S["s_cum"], 1)
                    advance(values, (3, 0, 0, 0)[h])
                    advance(gate, (0, 1, 1, 1)[h])
                    if h == 0:
                        finished(values)
                        results_read()
                    pe.wait_ge(S["s_w"], h + 1)
                    if h:
                        pe.wait_ge(S["s_pvu"], h)
                    for j in range(4):
                        for i in range(j + 1):
                            last = mm(A[:, 3, j * P:j * P + P], sA[:, SB_AT[i] + (j - i) * P:SB_AT[i] + (j - i + 1) * P],
                                      tA[:, i, h * P:h * P + P], start=(i == 0), stop=(i == j))
                    last.then_inc(S["s_pv"], 1)
                finished(gate)

            def ssd():
                pe.wait_ge(S["wdt_l"], 1)
                for k in range(8):
                    o = A[0:8, 3, :]
                    mm(o, wdt_hi[:, k, :], xT_hi[:, k, :], start=(k == 0), stop=False)
                    mm(o, wdt_hi[:, k, :], xT_lo[:, k, :], start=False, stop=False)
                    last = mm(o, wdt_lo[:, k, :], xT_hi[:, k, :], start=False, stop=(k == 7))
                last.then_inc(S["dt_p"], 1)
                feat4()
                pe.wait_ge(S["dt_row"], 1)
                for t in range(TILES):
                    last = nc.tensor.transpose(A[:, 2, 8 * t:8 * t + 8], xn[0:8, 1, 512 + t * P:512 + t * P + P],
                                               ident[0:8, 0:8])
                last.then_inc(S["dt_t"], 1)
                feat4()
                pe.wait_ge(S["dt_da"], 1)
                da = small[:, 3, :]
                mm(A[:, 2, 0:32], c1v("upto"), da, start=True, stop=True)
                mm(A[:, 2, 32:64], c1v("minus_ones"), da, start=True, stop=True).then_inc(S["dt_cs"], 1)
                gate = token_steps()
                advance(gate, 5)
                pe.wait_ge(S["conv_silu"], 8)
                for c in range(TILES):
                    if c >= 2:
                        pe.wait_ge(S["x_tc"], 2 * (c - 1))
                    b = c % 2
                    for i in range(4):
                        nc.tensor.transpose(A[:, b, i * P:i * P + P], fA[:, i, c * P:c * P + P], I)
                    for i in range(2):
                        if c >= 1 and i == 0:
                            pe.wait_ge(S["x_tc"], 2 * c)
                        elif i == 0:
                            pe.wait_ge(S["dt_sub"], 1)
                        last = nc.tensor.transpose(A[:, 2, i * P:i * P + P], fB[:, i, c * P:c * P + P], I)
                    last.then_inc(S["x_t"], 1)
                pe.wait_ge(S["x_tc"], 8)
                for c in range(TILES):
                    if c:
                        pe.wait_ge(S["d_in"], c)
                        pe.wait_ge(S["d_st"], c)
                    for h in range(SSD_H):
                        mm(A[:, h // 4, (h % 4) * P:(h % 4 + 1) * P], bcast(da[:, 8 * c + h:8 * c + h + 1], [P, P]),
                           c1v("upto"), start=True, stop=True)
                    for g in range(2):
                        last = mm(A[:, 2, g * P:g * P + P], fB[:, g, c * P:c * P + P], fB[:, 2 + g, c * P:c * P + P],
                                  start=True, stop=True)
                    last.then_inc(S["d_bc"], 1)
                    advance(gate, (2, 1, 0, 0)[c])
                    pe.wait_ge(S["d_t"], c + 1)
                    if c:
                        for g in range(2):
                            last = mm(A[:, 0, g * 256:g * 256 + 256], fB[:, 2 + g, c * P:c * P + P],
                                      state[:, g * 256:g * 256 + 256], start=True, stop=True)
                    if c < 3:
                        for g in range(2):
                            last = mm(A[:, 1, g * 256:g * 256 + 256], xn[:, c // 2, (c % 2) * 256 + g * P:(c % 2) * 256 + g * P + P],
                                      sA[:, c * 512 + g * 256:c * 512 + g * 256 + 256], start=True, stop=True)
                    last.then_inc(S["d_kv"], 1)
                    pe.wait_ge(S["d_sc"], c + 1)
                    if c:
                        pe.wait_ge(S["d_yu"], c)
                    for h in range(SSD_H):
                        last = mm(A[:, 3, h * 64:h * 64 + 64], sB[:, 1024 + h * P:1024 + h * P + P],
                                  fA[:, c, h * 64:h * 64 + 64], start=True, stop=True)
                    last.then_inc(S["d_y"], 1)
                finished(gate)

            def mixer_out():
                transposes(lambda t: mix[:, t, :], TILES, 1)
                pe.wait_ge(S["tr_lo"], N.tr)
                for half in range(2):
                    tok4(kbs=(4,), hi=mixT_hi, lo=mixT_lo)

            pe.wait_ge(const_in, 16)
            with pe.Fori(0, DEPTH) as l:
                Pos.l = l
                Pos.pair, Pos.off, Pos.ubase, Pos.u = l * (BLOCK1 // 2), 0, l * UNITS1, 0
                N.tr, N.src = 0, 0
                pe.wait_ge(layer_open, l + 1)
                pe.sem_inc(S["layer_begun"], 1)
                transposes(lambda t: xn[:, t, :], 2, 2)
                pe.wait_ge(S["tr_lo"], N.tr)
                feat4(N_MEM)
                gemm((4, 4), [(o, [tok(o, xT_hi, xT_lo, o // 2, col=(o % 2) * 256, n=256)]) for o in range(4)])
                transposes(lambda t: xn[:, t, :] if t < 2 else mem_t[:, t - 2, :], 4, 2)
                pe.wait_ge(S["tr_lo"], N.tr)
                feat4()
                mem_attention()
                mixer_out()
                feat4()
                feat4()
                tok4()
                retention()
                mixer_out()
                feat4()
                feat4()
                stick()
                mixer_out()
                ssd()
                mixer_out()
                assert Pos.off == BLOCK1 and Pos.u == UNITS1
                pe.sem_inc(pe_end, 1)

            def ffn():
                for n, (units, downs) in enumerate(FF_HALVES):
                    base_pair, base_off, base_u = Pos.pair, Pos.off, Pos.u
                    assert base_off % 2 == 0
                    ub = Pos.ubase
                    with pe.Fori(0, units) as u:
                        Pos.pair, Pos.off, Pos.ubase, Pos.u = base_pair + u, base_off, ub + u, base_u
                        feat4()
                    Pos.pair, Pos.off, Pos.ubase, Pos.u = base_pair, base_off + 2 * units, ub, base_u + units
                    for half in range(2):
                        gemm(downs, [(o, [tok(o, h_hi, h_lo, o)]) for o in range(4)],
                             lambda chunks: pe.wait_ge(S["ff_lo"], N.ff + chunks))
                    N.ff += 2 * units

            def bias():
                param(pe, Pos.l, "rpb_in")
                param(pe, Pos.l, "sel_in")
                for k in range(NA_R):
                    if k >= 4:
                        pe.wait_ge(S["b_gc"], k - 3)
                    mm(A[:, k % 4, 0:248], sel[0:15, k * P:k * P + P], rpb_rows[0:15, 0:248],
                       start=True, stop=True).then_inc(S["b_g"], 1)
                pe.wait_ge(S["b_gc"], NA_R)

            def pool_mixer():
                results_read()
                param(pe, Pos.l, "poolw_in")
                pe.wait_ge(const2_in, 16)
                for ch in range(2):
                    for gg in range(2):
                        g = 2 * ch + gg
                        for c in range(4):
                            lo, hi = max(0, 128 * c - 8), min(SEQ, 128 * c + 136)
                            o = c2v("pool")[:, (4 * g + c) * 144 + lo - (128 * c - 8):(4 * g + c) * 144 + hi - (128 * c - 8)]
                            last = mm(A[64 * gg:64 * gg + 64, ch, lo:hi], work[:, c * 256 + g * 64:c * 256 + g * 64 + 64], o,
                                      start=(c == 0), stop=(c == 3), skip_group_check=True)
                    last.then_inc(S["p_t"], 1)
                for ch in range(2):
                    pe.wait_ge(S["p_tc"], ch + 1)
                    mm(A[:, 2 + ch, :], poolw[:, ch, :], y2tmp(ch), start=True, stop=True).then_inc(S["p_y"], 1)

            def y2tmp(ch):
                return conv_out[:, ch * 512:ch * 512 + 512]

            def neighbourhood():
                pe.wait_ge(S["b_bm"], 1)
                pe.wait_ge(S["y2l"], 2)
                c_h = gemm_steps((4, 4), [(o, [feat(o, xT_hi, xT_lo, o * P)]) for o in range(4)], fine=True)
                combos = [(h, j) for h in range(NA_H) for j in range(4)]

                def scores(i):
                    h, j = combos[i]
                    r = 64 * (h % 2)
                    a, b = max(0, j - 1), min(4, j + 2)
                    if i >= 2:
                        pe.wait_ge(S["n_m"], i - 1)
                    mm(A[:, i % 2, 0:(b - a) * P], qp[r:r + 64, h // 2, j * P:j * P + P],
                       kp[r:r + 64, h // 2, a * P:b * P], start=True, stop=True).then_inc(S["n_s"], 1)

                def turn(i):
                    h, j = combos[i]
                    n = min(4, j + 2) - max(0, j - 1)
                    pe.wait_ge(S["n_pn"], i + 1)
                    if i:
                        pe.wait_ge(S["n_tc"], i)
                    for k in range(n):
                        last = nc.tensor.transpose(A[:, 2, k * P:k * P + P], p_slot(i)[:, k * P:k * P + P], I)
                    last.then_inc(S["n_t"], 1)

                def pv(i):
                    h, j = combos[i]
                    r = 64 * (h % 2)
                    a, b = max(0, j - 1), min(4, j + 2)
                    pe.wait_ge(S["n_tc"], i + 1)
                    if i % 8 == 0 and i:
                        pe.wait_ge(S["n_ol"], i // 8)
                    for k in range(a, b):
                        last = mm(A[r:r + 64, 3, j * P:j * P + P], vp[:, k, h * 64:h * 64 + 64],
                                  pt_slot(i)[:, (k - a) * P:(k - a + 1) * P],
                                  start=(k == a), stop=(k == b - 1), skip_group_check=True)
                    last.then_inc(S["n_o"], 1)

                for i in range(len(combos) + 3):
                    if i < len(combos):
                        scores(i)
                    if i in C_H_STEPS:
                        advance(c_h, 1)
                    if 2 <= i < len(combos) + 2:
                        turn(i - 2)
                    if i >= 3:
                        pv(i - 3)
                finished(c_h)

            with pe.Fori(0, DEPTH) as l:
                Pos.l = l
                Pos.pair, Pos.off = l * (BLOCK2 // 2) + DEPTH * BLOCK1 // 2, 0
                Pos.ubase, Pos.u = l * UNITS2 + DEPTH * UNITS1, 0
                N.tr, N.src, N.ff = 0, 0, 0
                pe.wait_ge(layer_open, l + 1 + DEPTH)
                pe.sem_inc(S["layer_begun"], 1)
                transposes(lambda t: x[:, t, :], 4, 2)
                pe.wait_ge(S["tr_lo"], N.tr)
                ffn()
                bias()
                transposes(lambda t: x[:, t, :], 4, 2, norm=0)
                pe.wait_ge(S["tr_lo"], N.tr)
                gemm((4, 4), [(b, [tok(b, xT_hi, xT_lo, 2 * b + i, n=256, at=256 * i, own_start=(i == 0)) for i in range(2)])
                              for b in range(2)] +
                     [(2 + i, [feat(2 + i, xT_hi, xT_lo, 256 + i * P)]) for i in range(2)])
                feat4()
                feat4()
                pe.wait_ge(S["perm_hi"], 1)
                pe.wait_ge(S["perm_lo"], 1)
                tok4(hi=y2_hi, lo=y2_lo)
                pool_mixer()
                neighbourhood()
                pe.wait_ge(S["n_ol"], 4)
                for half in range(2):
                    gemm((4, 4), [(o, [tok(o, y2_hi, y2_lo, o)]) for o in range(4)],
                         lambda chunks: pe.wait_ge(S["y2l"], 4) if chunks > 4 else None)
                transposes(lambda t: x[:, t, :], 4, 2, norm=1)
                pe.wait_ge(S["tr_lo"], N.tr)
                ffn()
                assert Pos.off == BLOCK2 and Pos.u == UNITS2, (Pos.off, Pos.u)
                pe.sem_inc(pe_end, 1)

        @block.scalar
        def _(act):
            fn = nc.scalar.activation
            for i in range(4):
                act.sem_inc(g_free[i], 1)
            act.dma_start(ident[:, :], const0).then_inc(const_in, 16)

            class Pos:
                pair, off, end, ubase, u = 0, 0, 0, 0, 0

            class N:
                tr, ch, rs, ff = 0, 0, 0, 0

            def link(ins):
                N.ch += 1
                ins.then_inc(S["act_chain"], 1)
                act.wait_ge(S["act_chain"], N.ch)

            def split(nk=KB):
                s = Pos.off % 2
                act.wait_ge(raw_in[s], (Pos.pair + Pos.off // 2 + 1) * 16)
                act.wait_ge(blk_used, 2 * Pos.pair + Pos.off + 1)
                fn(w_hi[:, s, 0:nk, :], raw[:, s, 0:nk, :], ACT.Copy).then_inc(hi_done, 1)
                Pos.off += 1

            def unit(evac, nxt):
                if nxt:
                    split(nxt[0])
                evac()
                for nk in nxt[1:]:
                    split(nk)
                Pos.u += 1
                Pos.end += len(nxt)

            def done(bank):
                if bank < 3:
                    act.wait_ge(g_done[bank], Pos.ubase + Pos.u + 1)
                else:
                    act.wait_ge(blk_used, 2 * Pos.pair + Pos.end + 2)

            def evac4(dst, func=ACT.Copy, src=None, scale=1.0):
                def go():
                    for b in range(4):
                        done(b)
                        fn(dst(b), src(b) if src else G[:, b, :], func, scale=scale).then_inc(g_free[b], 1)
                return go

            def gate_out():
                evac4(lambda b: tB[:, b, :], ACT.Silu)()
                Pos.u, Pos.end = Pos.u + 1, Pos.end + 1

            def tr_hi(dst, tiles, groups):
                for t in range(tiles):
                    for g in range(groups):
                        act.wait_ge(S["tr_done"], N.tr + 1)
                        fn(dst[:, 4 * g:4 * g + 4, t * P:t * P + P], A[:, N.tr % 4, :].rearrange("p (c t) -> p c t", c=4),
                           ACT.Copy).then_inc(S["tr_hi"], 1)
                        N.tr += 1

            def rsqrt(n, at=0, preload=True):
                N.rs += 1
                if preload:
                    act.preload_act_table_set(LN_EXP)
                act.wait_ge(S["rs_in"], N.rs)
                link(fn(rs_t[:, at:at + n], rs_v[:, at:at + n], ACT.Ln))
                fn(rs_r[:, at:at + n], rs_t[:, at:at + n], ACT.Exp, scale=-0.5).then_inc(S["rs_out"], 1)

            def layer_norm(i, between=None):
                for a in (0, 2):
                    rsqrt(2, a, preload=False)
                    if between:
                        between(a // 2)
                    act.wait_ge(S["ln_bias"], 2 * i + a // 2 + 1)
                    for t in (a, a + 1):
                        fn(x[:, t, :], x[:, t, :], ACT.Identity, scale=rs_r[:, t:t + 1],
                           bias=nmx[:, 0, t:t + 1]).then_inc(S["ln_std"], 1)

            def mem_attention():
                for q in range(TILES):
                    if q == 3:
                        split()
                    act.wait_ge(S["m_nb"], q + 1)
                    act.wait_ge(S["m_log"], q + 1)
                    if q:
                        act.wait_ge(S["m_pt"], q)
                    for h in range(HEADS):
                        fn(sA[:, h * 256:h * 256 + 256], A[:, h // 2, (h % 2) * 256:(h % 2) * 256 + 256], ACT.Exp,
                           bias=small[:, 0, h:h + 1], scale=SCALE, accum_out=small[:, 1, h:h + 1]).then_inc(S["m_p"], 1)
                gate_out()

            def stick():
                act.preload_act_table_set(LN_EXP)
                flat = A[:, :, :].rearrange("p b n -> p (b n)")[:, 0:1280]
                for h in range(HEADS):
                    if h == 3:
                        split()
                    act.wait_ge(S["s_log"], h + 1)
                    link(fn(sB[:, 0:1280], flat, ACT.Abs))
                    link(fn(sB[:, 0:1280], sB[:, 0:1280], ACT.Exp, scale=-1.0))
                    fn(sB[:, 0:1280], sB[:, 0:1280], ACT.Ln, bias=1.0).then_inc(S["s_ln"], 1)
                    if h == 0:
                        split()
                    act.wait_ge(S["s_cum"], h + 1)
                    fn(sA[:, 0:1280], flat, ACT.Exp).then_inc(S["s_w"], 1)
                    if h == 0:
                        evac4(lambda b: tA[:, b, :])()
                        split()
                        Pos.u, Pos.end = Pos.u + 1, Pos.end + 2
                gate_out()

            def silu_conv(buf):
                def go():
                    for b in range(4):
                        act.wait_ge(g_free[b], Pos.ubase + Pos.u + 2)
                        fn(buf[:, b, :], buf[:, b, :], ACT.Silu).then_inc(S["conv_silu"], 1)
                return go

            def ssd():
                unit(silu_conv(fA), (4, 4))
                act.preload_act_table_set(LN_EXP)
                param(act, Pos.l, "row_in", 2, 2)
                fn(small[:, 11, 0:8], row[:, A_LOG:A_LOG + 8], ACT.Exp).then_inc(S["dt_al"], 1)
                act.wait_ge(S["dt_ab"], 1)
                link(fn(small[:, 1, :], small[:, 1, :], ACT.Exp, scale=-1.0))
                fn(small[:, 1, :], small[:, 1, :], ACT.Ln, bias=1.0).then_inc(S["dt_ln"], 1)
                unit(silu_conv(fB), (4, 4))
                act.preload_act_table_set(LN_EXP)
                act.wait_ge(S["dt_sub"], 1)
                fn(small[:, 6, :], small[:, 4, :], ACT.Exp).then_inc(S["dt_ex"], 1)
                fn(small[:, 7, :], small[:, 5, :], ACT.Exp).then_inc(S["dt_ex"], 1)
                fn(small[:, 8, :], small[:, 9, :], ACT.Exp).then_inc(S["dt_ex"], 1)
                split()
                for c in range(TILES):
                    if c == 3:
                        gate_out()
                        act.preload_act_table_set(LN_EXP)
                    act.wait_ge(S["d_t"], c + 1)
                    fn(sB[:, 0:1024], sB[:, 0:1024], ACT.Exp).then_inc(S["d_e"], 1)

            def mixer_out(nxt):
                tr_hi(mixT_hi, TILES, 1)
                unit(lambda: None, (4,))
                unit(lambda: None, nxt)

            act.wait_ge(landed["mem_in"], 16)
            act.dma_start(x[:, :, :], x_in.rearrange("a (t p) d -> p (a t) d", p=P)).then_inc(x_loaded, 16)
            act.dma_start(cst[:, :], const1).then_inc(const1_in, 16)
            T, K2 = (4, 4), (4, 4)
            with act.Fori(0, DEPTH) as l:
                Pos.l = l
                Pos.pair, Pos.off, Pos.end, Pos.ubase, Pos.u = l * (BLOCK1 // 2), 0, 2, l * UNITS1, 0
                N.tr, N.ch, N.rs = 0, 0, 0
                split()
                split()
                act.wait_ge(layer_open, l + 1)
                act.sem_inc(S["layer_begun"], 1)
                rsqrt(2)
                tr_hi(xT_hi, 2, 2)
                rsqrt(4)
                unit(evac4(lambda b: mk[:, b, :], src=lambda b: G[:, b, 0:N_MEM]), K2)
                unit(evac4(lambda b: tA[:, b // 2, (b % 2) * 256:(b % 2) * 256 + 256], src=lambda b: G[:, b, 0:256]), K2)
                tr_hi(xT_hi, 4, 2)
                unit(evac4(lambda b: fA[:, b, :]), K2)
                mem_attention()
                mixer_out(K2)
                unit(evac4(lambda b: fA[:, b, :]), K2)
                unit(evac4(lambda b: fB[:, b, :]), K2)
                unit(evac4(lambda b: tA[:, b, :]), K2)
                split()
                rsqrt(16)
                gate_out()
                mixer_out(K2)
                unit(evac4(lambda b: fA[:, b, :], scale=SCALE), K2)
                unit(evac4(lambda b: fB[:, b, :]), K2)
                stick()
                param(act, Pos.l, "wdt_in")
                fn(wdt_hi[:, :, :], wdt[:, :, :], ACT.Copy).then_inc(S["wdt_h"], 1)
                mixer_out(K2)
                ssd()
                rsqrt(8)
                mixer_out(())
                rsqrt(4)
                assert Pos.off == BLOCK1 and Pos.u == UNITS1
                act.sem_inc(act_end, 1)

            def ffn(nxt):
                for n, (units, downs) in enumerate(FF_HALVES):
                    base_pair, base_off, base_u, ub = Pos.pair, Pos.off, Pos.u, Pos.ubase
                    c0 = N.ff
                    with act.Fori(0, units) as u:
                        Pos.pair, Pos.off, Pos.end = base_pair + u, base_off, base_off
                        Pos.ubase, Pos.u = ub + u, base_u
                        split()
                        for i in range(2):
                            done(i)
                            act.wait_ge(g_free[2 + i], ub + u + (base_u + 1))
                            fn(work[:, i * 512:i * 512 + 512], G[:, i, :], ACT.Silu).then_inc(g_free[i], 1)
                        for i in range(2):
                            act.wait_ge(g_free[2 + i], ub + u + (base_u + 2))
                            fn(h_hi[:, bass.ds(2 * u + i, 1), :].rearrange("p o n -> p (o n)"),
                               work[:, 1024 + i * 512:1536 + i * 512], ACT.Copy).then_inc(S["ff_hi"], 1)
                        split()
                    Pos.pair, Pos.off, Pos.end = base_pair, base_off + 2 * units, base_off + 2 * units + 1
                    Pos.ubase, Pos.u = ub, base_u + units
                    N.ff += 2 * units
                    split(downs[2])
                    unit(lambda: None, (4, 4, downs[2]))
                    if n == 1:
                        act.preload_act_table_set(LN_EXP)
                    unit(lambda: None, (4, 4) if n == 0 else nxt)

            with act.Fori(0, DEPTH) as l:
                Pos.l = l
                Pos.pair, Pos.off, Pos.end = l * (BLOCK2 // 2) + DEPTH * BLOCK1 // 2, 0, 2
                Pos.ubase, Pos.u = l * UNITS2 + DEPTH * UNITS1, 0
                N.tr, N.ch, N.rs, N.ff = 0, 0, 0, 0
                split()
                split()
                act.wait_ge(layer_open, l + 1 + DEPTH)
                act.sem_inc(S["layer_begun"], 1)
                tr_hi(xT_hi, 4, 2)
                ffn(K2)

                def bias_rows(half):
                    for k in range(4 * half, 4 * half + 4):
                        act.wait_ge(S["b_g"], k + 1)
                        fn(raw_rows.rearrange("p (h k e) -> p h k e", h=8, k=8)[:, :, k, :],
                           A[:, k % 4, 0:248].rearrange("p (h e) -> p h e", h=8), ACT.Copy).then_inc(S["b_gc"], 1)
                layer_norm(0, bias_rows)
                tr_hi(xT_hi, 4, 2)
                act.wait_ge(S["tr_hi"], N.tr)
                fn(y2_hi[:, :, :].rearrange("p k (c r) -> p k c r", r=NA_R),
                   xT_hi[:, :, :].bitcast(F32).rearrange("p k (r c) -> p k c r", c=GRID_W), ACT.Copy).then_inc(S["perm_hi"], 1)

                def ub():
                    for b in range(2):
                        done(b)
                        param(act, Pos.l, "shift_in", 16, 16)
                        fn(work[:, b * 512:b * 512 + 512], G[:, b, :], ACT.Copy).then_inc(g_free[b], 1)
                    for b in range(2):
                        done(2 + b)
                        fn(gate_b[:, b * 512:b * 512 + 512], G[:, 2 + b, :], ACT.Copy).then_inc(g_free[2 + b], 1)
                unit(ub, K2)

                act.wait_ge(S["b_bm"], 1)
                unit(evac4(lambda b: qp[:, b, :].rearrange("p (c r) -> p c r", r=NA_R),
                           src=lambda b: perm_view(G[:, b, :])), K2)
                unit(evac4(lambda b: kp[:, b, :].rearrange("p (c r) -> p c r", r=NA_R),
                           src=lambda b: perm_view(G[:, b, :])), K2)
                unit(evac4(lambda b: vp[:, b, :]), K2)
                for ch in range(2):
                    act.wait_ge(S["p_t"], ch + 1)
                    fn(conv_out[:, ch * 512:ch * 512 + 512], A[:, ch, :], ACT.Copy).then_inc(S["p_tc"], 1)
                param(act, Pos.l, "col2_in")
                for ch in range(2):
                    act.wait_ge(S["p_y"], ch + 1)
                    fn(y2_hi[:, 4 + ch, :], A[:, 2 + ch, :], ACT.Copy, scale=col2[:, ch, 3:4]).then_inc(S["y2h"], 1)
                combos = [(h, j) for h in range(NA_H) for j in range(4)]

                def exps(i):
                    h, j = combos[i]
                    n = (min(4, j + 2) - max(0, j - 1)) * P
                    act.wait_ge(S["n_m"], i + 1)
                    w = p_slot(i)[:, 0:n]
                    fn(w, w, ACT.Exp, bias=nmx[:, 0, i:i + 1], accum_out=nmx[:, 1, i:i + 1]).then_inc(S["n_p"], 1)

                def turned(i):
                    h, j = combos[i]
                    n = (min(4, j + 2) - max(0, j - 1)) * P
                    act.wait_ge(S["n_t"], i + 1)
                    if i >= 2:
                        act.wait_ge(S["n_o"], i - 1)
                    fn(pt_slot(i)[:, 0:n], A[:, 2, 0:n], ACT.Copy).then_inc(S["n_tc"], 1)

                def pair_out(i):
                    act.wait_ge(S["n_o"], 8 * i + 8)
                    fn(y2_hi[:, i, :].rearrange("p (r c) -> p c r", c=GRID_W),
                       A[:, 3, :].rearrange("p (c r) -> p c r", r=NA_R), ACT.Copy).then_inc(S["n_oh"], 1)

                for i in range(len(combos) + 3):
                    if i == C_H_STEPS[15] + 2:
                        split()
                    if 2 <= i < len(combos) + 2:
                        turned(i - 2)
                    if i < len(combos):
                        exps(i)
                    if i >= 3 and (i - 3) % 8 == 7:
                        pair_out((i - 3) // 8)
                for b in range(2):
                    done(b)
                    fn(work[:, b * 512:b * 512 + 512], G[:, b, :], ACT.Copy).then_inc(g_free[b], 1)
                split()
                Pos.u, Pos.end = Pos.u + 1, Pos.end + 2
                for ch in range(2):
                    act.wait_ge(S["z_y"], ch + 1)
                    fn(y2_hi[:, 6 + ch, :], gate_b[:, ch * 512:ch * 512 + 512], ACT.Copy).then_inc(S["y2h"], 1)
                unit(lambda: None, K2)
                act.preload_act_table_set(LN_EXP)
                unit(lambda: None, K2)
                layer_norm(1)
                tr_hi(xT_hi, 4, 2)
                ffn(())
                layer_norm(2)
                assert Pos.off == BLOCK2 and Pos.u == UNITS2
                act.sem_inc(act_end, 1)

        @block.vector
        def _(dve):
            tt, ts, stt = nc.vector.tensor_tensor, nc.vector.tensor_scalar, nc.vector.scalar_tensor_tensor
            dve.sem_inc(lo_done, 2)

            class Pos:
                pair, off, end, ubase, u = 0, 0, 0, 0, 0

            class N:
                tr, ch, rs, ff, half = 0, 0, 0, 0, 0

            def link(ins):
                N.ch += 1
                ins.then_inc(S["dve_chain"], 1)
                dve.wait_ge(S["dve_chain"], N.ch)

            def split(nk=KB):
                s = Pos.off % 2
                dve.wait_ge(hi_done, 2 * Pos.pair + Pos.off + 1)
                tt(w_lo[:, s, 0:nk, :], raw[:, s, 0:nk, :], w_hi[:, s, 0:nk, :].bitcast(F32),
                   ALU.subtract).then_inc(lo_done, 1)
                Pos.off += 1

            def unit(evac, nxt):
                if nxt:
                    split(nxt[0])
                evac()
                for nk in nxt[1:]:
                    split(nk)
                Pos.u += 1
                Pos.end += len(nxt)

            def done(bank):
                if bank < 3:
                    dve.wait_ge(g_done[bank], Pos.ubase + Pos.u + 1)
                else:
                    dve.wait_ge(blk_used, 2 * Pos.pair + Pos.end + 2)

            def none():
                pass

            def results_read():
                for bank in range(4):
                    dve.wait_ge(g_free[bank], Pos.ubase + Pos.u + 1)

            def tr_lo(dst_hi, dst_lo, tiles, groups):
                for t in range(tiles):
                    for g in range(groups):
                        dve.wait_ge(S["tr_hi"], N.tr + 1)
                        tt(dst_lo[:, 4 * g:4 * g + 4, t * P:t * P + P], A[:, N.tr % 4, :].rearrange("p (c t) -> p c t", c=4),
                           dst_hi[:, 4 * g:4 * g + 4, t * P:t * P + P].bitcast(F32), ALU.subtract).then_inc(S["tr_lo"], 1)
                        N.tr += 1

            def rsqrt(n, scale, eps):
                ts(rs_v[:, 0:n], rs_v[:, 0:n], scale, eps, ALU.mult, ALU.add).then_inc(S["rs_in"], 1)
                newton(n)

            def newton(n, at=0):
                v, r, t = rs_v[:, at:at + n], rs_r[:, at:at + n], rs_t[:, at:at + n]
                N.rs += 1
                dve.wait_ge(S["rs_out"], N.rs)
                link(tt(t, r, r, ALU.mult))
                link(tt(t, t, v, ALU.mult))
                link(ts(t, t, -0.5, 1.5, ALU.mult, ALU.add))
                link(tt(r, r, t, ALU.mult))

            def x_tile(t):
                return xn[:, t, :] if t < 2 else mem_t[:, t - 2, :]

            def rms_operand(src, tiles, g, meanwhile, loaded):
                for t in range(tiles):
                    ins = nc.vector.tensor_tensor_reduce(out=xn[:, 0, :], in0=src(t), in1=src(t), scale=1.0, scalar=0.0,
                                                         op0=ALU.mult, op1=ALU.add, accum_out=rs_v[:, t:t + 1])
                    link(ins)
                rsqrt(tiles, 1.0 / D, EPS)
                loaded()
                for t in range(tiles):
                    stt(out=x_tile(t), in0=src(t), scalar=rs_r[:, t:t + 1], in1=row[:, g:g + D],
                        op0=ALU.mult, op1=ALU.mult).then_inc(S["tr_src"], 1)
                meanwhile()
                tr_lo(xT_hi, xT_lo, tiles, 2)

            def heads(ap, n=4):
                return ap.unsqueeze(2).to_broadcast([P, n, P])

            def gate_split():
                split()
                Pos.u, Pos.end = Pos.u + 1, Pos.end + 1

            def mem_attention():
                for q in range(TILES):
                    if q == 3:
                        gate_split()
                    dve.wait_ge(S["m_log"], q + 1)
                    link(nc.vector.tensor_reduce(small[:, 2, 0:4],
                                                 A[:, 0:2, :].rearrange("p b (h n) -> p (b h) n", h=2), AX.X, ALU.max))
                    ts(small[:, 0, 0:4], small[:, 2, 0:4], -SCALE, None, ALU.mult).then_inc(S["m_nb"], 1)
                    dve.wait_ge(S["m_pt"], q + 1)
                    nc.vector.tensor_copy(sB[:, 0:1024], A[:, 2:4, :].rearrange("p b n -> p (b n)")).then_inc(S["m_ptc"], 1)
                    dve.wait_ge(S["m_p"], 4 * (q + 1))
                    link(nc.vector.reciprocal(small[:, 3, 0:4], small[:, 1, 0:4]))
                    dve.wait_ge(S["m_o"], q + 1)
                    m = mix[:, q, :].rearrange("p (h n) -> p h n", h=4)
                    tt(m, A[:, 0, :].rearrange("p (h n) -> p h n", h=4), heads(small[:, 3, 0:4]),
                       ALU.mult).then_inc(S["m_y"], 1)
                dve.wait_ge(S["m_y"], TILES)
                gated()

            def gated():
                results_read()
                for t in range(TILES):
                    tt(mix[:, t, :], mix[:, t, :], tB[:, t, :], ALU.mult).then_inc(S["tr_src"], 1)

            def mixer_out(first, nxt):
                tr_lo(mixT_hi, mixT_lo, TILES, 1)
                for half in range(2):
                    def add():
                        for b in range(4):
                            done(b)
                            o = y_acc[:, b, half * 512:half * 512 + 512]
                            if first:
                                ins = nc.vector.tensor_copy(o, G[:, b, :])
                            else:
                                ins = tt(o, o, G[:, b, :], ALU.add)
                            ins.then_inc(g_free[b], 1)
                            if half and not nxt:
                                dve.wait_ge(g_free[b], Pos.ubase + Pos.u + 2)
                                link(nc.vector.tensor_tensor_reduce(
                                    out=xn[:, 0, :], in0=y_acc[:, b, :], in1=y_acc[:, b, :], scale=1.0, scalar=0.0,
                                    op0=ALU.mult, op1=ALU.add, accum_out=rs_v[:, b:b + 1]))
                    unit(add, (4,) if half == 0 else nxt)

            def retention():
                dve.wait_ge(const1_in, 16)
                for i in range(8):
                    f = (fA if i < 4 else fB)[:, i % 4, :]
                    dve.wait_ge(S["rot_done"], i + 1)
                    tt(xn[:, 1, 0:512], A[:, i % 4, :], c1v("sin"), ALU.mult).then_inc(S["rot_used"], 1)
                    dve.wait_ge(S["rot_used"], i + 1)
                    dve.wait_ge(S["rot_cos"], i + 1)
                    link(tt(f, f, xn[:, 1, 0:512], ALU.add))
                nc.vector.sem_inc(S["ret_ready"], 1)
                xi = c1v("xi").rearrange("p (h n) -> p h n", h=4)
                for h in range(HEADS):
                    link(tt(sA[:, h * 512:h * 512 + 512].rearrange("p (c n) -> p c n", c=4),
                            fA[:, h, :].rearrange("p (c n) -> p c n", c=4),
                            xi[:, h:h + 1, :].to_broadcast([P, 4, P]), ALU.mult))
                for c in range(3):
                    dve.wait_ge(S["rz_t"], c + 1)
                    ins = tt(sB[:, c * 512:c * 512 + 512].rearrange("p (h n) -> p h n", h=4),
                             A[:, c, :].rearrange("p (h n) -> p h n", h=4), heads(c1v("zeta")), ALU.mult)
                    ins.then_inc(S["rz_used"], 1)
                for c in range(TILES):
                    dve.wait_ge(S["r_s"], c + 1)
                    if c:
                        dve.wait_ge(S["r_y"], c)
                    tt(xn[:, 0, 0:512], A[:, 0, :], c1v("intra"), ALU.mult).then_inc(S["r_sm"], 1)
                    if c == 1:
                        gate_split()
                    dve.wait_ge(S["r_y"], c + 1)
                    nc.vector.tensor_copy(mix[:, c, :], A[:, 1, :]).then_inc(S["r_yu"], 1)
                    if c < 3:
                        dve.wait_ge(S["r_kv"], c + 1)
                        for h in range(HEADS):
                            o, k = state[:, h * P:h * P + P], A[:, 2, h * P:h * P + P]
                            if c == 0:
                                nc.vector.tensor_copy(o, k).then_inc(S["r_st"], 1)
                            else:
                                stt(out=o, in0=o, scalar=RET_DECAY[h], in1=k, op0=ALU.mult,
                                    op1=ALU.add).then_inc(S["r_st"], 1)
                    dve.wait_ge(S["r_yu"], c + 1)
                    for h in range(HEADS):
                        ins = nc.vector.bn_stats(stats[:, 4 * c + h, :], mix[:, c, h * P:h * P + P])
                link(ins)
                for i in range(16):
                    ins = nc.vector.bn_aggr(mean_var[:, i, :], stats[:, i, :])
                link(ins)
                ts(rs_v[:, 0:16], mean_var[:, :, 1], EPS, None, ALU.add).then_inc(S["rs_in"], 1)
                newton(16)
                for t in range(TILES):
                    m = mix[:, t, :].rearrange("p (h n) -> p h n", h=4)
                    link(tt(m, m, heads(mean_var[:, 4 * t:4 * t + 4, 0]), ALU.subtract))
                    link(tt(m, m, heads(rs_r[:, 4 * t:4 * t + 4]), ALU.mult))
                    if t == 0:
                        results_read()
                    tt(mix[:, t, :], mix[:, t, :], tB[:, t, :], ALU.mult).then_inc(S["tr_src"], 1)

            SB_AT = (0, 512, 1024, 896)

            def stick():
                flat = A[:, :, :].rearrange("p b n -> p (b n)")[:, 0:1280]
                E = sB[:, 0:1280]
                for h in range(HEADS):
                    if h == 3:
                        gate_split()
                    dve.wait_ge(S["s_ln"], h + 1)
                    link(stt(out=E, in0=flat, scalar=0.0, in1=E, op0=ALU.max, op1=ALU.add))
                    for i in range(4):
                        e = sB[:, SB_AT[i]:SB_AT[i] + P]
                        ins = tt(e, e, c1v("before"), ALU.mult)
                    ins.then_inc(S["s_sp"], 1)
                    if h == 0:
                        split()
                    dve.wait_ge(S["s_pv"], h + 1)
                    nc.vector.tensor_copy(mix[:, :, h * P:h * P + P],
                                          A[:, 3, :].rearrange("p (j n) -> p j n", j=4)).then_inc(S["s_pvu"], 1)
                    if h == 0:
                        split()
                        Pos.u, Pos.end = Pos.u + 1, Pos.end + 2
                dve.wait_ge(S["s_pvu"], 4)
                gated()

            def conv_in(buf, base):
                def go():
                    param(dve, Pos.l, "conv_in")
                    for b in range(4):
                        done(b)
                        f, w = buf[:, b, :], conv[:, base + b, :]
                        link(ts(f, G[:, b, :], w[:, 3:4], w[:, 4:5], ALU.mult, ALU.add))
                        for s in (1, 2, 3):
                            ins = stt(out=f[:, s:], in0=G[:, b, 0:512 - s], scalar=w[:, 3 - s:4 - s], in1=f[:, s:],
                                      op0=ALU.mult, op1=ALU.add)
                            if s < 3:
                                link(ins)
                        ins.then_inc(g_free[b], 1)
                return go

            def per_head(ap, c=None):
                return ap.unsqueeze(2).to_broadcast([P, ap.shape[1], 64])

            def ssd():
                dve.wait_ge(S["dt_p"], 1)
                nc.vector.tensor_copy(xn[0:8, 1, 512:1024], A[0:8, 3, :]).then_inc(S["dt_row"], 1)
                unit(conv_in(fA, 0), (4, 4))
                dve.wait_ge(S["dt_t"], 1)
                u, ab = small[:, 0, :], small[:, 1, :]
                link(tt(u.rearrange("p (t h) -> p t h", h=8), A[:, 2, 0:32].rearrange("p (t h) -> p t h", h=8),
                        row[:, DT_B:DT_B + 8].unsqueeze(1).to_broadcast([P, 4, 8]), ALU.add))
                stt(out=ab, in0=u, scalar=-1.0, in1=u, op0=ALU.mult, op1=ALU.max).then_inc(S["dt_ab"], 1)
                dve.wait_ge(S["dt_ln"], 1)
                dl = small[:, 2, :]
                link(stt(out=dl, in0=u, scalar=0.0, in1=ab, op0=ALU.max, op1=ALU.add))
                dve.wait_ge(S["dt_al"], 1)
                stt(out=small[:, 3, :].rearrange("p (t h) -> p t h", h=8), in0=dl.rearrange("p (t h) -> p t h", h=8),
                    scalar=-1.0, in1=small[:, 11, 0:8].unsqueeze(1).to_broadcast([P, 4, 8]),
                    op0=ALU.mult, op1=ALU.mult).then_inc(S["dt_da"], 1)
                unit(conv_in(fB, 4), (4, 4))
                dve.wait_ge(S["dt_cs"], 1)
                nc.vector.tensor_copy(small[:, 4, :], A[:, 2, 0:32])
                link(ts(small[:, 5, :], A[:, 2, 32:64], -1.0, None, ALU.mult))
                tt(small[:, 9, :], small[:, 5, :], small[:, 4, :], ALU.subtract).then_inc(S["dt_sub"], 1)
                gate_split()
                for c in range(TILES):
                    dve.wait_ge(S["x_t"], c + 1)
                    nc.vector.tensor_copy(tA[:, c, :], A[:, c % 2, :]).then_inc(S["x_tc"], 1)
                    nc.vector.tensor_copy(xn[:, c // 2, (c % 2) * 256:(c % 2) * 256 + 256],
                                          A[:, 2, 0:256]).then_inc(S["x_tc"], 1)
                dve.wait_ge(S["x_tc"], 8)

                def weighted(c):
                    f2 = fA[:, c, :].rearrange("p (h n) -> p h n", n=64)
                    link(tt(f2, tA[:, c, :].rearrange("p (h n) -> p h n", n=64), per_head(dl[:, 8 * c:8 * c + 8]), ALU.mult))
                    if c < 3:
                        link(tt(sA[:, c * 512:c * 512 + 512].rearrange("p (h n) -> p h n", n=64), f2,
                                per_head(small[:, 8, 8 * c:8 * c + 8]), ALU.mult))

                def gated_squares(c):
                    m = mix[:, c, :]
                    link(tt(m, m, tB[:, c, :], ALU.mult))
                    for g in range(2):
                        v = m[:, g * 256:g * 256 + 256]
                        link(nc.vector.tensor_tensor_reduce(out=sB[:, 512 + g * 256:768 + g * 256], in0=v, in1=v, scale=1.0,
                                                            scalar=0.0, op0=ALU.mult, op1=ALU.add,
                                                            accum_out=rs_v[:, 2 * c + g:2 * c + g + 1]))
                dve.wait_ge(S["dt_ex"], 3)
                weighted(0)
                for c in range(TILES):
                    t = sB[:, 0:1024].rearrange("p (h n) -> p h n", n=P)
                    dve.wait_ge(S["d_bc"], c + 1)
                    link(tt(t, A[:, 0:2, :].rearrange("p b (h n) -> p (b h) n", n=P),
                            heads(small[:, 4, 8 * c:8 * c + 8], 8), ALU.subtract))
                    tt(t, t, c1v("upto_neg").unsqueeze(1).to_broadcast([P, 8, P]), ALU.min).then_inc(S["d_t"], 1)
                    dve.wait_ge(S["d_e"], c + 1)
                    if c:
                        dve.wait_ge(S["d_y"], c)
                    for g in range(2):
                        ins = tt(sB[:, 1024 + g * 512:1536 + g * 512].rearrange("p (h n) -> p h n", n=P),
                                 sB[:, g * 512:g * 512 + 512].rearrange("p (h n) -> p h n", n=P),
                                 A[:, 2, g * P:g * P + P].unsqueeze(1).to_broadcast([P, 4, P]), ALU.mult)
                    ins.then_inc(S["d_sc"], 1)
                    m, part = mix[:, c, :], sB[:, 0:512]
                    dve.wait_ge(S["d_kv"], c + 1)
                    dve.wait_ge(S["d_skip"], c + 1)
                    if c:
                        dve.wait_ge(S["d_sc"], c + 1)
                        tt(part.rearrange("p (h n) -> p h n", n=64), A[:, 0, :].rearrange("p (h n) -> p h n", n=64),
                           per_head(small[:, 6, 8 * c:8 * c + 8]), ALU.mult).then_inc(S["d_in"], 1)
                    else:
                        nc.vector.sem_inc(S["d_in"], 1)
                    if c == 0:
                        nc.vector.tensor_copy(state[:, :], A[:, 1, :]).then_inc(S["d_st"], 1)
                    elif c < 3:
                        s3 = state[:, :].rearrange("p (h n) -> p h n", n=64)
                        link(tt(s3, s3, per_head(small[:, 7, 8 * c:8 * c + 8]), ALU.mult))
                        tt(state[:, :], state[:, :], A[:, 1, :], ALU.add).then_inc(S["d_st"], 1)
                    if c:
                        dve.wait_ge(S["d_in"], c + 1)
                        link(tt(m, m, part, ALU.add))
                    if c < 3:
                        weighted(c + 1)
                    else:
                        results_read()
                        for k in range(3):
                            gated_squares(k)
                    dve.wait_ge(S["d_y"], c + 1)
                    link(tt(m, m, A[:, 3, :], ALU.add))
                    nc.vector.sem_inc(S["d_yu"], 1)
                gated_squares(3)
                rsqrt(8, 1.0 / 256, EPS)
                for c in range(TILES):
                    for g in range(2):
                        o = mix[:, c, g * 256:g * 256 + 256]
                        ins = stt(out=o, in0=o, scalar=rs_r[:, 2 * c + g:2 * c + g + 1],
                                  in1=row[:, SSD_G + g * 256:SSD_G + g * 256 + 256], op0=ALU.mult, op1=ALU.mult)
                    ins.then_inc(S["tr_src"], 1)

            def end_layer(n):
                dve.wait_ge(pe_end, n)
                dve.wait_ge(act_end, n)
                dve.wait_ge(pool_end, n)
                nc.vector.sem_inc(S["layer_left"], 1)
                nc.vector.sem_clear(STAGES)
                nc.vector.memset(rs_t[:, 0:2], 0.0).then_inc(layer_open, 1)

            nc.vector.sem_inc(layer_open, 1)
            K2 = (4, 4)
            with dve.Fori(0, DEPTH) as l:
                Pos.l = l
                Pos.pair, Pos.off, Pos.end, Pos.ubase, Pos.u = l * (BLOCK1 // 2), 0, 2, l * UNITS1, 0
                N.tr, N.ch, N.rs = 0, 0, 0
                param(dve, Pos.l, "mem_in")
                rms_operand(lambda t: mem_t[:, t, :], 2, MEM_G, split, lambda: param(dve, Pos.l, "mem_g_in"))
                split()
                dve.wait_ge(x_loaded, 16)

                def memory_units():
                    unit(none, K2)
                    unit(none, K2)
                rms_operand(lambda t: x[:, t, :], 4, PRE_G, memory_units, lambda: param(dve, Pos.l, "row_in", 2, 2))
                unit(none, K2)
                mem_attention()
                mixer_out(True, K2)
                for _ in range(3):
                    unit(none, K2)
                retention()
                mixer_out(False, K2)
                for _ in range(2):
                    unit(none, K2)
                stick()
                dve.wait_ge(S["wdt_h"], 1)
                tt(wdt_lo[:, :, :], wdt[:, :, :], wdt_hi[:, :, :].bitcast(F32), ALU.subtract).then_inc(S["wdt_l"], 1)
                mixer_out(False, K2)
                ssd()
                mixer_out(False, ())
                rsqrt(4, 1.0 / D, EPS)
                for t in range(4):
                    stt(out=y_acc[:, t, :], in0=y_acc[:, t, :], scalar=rs_r[:, t:t + 1], in1=row[:, POST_G:POST_G + D],
                        op0=ALU.mult, op1=ALU.mult).then_inc(S["y_scaled"], 1)
                nc.vector.sem_inc(S["row_used"], 1)
                for t in (2, 3):
                    dve.wait_ge(S["y_scaled"], t + 1)
                    tt(x[:, t, :], x[:, t, :], y_acc[:, t, :], ALU.add).then_inc(S["x_added"], 1)
                dve.wait_ge(S["x_added"], 4)
                assert Pos.off == BLOCK1 and Pos.u == UNITS1
                end_layer(l + 1)

            def ln_scale(a):
                newton(2, a)
                stt(out=nmx[:, 0, a:a + 2], in0=mean_var[:, a:a + 2, 0], scalar=-1.0, in1=rs_r[:, a:a + 2],
                    op0=ALU.mult, op1=ALU.mult).then_inc(S["ln_bias"], 1)

            def late_split():
                split()
                Pos.end += 1

            def add_half(scale, half, eps=None):
                def go():
                    for b in range(4):
                        done(b)
                        o = x[:, b, half * 512:half * 512 + 512]
                        if scale == 1.0:
                            ins = tt(o, o, G[:, b, :], ALU.add)
                        else:
                            ins = stt(out=o, in0=o, scalar=scale, in1=G[:, b, :], op0=ALU.mult, op1=ALU.add)
                        ins.then_inc(g_free[b], 1)
                        if eps is None:
                            continue
                        dve.wait_ge(g_free[b], Pos.ubase + Pos.u + 2)
                        ins = nc.vector.bn_stats(stats[:, 2 * b + half, :], o)
                        if half and b % 2:
                            link(ins)
                            for t in (b - 1, b):
                                ins = nc.vector.bn_aggr(mean_var[:, t, :],
                                                        stats[:, 2 * t:2 * t + 2, :].rearrange("p a b -> p (a b)"))
                            link(ins)
                            ts(rs_v[:, b - 1:b + 1], mean_var[:, b - 1:b + 1, 1], eps, None, ALU.add).then_inc(S["rs_in"], 1)
                        if half and b == 2:
                            ln_scale(0)
                return go

            def ffn(nxt):
                for n, (units, downs) in enumerate(FF_HALVES):
                    base_pair, base_off, base_u, ub = Pos.pair, Pos.off, Pos.u, Pos.ubase
                    c0 = N.ff
                    with dve.Fori(0, units) as u:
                        Pos.pair, Pos.off, Pos.end = base_pair + u, base_off, base_off
                        Pos.ubase, Pos.u = ub + u, base_u
                        split()
                        for i in range(2):
                            done(2 + i)
                            dve.wait_ge(g_free[i], ub + u + base_u + 2)
                            ins = tt(work[:, 1024 + i * 512:1536 + i * 512], work[:, i * 512:i * 512 + 512],
                                     G[:, 2 + i, :], ALU.mult)
                            ins.then_inc(g_free[2 + i], 1)
                        for i in range(2):
                            dve.wait_ge(S["ff_hi"], 2 * u + (c0 + i + 1))
                            a = bass.ds(2 * u + i, 1)
                            tt(h_lo[:, a, :].rearrange("p o n -> p (o n)"), work[:, 1024 + i * 512:1536 + i * 512],
                               h_hi[:, a, :].rearrange("p o n -> p (o n)").bitcast(F32), ALU.subtract).then_inc(S["ff_lo"], 1)
                        split()
                    Pos.pair, Pos.off, Pos.end = base_pair, base_off + 2 * units, base_off + 2 * units + 1
                    Pos.ubase, Pos.u = ub, base_u + units
                    N.ff += 2 * units
                    split(downs[2])
                    scale, eps = (2.0 * ALPHA, None) if n == 0 else (1.0, 4.0 * LN_EPS)
                    unit(add_half(scale, 0, eps), (4, 4, downs[2]))
                    unit(add_half(scale, 1, eps), (4, 4) if n == 0 else nxt)

            def layer_norm(i):
                if i == 0:
                    nc.vector.sem_inc(S["half_done"], 1)
                param(dve, Pos.l, "ln_in", i + 1, 3)
                for t in range(TILES):
                    if t == 2:
                        ln_scale(2)
                    dve.wait_ge(S["ln_std"], 4 * i + t + 1)
                    tt(x[:, t, :], x[:, t, :], lnr[:, 0, :], ALU.mult).then_inc(S["ln_gain"], 1)
                    if t % 2:
                        dve.wait_ge(S["ln_gain"], 4 * i + t + 1)
                        tt(x[:, t, :], x[:, t, :], lnr[:, 1, :], ALU.add).then_inc(S["ln_odd"], 1)

            with dve.Fori(0, DEPTH) as l:
                Pos.l = l
                Pos.pair, Pos.off, Pos.end = l * (BLOCK2 // 2) + DEPTH * BLOCK1 // 2, 0, 2
                Pos.ubase, Pos.u = l * UNITS2 + DEPTH * UNITS1, 0
                N.tr, N.ch, N.rs, N.ff, N.half = 0, 0, 0, 0, 0
                nc.vector.sem_inc(S["tr_src"], 4)
                split()
                tr_lo(xT_hi, xT_lo, 4, 2)
                split()
                ffn((4,))
                layer_norm(0)
                tr_lo(xT_hi, xT_lo, 4, 2)
                late_split()
                dve.wait_ge(S["tr_lo"], N.tr)
                nc.vector.tensor_copy(y2_lo[:, :, :].rearrange("p k (c r) -> p k c r", r=NA_R),
                                      xT_lo[:, :, :].bitcast(F32).rearrange("p k (r c) -> p k c r", c=GRID_W)
                                      ).then_inc(S["perm_lo"], 1)
                split()
                param(dve, Pos.l, "shift_in", 16, 16)
                dve.wait_ge(const2_in, 16)
                masks = c2v("masks").rearrange("p (m c r) -> p m c r", m=5, c=16)
                for h in range(NA_H):
                    for m, off in enumerate((16, 0, 16, 32, 16)):
                        ins = tt(bm[:, h, m, :].rearrange("p (c r) -> p c r", c=16),
                                 shifted[:, h, :, off:off + 16].rearrange("p k e -> p e k"), masks[:, m], ALU.add)
                ins.then_inc(S["b_bm"], 1)
                split()
                Pos.u, Pos.end = Pos.u + 1, Pos.end + 2

                for _ in range(3):
                    unit(none, K2)
                param(dve, Pos.l, "col2_in")
                for ch in range(2):
                    dve.wait_ge(S["y2h"], ch + 1)
                    stt(out=y2_lo[:, 4 + ch, :], in0=A[:, 2 + ch, :], scalar=col2[:, ch, 3:4], in1=y2_hi[:, 4 + ch, :].bitcast(F32),
                        op0=ALU.mult, op1=ALU.subtract).then_inc(S["y2l"], 1)
                combos = [(h, j) for h in range(NA_H) for j in range(4)]

                def biased(i):
                    h, j = combos[i]
                    nb = min(4, j + 2) - max(0, j - 1)
                    n = nb * P
                    dve.wait_ge(S["n_s"], i + 1)
                    if i == 0:
                        dve.wait_ge(S["y2l"], 2)
                        dve.wait_ge(S["y2h"], 2)
                    if i >= 3:
                        dve.wait_ge(S["n_t"], i - 2)
                    w = p_slot(i)[:, 0:n]
                    b = {0: bm[:, h, 0:4:3, :], 1: bm[:, h, 1:4, :], 2: bm[:, h, 1:4, :], 3: bm[:, h, 1:5:3, :]}[j]
                    link(stt(out=w.rearrange("p (b n) -> p b n", n=P),
                             in0=A[:, i % 2, 0:n].rearrange("p (b n) -> p b n", n=P), scalar=NA_D ** -0.5, in1=b,
                             op0=ALU.mult, op1=ALU.add))
                    link(nc.vector.tensor_reduce(nmx[:, 2, i:i + 1], w, AX.X, ALU.max))
                    ts(nmx[:, 0, i:i + 1], nmx[:, 2, i:i + 1], -1.0, None, ALU.mult).then_inc(S["n_m"], 1)

                def normed(i):
                    h, j = combos[i]
                    n = (min(4, j + 2) - max(0, j - 1)) * P
                    dve.wait_ge(S["n_p"], i + 1)
                    link(nc.vector.reciprocal(nmx[:, 3, i:i + 1], nmx[:, 1, i:i + 1]))
                    w = p_slot(i)[:, 0:n]
                    ts(w, w, nmx[:, 3, i:i + 1], None, ALU.mult).then_inc(S["n_pn"], 1)

                def pair_out(i):
                    dve.wait_ge(S["n_oh"], i + 1)
                    tt(y2_lo[:, i, :].rearrange("p (r c) -> p c r", c=GRID_W), A[:, 3, :].rearrange("p (c r) -> p c r", r=NA_R),
                       y2_hi[:, i, :].bitcast(F32).rearrange("p (r c) -> p c r", c=GRID_W),
                       ALU.subtract).then_inc(S["n_ol"], 1)

                for i in range(len(combos) + 3):
                    if i == C_H_STEPS[15] + 2:
                        split()
                    if i < len(combos):
                        biased(i)
                    if 1 <= i <= len(combos):
                        normed(i - 1)
                    if i >= 3 and (i - 3) % 8 == 7:
                        pair_out((i - 3) // 8)
                z = [work[:, b * 512:b * 512 + 512] for b in range(2)]
                for b in range(2):
                    done(2 + b)
                    dve.wait_ge(g_free[b], Pos.ubase + Pos.u + 2)
                    tt(z[b], z[b], G[:, 2 + b, :], ALU.mult).then_inc(g_free[2 + b], 1)
                Pos.u, Pos.end = Pos.u + 1, Pos.end + 2
                results_read()
                for b in range(2):
                    o = conv_out[:, b * 512:b * 512 + 512]
                    gb = gate_b[:, b * 512:b * 512 + 512]
                    link(ts(o, z[b], col2[:, b, 1:2], None, ALU.mult))
                    link(stt(out=o[:, 1:], in0=z[b][:, 0:511], scalar=col2[:, b, 0:1], in1=o[:, 1:], op0=ALU.mult, op1=ALU.add))
                    link(stt(out=o[:, 0:511], in0=z[b][:, 1:], scalar=col2[:, b, 2:3], in1=o[:, 0:511], op0=ALU.mult, op1=ALU.add))
                    tt(gb, gb, o, ALU.mult).then_inc(S["z_y"], 1)
                for ch in range(2):
                    dve.wait_ge(S["y2h"], ch + 3)
                    tt(y2_lo[:, 6 + ch, :], gate_b[:, ch * 512:ch * 512 + 512], y2_hi[:, 6 + ch, :].bitcast(F32),
                       ALU.subtract).then_inc(S["y2l"], 1)
                split()
                unit(add_half(ALPHA, 0, LN_EPS), K2)
                unit(add_half(ALPHA, 1, LN_EPS), (4,))
                layer_norm(1)
                tr_lo(xT_hi, xT_lo, 4, 2)
                late_split()
                ffn(())
                layer_norm(2)
                assert Pos.off == BLOCK2 and Pos.u == UNITS2
                end_layer(l + 1 + DEPTH)

        @block.gpsimd
        def _(pool):
            def load_mem():
                pool.dma_start(mem_t,
                               mem_in.rearrange("a (t p) d -> p (a t) d", p=P)).then_inc(landed["mem_in"], 16)

            def load_mem_gain(l):
                pool.dma_start(row[:, MEM_G:MEM_G + D], rows1[bass.ds(l, 1), MEM_G:MEM_G + D].to_broadcast([P, D])
                               ).then_inc(landed["mem_g_in"], 16)
            load_mem()
            load_mem_gain(0)
            with pool.Fori(0, DEPTH) as l:
                pool.wait_ge(layer_open, l + 1)
                pool.sem_inc(S["layer_begun"], 1)
                for a, b in ((PRE_G, MEM_G), (SSD_G, ROW1)):
                    pool.dma_start(row[:, a:b], rows1[bass.ds(l, 1), a:b].to_broadcast([P, b - a])).then_inc(landed["row_in"], 16)
                pool.dma_start(conv[:, :, :].rearrange("p a b -> p (a b)"),
                               conv1[bass.ds(l, 1)].rearrange("o p n -> (o p) n")).then_inc(landed["conv_in"], 16)
                pool.dma_start(wdt[:, :, :].rearrange("p a b -> p (a b)"),
                               w_dt[bass.ds(l, 1)].rearrange("o p n -> (o p) n")).then_inc(landed["wdt_in"], 16)
                param(pool, l, "conv_in")
                param(pool, l, "wdt_in")
                pool.wait_ge(const1_in, 16)
                for i in range(8):
                    pool.wait_ge(S["rot_done"], i + 1)
                    f = (fA if i < 4 else fB)[:, i % 4, :]
                    nc.gpsimd.tensor_tensor(f, f, c1v("cos"), ALU.mult).then_inc(S["rot_cos"], 1)
                param(pool, l, "row_in", 2, 2)
                for c in range(TILES):
                    pool.wait_ge(S["x_tc"], 2 * c + 1)
                    nc.gpsimd.tensor_tensor(mix[:, c, :].rearrange("p (h n) -> p h n", n=64),
                                            tA[:, c, :].rearrange("p (h n) -> p h n", n=64),
                                            row[:, D_SKIP:D_SKIP + 8].unsqueeze(2).to_broadcast([P, 8, 64]),
                                            ALU.mult).then_inc(S["d_skip"], 1)
                pool.wait_ge(S["d_y"], 4)
                load_mem()
                load_mem_gain(l + 1)
                for t in range(2):
                    pool.wait_ge(S["y_scaled"], t + 1)
                    nc.gpsimd.tensor_tensor(x[:, t, :], x[:, t, :], y_acc[:, t, :], ALU.add).then_inc(S["x_added"], 1)
                pool.wait_ge(S["row_used"], 1)
                param(pool, l + 1, "mem_in")
                param(pool, l + 1, "mem_g_in")
                pool.sem_inc(pool_end, 1)
            pool.wait_ge(layer_open, DEPTH + 1)
            pool.dma_start(cst2[:, :], const2).then_inc(const2_in, 16)
            with pool.Fori(0, DEPTH) as l:
                pool.wait_ge(layer_open, l + 1 + DEPTH)
                pool.sem_inc(S["layer_begun"], 1)
                def load_ln(i):
                    pool.dma_start(lnr[:, :, :].rearrange("p a b -> p (a b)"),
                                   ln_rows[bass.ds(l, 1), i, :].to_broadcast([P, 2 * D])).then_inc(landed["ln_in"], 16)

                def add_bias(i):
                    param(pool, l, "ln_in", i + 1, 3)
                    for t in (0, 2):
                        pool.wait_ge(S["ln_gain"], 4 * i + t + 1)
                        nc.gpsimd.tensor_tensor(x[:, t, :], x[:, t, :], lnr[:, 1, :], ALU.add).then_inc(S["ln_even"], 1)
                    pool.wait_ge(S["ln_even"], 2 * i + 2)
                    pool.wait_ge(S["ln_odd"], 2 * i + 2)
                pool.dma_start(rpb_rows[0:15, 0:248], rpb[bass.ds(l, 1)].rearrange("o p n -> (o p) n")).then_inc(landed["rpb_in"], 16)
                pool.dma_start(sel[0:15, :], sel_in).then_inc(landed["sel_in"], 16)
                load_ln(0)
                pool.dma_start(col2[:, :, :].rearrange("p a b -> p (a b)"),
                               cols2[bass.ds(l, 1)].rearrange("o p n -> (o p) n")).then_inc(landed["col2_in"], 16)
                pool.wait_ge(S["half_done"], 1)
                add_bias(0)
                pool.memset(qkv[:, 0:3072], 0.0).then_inc(S["b_raw"], 1)
                pool.wait_ge(S["b_raw"], 1)
                pool.wait_ge(S["b_gc"], NA_R)
                pool.dma_start(poolw[:, :, :].rearrange("p a b -> p (a b)"),
                               pool_w[bass.ds(l, 1)].rearrange("o p n -> (o p) n")).then_inc(landed["poolw_in"], 16)
                for c in range(16):
                    pool.dma_start(shifted[8 * c:8 * c + 8, :, :, c + 1:c + 32],
                                   raw_rows[8 * c:8 * c + 8, :].rearrange("p (h k e) -> p h k e", h=8, k=8)
                                   ).then_inc(landed["shift_in"], 16)
                param(pool, l, "shift_in", 16, 16)
                pool.sem_inc(S["layer_begun"], 1)
                pool.wait_ge(S["y2l"], 4)
                load_ln(1)
                add_bias(1)
                load_ln(2)
                add_bias(2)
                pool.sem_inc(pool_end, 1)
            pool.wait_ge(layer_open, 2 * DEPTH + 1)
            pool.dma_start(out.rearrange("a (t p) d -> p (a t) d", p=P), x[:, :, :]).then_inc(out_done, 16)
            pool.wait_ge(out_done, 16)


def weight_stream(v):
    out = []

    def add(w, col, rows=None):
        r0, r1 = rows or (0, w.shape[0])
        for r in range(r0, r1, KB * P):
            b = w[r:min(r + KB * P, r1), col:col + BC]
            b = b.reshape(-1, P, BC).transpose(1, 0, 2)
            if b.shape[1] < KB:
                b = np.concatenate([b, np.zeros((P, KB - b.shape[1], BC), b.dtype)], axis=1)
            out.append(b.reshape(P, KB * BC))

    for l in range(DEPTH):
        w, wo, kv = v["w_in"][l], v["w_out"][l], v["w_mem_kv"][l]

        def mixer(cols, first_row):
            for c in cols:
                add(w, c)
            for half in range(2):
                add(wo, half * BC, (first_row, first_row + GW))
        add(kv, 0)
        add(kv, GW)
        mixer((5640, 6152), 1536)
        mixer((0, 512, 1024, 1536), 0)
        mixer((3592, 4104, 4616, 5128), 1024)
        mixer((2048, 2560, 3072), 512)
    for l in range(DEPTH):
        def ffn(name):
            g, u, d = (v[f"{name}_w_{p}_2"][l] for p in ("gate", "up", "down"))
            gu = np.stack([g.reshape(D, 11, 256), u.reshape(D, 11, 256)], axis=2).reshape(D, -1)
            at = 0
            for units, downs in FF_HALVES:
                for i in range(at, at + units):
                    add(gu, i * BC)
                for half in range(2):
                    add(d, half * BC, (at * 256, (at + units) * 256))
                at += units
        ffn("ffn1")
        for c in (0, 2, 3, 4, 1):
            add(v["w_in_2"][l], c * BC)
        wo = v["w_out_2"][l]
        for half in range(2):
            add(wo, half * BC, (2 * CONV2, D))
            add(wo, half * BC, (0, 2 * CONV2))
        ffn("ffn2")
    return np.stack(out)


def kernel(**inputs):
    import concourse.bacc as bacc
    from concourse.bass_utils import run_bass_kernel_spmd

    v = {k: np.ascontiguousarray(a) for k, a in inputs.items()}
    f = np.float32
    c0, c1, c2, c3 = (np.concatenate([a.astype(f) for a in c.values()], axis=1) for c in constants())
    rows1 = np.concatenate([v["pre_norm_g"], v["post_norm_g"], v["mem_norm_g"], v["ssd_norm_g"], v["dt_bias"],
                            v["a_log"], v["d_skip"]], axis=1)
    rows1 = np.concatenate([rows1, rows1[-1:]])
    conv1 = np.concatenate([v["conv_w"], v["conv_b"][:, None]], axis=1).reshape(DEPTH, 5, 8, P)
    conv1 = conv1.transpose(0, 3, 2, 1).reshape(DEPTH, P, 40)
    w_dt = v["w_in"][:, :, 3584:3592].reshape(DEPTH, 8, P, 8).transpose(0, 2, 1, 3).reshape(DEPTH, P, 64)
    ln_rows = np.stack([v["ln_g_2"], v["ln_b_2"]], axis=2).reshape(DEPTH, 3, 2 * D)
    pool_w = np.zeros((DEPTH, P, 2, P), f)
    for g in range(4):
        a = 64 * (g % 2)
        pool_w[:, a:a + 64, g // 2, a:a + 64] = v["pool_w_2"][:, g]
    cols2 = np.concatenate([v["conv_w_2"], v["pool_scale_2"][:, None]], axis=1).reshape(DEPTH, 4, 2, P)
    cols2 = cols2.transpose(0, 3, 2, 1).reshape(DEPTH, P, 8)
    rpb = v["rpb_2"].transpose(0, 2, 1, 3).reshape(DEPTH, 15, NA_H * 31)

    arrays = {"in_x": v["x"], "in_mem": v["mem"], "in_stream": weight_stream(v), "in_const0": c0, "in_const1": c1,
              "in_const2": c2, "in_rows1": rows1, "in_conv1": conv1, "in_w_dt": w_dt, "in_ln_rows": ln_rows,
              "in_pool_w": pool_w.reshape(DEPTH, P, 2 * P), "in_cols2": cols2, "in_rpb": rpb, "in_sel": c3}
    arrays = {k: np.ascontiguousarray(a) for k, a in arrays.items()}
    nc = bacc.Bacc("TRN2", target_bir_lowering=False, num_devices=1)
    args = [nc.dram_tensor(k, a.shape, mybir.dt.from_np(a.dtype), kind="ExternalInput").ap() for k, a in arrays.items()]
    out = nc.dram_tensor("out_0", (1, SEQ, D), F32, kind="ExternalOutput").ap()
    build(nc, *args, out)
    r = run_bass_kernel_spmd(nc, [arrays], core_ids=[0])
    return r.results[0]["out_0"]
```
